# Optimizing a Trainium2 kernel written in Bass

```python
import jax, jax.numpy as jnp
from jax import lax
import numpy as np

D_MODEL = 1024
BATCH = 1
SEQ = 512
DEPTH = 1
DEC_BATCH = 8
DEC_SEQ = 1
PAST_LEN = 1024
PAGE_SIZE = 128

HEAD_DIM = 64
N_ATTN_HEADS = 12
D_ATTN = N_ATTN_HEADS * HEAD_DIM
D_CONV = D_MODEL - D_ATTN
CONV_WIDTH = 3
DILATED_BRANCHES = ((128, 1), (512, 4), (2048, 16))
MAX_WINDOW = 2048
ATT_BLOCK = 128
ATTN_SCALE = HEAD_DIM ** -0.5
ROPE_THETA = 10000.0
EPS = 1e-6
N_GROUPS = 4
EXPERTS_PER_GROUP = 8
N_EXPERTS = N_GROUPS * EXPERTS_PER_GROUP
TOP_K_IN_GROUP = 2
D_EXPERT = 256
D_IN_PROJ = 3 * D_ATTN + 3 * D_CONV
SPLITS = (D_ATTN, 2 * D_ATTN, 3 * D_ATTN, 3 * D_ATTN + D_CONV, 3 * D_ATTN + 2 * D_CONV)

kernel_name = "hymba_dilated_window_shortconv_hier_moe_step"

def rms_norm(x, g):
    xf = x.astype(jnp.float32)
    y = xf * lax.rsqrt(jnp.mean(xf * xf, axis=-1, keepdims=True) + EPS)
    return (y * g.astype(jnp.float32)).astype(x.dtype)

def rope(x, pos):
    half = HEAD_DIM // 2
    inv = ROPE_THETA ** (-jnp.arange(half, dtype=jnp.float32) / half)
    ang = pos.astype(jnp.float32)[:, None] * inv[None, :]
    cos = jnp.cos(ang)[:, None, :]
    sin = jnp.sin(ang)[:, None, :]
    xf = x.astype(jnp.float32)
    x1, x2 = xf[..., :half], xf[..., half:]
    return jnp.concatenate([x1 * cos - x2 * sin, x2 * cos + x1 * sin], axis=-1).astype(x.dtype)

def mix_input(x, pos, g_norm_mix, w_in, g_q, g_k):
    B_, T_ = x.shape[:2]
    xn = rms_norm(x, g_norm_mix)
    z = xn @ w_in
    q, k, v, b_gate, c_gate, u_in = jnp.split(z, SPLITS, axis=-1)
    heads = lambda t: t.reshape(B_, T_, N_ATTN_HEADS, HEAD_DIM)
    q = rope(rms_norm(heads(q), g_q), pos)
    k = rope(rms_norm(heads(k), g_k), pos)
    return q, k, heads(v), b_gate, c_gate * u_in

def dilated_branch_prompt(q, k, v, dil, sub_window):
    B_, S_, H_, Dh_ = q.shape
    L = S_ // dil
    nb = -(-L // ATT_BLOCK)
    Lp = nb * ATT_BLOCK

    def sub_blocks(t):
        t = t.reshape(B_, L, dil, H_, Dh_).transpose(0, 2, 1, 3, 4)
        t = jnp.pad(t, ((0, 0), (0, 0), (0, Lp - L), (0, 0), (0, 0)))
        return t.reshape(B_, dil, nb, ATT_BLOCK, H_, Dh_)

    qb, kb, vb = sub_blocks(q), sub_blocks(k), sub_blocks(v)
    prev = lambda t: jnp.pad(t, ((0, 0), (0, 0), (1, 0), (0, 0), (0, 0), (0, 0)))[:, :, :-1]
    kk = jnp.concatenate([prev(kb), kb], axis=3)
    vv = jnp.concatenate([prev(vb), vb], axis=3)
    s = jnp.einsum('brnqhd,brnkhd->brnhqk', qb, kk) * ATTN_SCALE
    qi = jnp.arange(ATT_BLOCK)[:, None] + ATT_BLOCK
    kj = jnp.arange(2 * ATT_BLOCK)[None, :]
    dist = qi - kj
    band = (dist >= 0) & (dist <= sub_window)
    has_prev = (jnp.arange(nb)[:, None, None] > 0) | (kj >= ATT_BLOCK)[None]
    valid = band[None] & has_prev
    s = jnp.where(valid[:, None], s, -jnp.inf)
    m = jnp.max(s, axis=-1)
    p = jnp.exp(s - m[..., None])
    den = jnp.sum(p, axis=-1)
    num = jnp.einsum('brnhqk,brnkhd->brnqhd', p, vv)

    num = num.reshape(B_, dil, Lp, H_, Dh_)[:, :, :L].transpose(0, 2, 1, 3, 4).reshape(B_, S_, H_, Dh_)
    unblock = lambda t: t.transpose(0, 1, 2, 4, 3).reshape(B_, dil, Lp, H_)[:, :, :L].transpose(0, 2, 1, 3).reshape(B_, S_, H_)
    return num, unblock(den), unblock(m)

def dilated_branch_sample(q, k_all, v_all, w_buf, dil, sub_window):
    T_ = q.shape[1]
    n_keys = sub_window + 1
    idx = w_buf + jnp.arange(T_)[:, None] - dil * jnp.arange(n_keys)[None, :]
    valid = idx >= 0
    idx_c = jnp.maximum(idx, 0)
    kg = k_all[:, idx_c]
    vg = v_all[:, idx_c]
    s = jnp.einsum('bthd,btnhd->bthn', q, kg) * ATTN_SCALE
    s = jnp.where(valid[None, :, None, :], s, -jnp.inf)
    m = jnp.max(s, axis=-1)
    p = jnp.exp(s - m[..., None])
    den = jnp.sum(p, axis=-1)
    num = jnp.einsum('bthn,btnhd->bthd', p, vg)
    return num, den, m

def merge_by_denominator(parts):
    m_all = parts[0][2]
    for _, _, m in parts[1:]:
        m_all = jnp.maximum(m_all, m)
    num_t, den_t = 0.0, 0.0
    for num, den, m in parts:
        c = jnp.exp(m - m_all)
        num_t = num_t + num * c[..., None]
        den_t = den_t + den * c
    return num_t / den_t[..., None]

def hier_moe(xn, w_router_group, w_router_expert, w_gate, w_up, w_down):
    shp = xn.shape
    t = xn.reshape(-1, D_MODEL)
    lg = (t @ w_router_group).astype(jnp.float32)
    pg = jax.nn.softmax(lg, axis=-1)
    g = jnp.argmax(lg, axis=-1)
    p_g = jnp.max(pg, axis=-1, keepdims=True)
    le = (t @ w_router_expert).astype(jnp.float32).reshape(-1, N_GROUPS, EXPERTS_PER_GROUP)
    le_g = jnp.einsum('nge,ng->ne', le, jax.nn.one_hot(g, N_GROUPS, dtype=jnp.float32))
    top_v, top_i = lax.top_k(le_g, TOP_K_IN_GROUP)
    w_sel = jax.nn.softmax(top_v, axis=-1) * p_g
    eid = g[:, None] * EXPERTS_PER_GROUP + top_i
    combine = jnp.einsum('nk,nke->ne', w_sel, jax.nn.one_hot(eid, N_EXPERTS, dtype=jnp.float32))

    def expert_step(acc, ew):
        wg, wu, wd, cw = ew
        h = jax.nn.silu(t @ wg) * (t @ wu)
        return acc + cw[:, None] * (h @ wd).astype(jnp.float32), None

    y, _ = lax.scan(expert_step, jnp.zeros(t.shape, jnp.float32), (w_gate, w_up, w_down, combine.T))
    return y.astype(xn.dtype).reshape(shp)

def finish_layer(x, attn, b_gate, conv_out, g_attn_out, g_conv_out, w_out,
                 g_norm_ffn, w_router_group, w_router_expert, w_gate, w_up, w_down):
    B_, T_ = x.shape[:2]
    a = rms_norm(attn.reshape(B_, T_, D_ATTN), g_attn_out)
    c = rms_norm(b_gate * conv_out, g_conv_out)
    h = x + jnp.concatenate([a, c], axis=-1) @ w_out
    return h + hier_moe(rms_norm(h, g_norm_ffn), w_router_group, w_router_expert, w_gate, w_up, w_down)

def prompt_layer(x, g_norm_mix, w_in, g_q, g_k, w_conv, g_attn_out, g_conv_out, w_out,
                 g_norm_ffn, w_router_group, w_router_expert, w_gate, w_up, w_down):
    S_ = x.shape[1]
    q, k, v, b_gate, u = mix_input(x, jnp.arange(S_), g_norm_mix, w_in, g_q, g_k)
    qf, kf, vf = q.astype(jnp.float32), k.astype(jnp.float32), v.astype(jnp.float32)
    parts = [dilated_branch_prompt(qf, kf, vf, d, w // d) for (w, d) in DILATED_BRANCHES]
    attn = merge_by_denominator(parts).astype(x.dtype)
    up = jnp.pad(u, ((0, 0), (CONV_WIDTH - 1, 0), (0, 0)))
    conv_out = sum(w_conv[j] * up[:, j:j + S_] for j in range(CONV_WIDTH))
    y = finish_layer(x, attn, b_gate, conv_out, g_attn_out, g_conv_out, w_out,
                     g_norm_ffn, w_router_group, w_router_expert, w_gate, w_up, w_down)
    keep = min(MAX_WINDOW, S_)
    return y, k[:, S_ - keep:], v[:, S_ - keep:], u[:, S_ - (CONV_WIDTH - 1):]

def sample_layer(x, cache_k, cache_v, state_conv, g_norm_mix, w_in, g_q, g_k, w_conv, g_attn_out, g_conv_out, w_out,
                 g_norm_ffn, w_router_group, w_router_expert, w_gate, w_up, w_down):
    T_ = x.shape[1]
    w_buf = cache_k.shape[1]
    q, k, v, b_gate, u = mix_input(x, PAST_LEN + jnp.arange(T_), g_norm_mix, w_in, g_q, g_k)
    k_all = jnp.concatenate([cache_k.astype(jnp.float32), k.astype(jnp.float32)], axis=1)
    v_all = jnp.concatenate([cache_v.astype(jnp.float32), v.astype(jnp.float32)], axis=1)
    qf = q.astype(jnp.float32)
    parts = [dilated_branch_sample(qf, k_all, v_all, w_buf, d, w // d) for (w, d) in DILATED_BRANCHES]
    attn = merge_by_denominator(parts).astype(x.dtype)
    full = jnp.concatenate([state_conv.astype(u.dtype), u], axis=1)
    conv_out = sum(w_conv[j] * full[:, j:j + T_] for j in range(CONV_WIDTH))
    y = finish_layer(x, attn, b_gate, conv_out, g_attn_out, g_conv_out, w_out,
                     g_norm_ffn, w_router_group, w_router_expert, w_gate, w_up, w_down)
    return y, k, v, full[:, T_:]

def setup_inputs(seed: int = 0) -> dict:
    key = jax.random.key(seed)
    ks = jax.random.split(key, 20)
    f32 = jnp.float32
    w_buf = min(MAX_WINDOW, PAST_LEN)
    nrm = lambda kk, shape, scale: jax.random.normal(kk, shape, f32) * scale
    gain = lambda kk, shape: 1.0 + 0.02 * jax.random.normal(kk, shape, f32)
    return {
        "x_prompt": nrm(ks[0], (BATCH, SEQ, D_MODEL), 1.0),
        "x_sample": nrm(ks[1], (DEC_BATCH, DEC_SEQ, D_MODEL), 1.0),
        "cache_k": nrm(ks[2], (DEPTH, DEC_BATCH, w_buf, N_ATTN_HEADS, HEAD_DIM), 1.0),
        "cache_v": nrm(ks[3], (DEPTH, DEC_BATCH, w_buf, N_ATTN_HEADS, HEAD_DIM), 1.0),
        "state_conv": nrm(ks[4], (DEPTH, DEC_BATCH, CONV_WIDTH - 1, D_CONV), 1.0),
        "g_norm_mix": gain(ks[5], (DEPTH, D_MODEL)),
        "w_in": nrm(ks[6], (DEPTH, D_MODEL, D_IN_PROJ), D_MODEL ** -0.5),
        "g_q": gain(ks[7], (DEPTH, HEAD_DIM)),
        "g_k": gain(ks[8], (DEPTH, HEAD_DIM)),
        "w_conv": nrm(ks[9], (DEPTH, CONV_WIDTH, D_CONV), CONV_WIDTH ** -0.5),
        "g_attn_out": gain(ks[10], (DEPTH, D_ATTN)),
        "g_conv_out": gain(ks[11], (DEPTH, D_CONV)),
        "w_out": nrm(ks[12], (DEPTH, D_MODEL, D_MODEL), D_MODEL ** -0.5),
        "g_norm_ffn": gain(ks[13], (DEPTH, D_MODEL)),
        "w_router_group": nrm(ks[14], (DEPTH, D_MODEL, N_GROUPS), D_MODEL ** -0.5),
        "w_router_expert": nrm(ks[15], (DEPTH, D_MODEL, N_EXPERTS), D_MODEL ** -0.5),
        "w_gate": nrm(ks[16], (DEPTH, N_EXPERTS, D_MODEL, D_EXPERT), D_MODEL ** -0.5),
        "w_up": nrm(ks[17], (DEPTH, N_EXPERTS, D_MODEL, D_EXPERT), D_MODEL ** -0.5),
        "w_down": nrm(ks[18], (DEPTH, N_EXPERTS, D_EXPERT, D_MODEL), D_EXPERT ** -0.5),
    }

def reference(x_prompt, x_sample, cache_k, cache_v, state_conv, g_norm_mix, w_in, g_q, g_k, w_conv,
              g_attn_out, g_conv_out, w_out, g_norm_ffn, w_router_group, w_router_expert, w_gate, w_up, w_down):
    yp, ys = x_prompt, x_sample
    kp, vp, cp, ksm, vsm, csm = [], [], [], [], [], []
    for l in range(DEPTH):
        weights = (g_norm_mix[l], w_in[l], g_q[l], g_k[l], w_conv[l], g_attn_out[l], g_conv_out[l], w_out[l],
                   g_norm_ffn[l], w_router_group[l], w_router_expert[l], w_gate[l], w_up[l], w_down[l])
        yp, k_p, v_p, c_p = prompt_layer(yp, *weights)
        ys, k_s, v_s, c_s = sample_layer(ys, cache_k[l], cache_v[l], state_conv[l], *weights)
        kp.append(k_p); vp.append(v_p); cp.append(c_p)
        ksm.append(k_s); vsm.append(v_s); csm.append(c_s)
    return (yp, ys, jnp.stack(kp), jnp.stack(vp), jnp.stack(cp), jnp.stack(ksm), jnp.stack(vsm), jnp.stack(csm))


_drawn_inputs = setup_inputs


def setup_inputs(seed=0):
    import zlib

    import numpy as np

    out = dict(_drawn_inputs(seed))
    spreads = {}
    factors = {'g_q': 2.897, 'g_k': 2.823, 'g_conv_out': 3.02, 'g_norm_ffn': 2.791}
    for name, (base, spread) in spreads.items():
        noise = np.random.default_rng([zlib.crc32(name.encode()), seed]).standard_normal(out[name].shape)
        drawn = base * np.exp(spread * noise) if base else spread * noise
        out[name] = __import__('jax').numpy.asarray(drawn.astype(out[name].dtype))
    for name, factor in factors.items():
        out[name] = (out[name] * factor).astype(out[name].dtype)
    return out
```

```python
from contextlib import ExitStack

import numpy as np

import concourse.bass as bass
from concourse import mybir
from concourse.alu_op_type import AluOpType as ALU

F32 = mybir.dt.float32
U32 = mybir.dt.uint32
I32 = mybir.dt.int32
ACT = mybir.ActivationFunctionType
AX = mybir.AxisListType

P = 128
SEQ, DEC, D = 512, 8, 1024
NT = SEQ // P
TILES = [P] * NT + [DEC]
KD = D // P
H, DH = 12, 64
DA, DC = H * DH, 256
NP = H // 2
EPS = 1e-6
G, EG, E, F = 4, 8, 32, 256
WBUF = 1024
CW = 384
QK_CHUNKS, QKV_CHUNKS, CHUNKS = 4, 6, 8
WRING = 3
SL = 64
PAIRS = E // 2
WSLOTS = 3
OV_PAIRS = 9
TOK = SEQ + DEC
CHOICES = 2 * TOK
OV_ROWS = 512
OV_BASE = E * SL
TABLE = OV_BASE + E * OV_ROWS + 2 * OV_PAIRS * SL
EMPTY = 1 << 14
NEG = -1.0e30


def ds(i, n):
    return bass.ds(i, n)


def constants():
    f = np.float32
    seg = {}
    p = np.arange(P)
    seg["ident"] = np.eye(P)
    seg["tri"] = (p[:, None] < p[None, :])
    seg["ones"] = np.ones((P, P))
    d = p[:, None] + 3 * P - np.arange(SEQ)[None, :]
    c = ((d >= 0) & (d <= 128)).astype(int) + ((d >= 0) & (d % 4 == 0) & (d <= 512)) + ((d >= 0) & (d % 16 == 0))
    seg["logc"] = np.where(c > 0, np.log(np.maximum(c, 1)), NEG)
    half = DH // 2
    inv = (f(10000.0) ** (-np.arange(half, dtype=f) / f(half))).astype(f)
    pos = np.concatenate([np.arange(SEQ).reshape(NT, P).T, np.full((P, 1), WBUF)], 1).astype(f)
    ang = (pos[:, :, None] * inv[None, None, :]).astype(f)
    cos, sin = np.cos(ang), np.sin(ang)
    seg["cos"] = np.concatenate([cos, cos], 2).reshape(P, -1)
    seg["sin"] = np.concatenate([-sin, sin], 2).reshape(P, -1)
    rows = np.concatenate([896 + p, 512 + 4 * np.arange(96), 16 * np.arange(32)])
    d = np.concatenate([WBUF - rows, [0]])
    c = (d <= 128).astype(int) + ((d % 4 == 0) & (d <= 512)) + (d % 16 == 0)
    seg["slogc"] = np.tile(np.log(c)[None], (P, 1))
    q = np.arange(P)
    seg["head"] = (q[:, None] % H == np.arange(H)[None]) & (q[:, None] < DEC * H)
    seg["sample"] = (q[:, None] // H == np.arange(DEC)[None])
    seg["sampleT"] = (np.arange(DEC * H)[None] // H == q[:, None])
    seg["quad"] = (q[:, None] % 32 == np.arange(DEC)[None])
    seg["quada"] = seg["quad"] & (q[:, None] < 96)
    seg["quadc"] = seg["quad"] & (q[:, None] >= 96)
    seg["valid"] = (np.arange(NT + 1)[None] < NT) | (q[:, None] < DEC)
    seg["iota"] = np.tile(np.arange(EG)[None], (P, 1))
    e = np.arange(E)
    seg["mainrow"] = np.tile(((e % 2) * SL * PAIRS + e // 2)[None], (P, 1))
    seg["ovrow"] = np.tile((OV_BASE + e * OV_ROWS - SL)[None], (P, 1))
    seg["limits"] = np.tile((SL * (1 + np.arange(8)))[None], (P, 1))
    at, n = {}, 0
    for k, v in seg.items():
        at[k] = (n, v.shape[1])
        n += v.shape[1]
    return np.concatenate([v.astype(f) for v in seg.values()], 1), at


def payload():
    t = np.minimum(np.arange(NT + 1)[None, :] * P + np.arange(P)[:, None], TOK - 1)
    pay = np.zeros((P, NT + 1, 2, 2), np.uint32)
    pay[..., 0] = t[:, :, None]
    pay[..., 1] = 2 * t[:, :, None] + np.arange(2)
    return pay.reshape(P, -1)


def empty_table():
    return np.full((P, TABLE // P * 2), EMPTY, np.uint32)


AT = constants()[1]


def build(nc, x_prompt, x_sample, cache_k, cache_v, state_conv, g_norm_mix, w_in, g_q, g_k, w_conv, g_attn_out,
          g_conv_out, w_out, g_norm_ffn, w_router_group, w_router_expert, w_gate, w_up, w_down, const, pay, empty,
          y_prompt, y_sample, k_prompt, v_prompt, conv_prompt, k_sample, v_sample, conv_sample):
    ctx = ExitStack()
    with ctx:
        def sb(name, shape, dt=F32):
            return ctx.enter_context(nc.sbuf_tensor(name, shape, dt))

        def sem(name):
            return ctx.enter_context(nc.semaphore(name))

        hn_rows = nc.dram_tensor("hn_rows", [TOK, D], F32, kind="Internal").ap()
        results = nc.dram_tensor("results", [CHOICES, D], F32, kind="Internal").ap()
        table = nc.dram_tensor("table", [TABLE, 2], U32, kind="Internal").ap()

        bank = [ctx.enter_context(nc.psum_tensor(f"bank{i}", [P, 512], F32)) for i in range(8)]

        SLOT = 12288
        ring = sb("ring", [P, WSLOTS * SLOT])
        work = sb("work", [P, 8192])
        x = sb("x", [P, NT + 1, D])
        rt = sb("rt", [P, 1600])

        def cut(t, off, *dims):
            n = int(np.prod(dims))
            v = t[:, off:off + n]
            if len(dims) == 2:
                return v.rearrange("p (a b) -> p a b", a=dims[0])
            if len(dims) == 3:
                return v.rearrange("p (a b c) -> p a b c", a=dims[0], b=dims[1])
            if len(dims) == 4:
                return v.rearrange("p (a b c d) -> p a b c d", a=dims[0], b=dims[1], c=dims[2])
            return v

        wchunk = [cut(ring, i * 3072, KD, CW) for i in range(WRING)]
        rope_g = [cut(ring, 9216 + i * 320, NT + 1, DH) for i in range(4)]
        zsq = cut(ring, 10496, CW)
        zn = cut(ring, 10880, CW)
        zcos = cut(ring, 11264, CW)
        zsin = cut(ring, 11648, CW)
        probs_s = cut(ring, 6144, 2, DEC, DEC * H)
        head_out = cut(ring, 7680, DA)
        attn_s = cut(ring, 8448, DA)
        scores_sb = [cut(ring, i * 512, 512) for i in range(2)]
        probs_t = [cut(ring, 1024 + i * 512, 512) for i in range(2)]
        ysq = cut(ring, 2048, 2, TOK)
        qT = cut(ring, SLOT, NP, SEQ)
        kT = cut(ring, SLOT + 3072, NP, SEQ)
        v_rows = cut(ring, SLOT + 6144, NT, DA)
        attn = cut(ring, SLOT + 9216, NT, DA)
        xn = cut(ring, SLOT + 6144, NT + 1, D)
        junk_x = cut(ring, SLOT + 11264, D)
        bT = cut(ring, SLOT + 9216, 2, TOK)
        cuT = cut(ring, SLOT + 10256, 2, 2 + SEQ)
        cu_s = cut(ring, SLOT + 11284, 2, 3, DEC)
        conv_rows = cut(ring, SLOT + 11400, 512)
        wout = cut(ring, 2 * SLOT, KD, D)
        xT = cut(ring, 2 * SLOT + 8192, KD, SEQ)
        attnT = cut(ring, 2 * SLOT + 8192, NP, SEQ)
        partial = cut(work, 6656, CW)

        kv = [cut(work, i * 1536, 2, DA) for i in range(2)]
        qs, ks, vs = (cut(work, 3072 + i * DA, DA) for i in range(3))
        rot = [cut(work, 5376 + i * CW, CW) for i in range(2)]
        xsT = cut(work, 6144, KD, 32)
        mixsT = cut(work, 6400, KD, 32)
        yT = cut(work, 7152, 2, TOK)
        cos = cut(work, 7152, NT + 1, DH)
        sin = cut(work, 7472, NT + 1, DH)
        hn = [cut(work, i * D, D) for i in range(2)]
        hnT = [cut(work, 2048 + i * D, KD, P) for i in range(2)]
        junk = cut(work, 4096, D)
        partial_o = cut(work, 5120, D)

        gate_up = [[cut(ring, s * SLOT + h * 4096, KD, 2 * F) for h in range(2)] for s in range(WSLOTS)]
        down = [[cut(ring, s * SLOT + 8192 + h * 2048, 2, D) for h in range(2)] for s in range(WSLOTS)]
        xg = [cut(work, s * D, D) for s in range(WSLOTS)]
        xgT = cut(work, 3072, KD, P)
        yo = [cut(work, 4096 + s * D, D) for s in range(WSLOTS)]
        hs = cut(work, 7168, F)
        hgu = cut(work, 7424, F)
        hT = cut(work, 7680, 2, P)
        back = [cut(ring, i * 2048, 2, D) for i in range(NT + 1)]

        ident = sb("ident", [P, P])
        tri = sb("tri", [P, P])
        ones = sb("ones", [P, P])
        NSMALL = AT["limits"][0] + 8 - AT["head"][0]
        small = sb("small", [P, NSMALL])
        logc = cut(rt, 0, SEQ)
        slogc = cut(rt, 512, 257)
        raw_s, neg_s, prob_s = (cut(rt, 769 + i * 257, 257) for i in range(3))

        def sm(name):
            o, n = AT[name]
            o -= AT["head"][0]
            return small[:, o:o + n]

        gains = sb("gains", [P, 32])
        gain_rows = cut(rt, 1540, 60)
        gain_in = cut(work, 3072, P)
        gqk = cut(work, 3200, 2, DH)
        state_in = cut(rt, 1026, DC)
        wr = sb("wr", [P, KD, G + E])
        logits = sb("logits", [P, NT + 1, G + E])
        st = sb("st", [P, 184])
        pay_sb = sb("pay_sb", [P, NT + 1, 2, 2], U32)
        tbl = sb("tbl", [P, PAIRS, 2], U32)
        idx = sb("idx", [P, WSLOTS, 2], U32)
        addr = sb("addr", [P, 2, NT + 1], U32)
        flag = sb("flag", [P, 1], I32)
        ov_list = sb("ov_list", [1, 2, 2 * OV_PAIRS], I32)

        ssx, stdx, rx = st[:, 0:5], st[:, 5:10], st[:, 10:15]
        zss, zstd, zr = st[:, 15:21], st[:, 21:27], st[:, 27:33]
        den = st[:, 160:184]
        rden = [st[:, 140 + 2 * i:142 + 2 * i] for i in range(2)]
        nmax = st[:, 47:51]
        ssa, ra = st[:, 51:56], st[:, 56:61]
        ssc, rc = st[:, 61:66], st[:, 66:71]
        stda = st[:, 71:76]
        sself = st[:, 76:88]
        smask = st[:, 88:100]
        nm_s, den_s, rden_s = st[:, 100:101], st[:, 101:102], st[:, 102:103]
        self8 = st[:, 103:111]
        ssf, stdf, rf = st[:, 111:116], st[:, 116:121], st[:, 121:126]
        eps = st[:, 126:127]
        selfT = raw_s[0:DEC, 0:DEC * H]
        sc = cut(rt, 1283, 2, DEC * H)
        w12 = st[:, 130:140].rearrange("p (k t) -> p k t", k=2)

        names = """const_in x_in xs_in gains_in misc_in table_in wr_in wout_in logc_in
            x_squared x_std x_scaled x_turned x_evac gains_turned gains_evac rope_ready pads_zero
            z_done z_squared z_ssq z_std z_copied z_cos z_sin rot_done rot_turned rot_evac v_evac rows_out
            part_done part_evac comb_done comb_read blk_done blk_evac cu_ready conv_done y_squared y_gained ssc_done
            ssc_std conv_std state_turned conv_turned conv_evac conv_out
            qb_done qb_used scores_s turned_s self_spread soft_in soft_done probs_turned probs_placed v_used pv_s head_done
            gathered_s attn_s_done
            s_done masked exp_done p_turned p_evac o_done o_evac
            a_squared a_std a_r a_turned a_evac op_done op_evac opp_evac h_done
            h_squared h_std h_scaled h_turned h_evac r_done r_evac hn_out_sem
            r_exp1 r_sub r_sub2 r_exp2 assign count_done addr_done list_done scattered tbl_in idx_ready ov_in
            xg_in xg_turned xg_evac gu_done silu_done act_done ht_done ht_evac dn_done dn_evac_a dn_evac_v res_out
            y_ready y_out ov_done gather_go scatter_go dve_link act_link pool_link flag_ready zero_rows""".split()
        S = {n: sem(n) for n in names}
        w_in_s = [sem(f"w_loaded{i}") for i in range(WRING)]
        kv_in = [sem(f"kv_loaded{i}") for i in range(2)]
        ew_in = [sem(f"expert_loaded{i}") for i in range(WSLOTS)]
        xg_sem = [sem(f"xg_in{i}") for i in range(WSLOTS)]
        res_sem = [sem(f"res_out{i}") for i in range(WSLOTS)]
        hn_sem = [sem(f"hn_out{i}") for i in range(2)]
        rot_out = [sem(f"rot_out{i}") for i in range(2)]
        back_in = [sem(f"back_in{i}") for i in range(NT + 1)]
        x_in = [sem(f"x_in{i}") for i in range(NT + 1)]

        w_in_v = w_in[0].rearrange("(k p) n -> p k n", p=P)
        w_out_v = w_out[0].rearrange("(k p) n -> p k n", p=P)
        x_rows = x_prompt[0].rearrange("(t p) d -> t p d", p=P)
        xs_rows = x_sample.rearrange("b t d -> (b t) d")
        k_out = k_prompt[0, 0].rearrange("(t p) h d -> t p (h d)", p=P)
        v_out = v_prompt[0, 0].rearrange("(t p) h d -> p t (h d)", p=P)
        y_rows = y_prompt[0].rearrange("(t p) d -> t p d", p=P)
        ys_rows = y_sample.rearrange("b t d -> (b t) d")
        ck = cache_k[0].rearrange("b r h d -> b r (h d)")
        cv = cache_v[0].rearrange("b r h d -> b r (h d)")

        def bc(ap, axis, n, shape):
            return ap.unsqueeze(axis).to_broadcast(shape)

        class Chain:
            def __init__(self, eng, s):
                self.eng, self.s, self.n = eng, s, 0

            def step(self, ins):
                self.n += 1
                ins.then_inc(self.s, 1)
                self.eng.wait_ge(self.s, self.n)

        block = ctx.enter_context(nc.Block())
        def unit(c, t):
            return c * NT + t

        def state_cols(h):
            return state_in[0:16, h * P:(h + 1) * P]

        def r(off, *dims):
            return cut(rt, off, *dims)

        T5 = NT + 1
        assigned = r(0, 160)
        e12 = r(160, 2, T5, E)
        tmp = r(480, 2, T5, E)
        posn = r(800, T5, E)
        total = r(960, E)
        leg, cand, cand2 = r(992, T5, EG), r(1032, T5, EG), r(1072, T5, EG)
        oh1, oh2 = r(1112, T5, EG), r(1152, T5, EG)
        ohg, cg, eg = r(1192, T5, G), r(1212, T5, G), r(1232, T5, G)
        gm, gsum, pg, m1, m2, dd, e2, mn = (r(1252 + 5 * i, T5) for i in range(8))
        pk, mr, ov, isov = (r(1292 + 10 * i, 2, T5) for i in range(4))
        nb, cum_a, cum_b = r(1332, E), r(1364, E), r(1396, E)
        lst, lst2 = r(1428, 2 * OV_PAIRS), r(1446, 2 * OV_PAIRS)

        @block.sync
        def _(sp):
            def cseg(name, dst):
                o, n = AT[name]
                return sp.dma_start(dst, const[:, o:o + n])

            for t in range(NT):
                sp.dma_start(x[:, t, :], x_rows[t]).then_inc(x_in[t], 16)
                if t == 0:
                    cseg("ident", ident[:, :]).then_inc(S["const_in"], 16)
                    for r, (g, n) in enumerate(((g_norm_mix, 8), (g_norm_ffn, 8), (g_attn_out, 6), (g_conv_out, 2))):
                        r0 = (0, 8, 16, 22)[r]
                        sp.dma_start(gain_in[r0:r0 + n, :], g[0].rearrange("(k p) -> k p", p=P)).then_inc(S["gains_in"], 16)
                    sp.dma_start(gain_in[24:30, :], w_conv[0].rearrange("j (k p) -> (j k) p", p=P)).then_inc(S["gains_in"], 16)
            sp.dma_start(x[0:DEC, NT, :], xs_rows).then_inc(x_in[NT], 16)
            for c in range(WRING):
                sp.dma_start(wchunk[c], w_in_v[:, :, c * CW:(c + 1) * CW]).then_inc(w_in_s[c], 16)
            cseg("cos", cos.rearrange("p a b -> p (a b)")).then_inc(S["misc_in"], 16)
            cseg("sin", sin.rearrange("p a b -> p (a b)")).then_inc(S["misc_in"], 16)
            sp.dma_start(gqk[:, 0, :], g_q[0].partition_broadcast(P)).then_inc(S["misc_in"], 16)
            sp.dma_start(gqk[:, 1, :], g_k[0].partition_broadcast(P)).then_inc(S["misc_in"], 16)
            sp.dma_start(state_in[0:2 * DEC, :], state_conv[0].rearrange("b j c -> (b j) c")).then_inc(S["misc_in"], 16)
            sp.dma_start(small[:, :], const[:, AT["head"][0]:AT["head"][0] + NSMALL]).then_inc(S["misc_in"], 16)
            cseg("logc", logc).then_inc(S["logc_in"], 16)
            cseg("slogc", slogc).then_inc(S["logc_in"], 16)
            cseg("tri", tri[:, :]).then_inc(S["wr_in"], 16)
            cseg("ones", ones[:, :]).then_inc(S["wr_in"], 16)
            sp.dma_start(wr[:, :, 0:G], w_router_group[0].rearrange("(k p) n -> p k n", p=P)).then_inc(S["wr_in"], 16)
            sp.dma_start(wr[:, :, G:G + E], w_router_expert[0].rearrange("(k p) n -> p k n", p=P)).then_inc(S["wr_in"], 16)
            sp.dma_start(pay_sb[:, :, :, :].rearrange("p t k w -> p (t k w)"), pay).then_inc(S["wr_in"], 16)
            sp.dma_start(table.rearrange("(p n) w -> p (n w)", p=P), empty).then_inc(S["table_in"], 16)
            sp.dma_start(conv_sample[0, :, 0, :], state_conv[0, :, 1, :]).then_inc(S["conv_out"], 16)

            def cached(b, src, s):
                sp.dma_start(kv[b % 2][:, 0, :], src[b, WBUF - P:WBUF, :]).then_inc(s, 16)
                sp.dma_start(kv[b % 2][0:96, 1, :], src[b, 512:896:4, :]).then_inc(s, 16)
                sp.dma_start(kv[b % 2][96:128, 1, :], src[b, 0:512:16, :]).then_inc(s, 16)

            def wload(c):
                if c - WRING < QKV_CHUNKS:
                    sp.wait_ge(S["part_done"], c - WRING + 1)
                sp.dma_start(wchunk[c % WRING], w_in_v[:, :, c * CW:(c + 1) * CW]).then_inc(w_in_s[c % WRING], 16)

            for b in range(2):
                cached(b, ck, kv_in[b])
            wload(3)
            wload(4)
            sp.dma_start(wout, w_out_v).then_inc(S["wout_in"], 16)
            for c in (5, 6, 7):
                wload(c)
                if c == 6:
                    for t in range(NT):
                        pass
            for b in range(2, DEC):
                sp.wait_ge(S["scores_s"], b - 1)
                cached(b, ck, kv_in[b % 2])
            for b in range(2):
                sp.wait_ge(S["scores_s"], DEC - 1 + b)
                cached(b, cv, kv_in[b])
            sp.wait_ge(S["v_evac"], 2 * NT)
            sp.dma_start(v_out, v_rows).then_inc(S["rows_out"], 16)
            sp.wait_ge(S["comb_read"], QKV_CHUNKS)
            sp.dma_start(k_sample[0].rearrange("b t h d -> (b t) (h d)"), ks[0:DEC, :]).then_inc(S["rows_out"], 16)
            sp.dma_start(v_sample[0].rearrange("b t h d -> (b t) (h d)"), vs[0:DEC, :]).then_inc(S["rows_out"], 16)
            for b in range(2, DEC):
                sp.wait_ge(S["v_used"], b - 1)
                cached(b, cv, kv_in[b % 2])
            sp.wait_ge(S["conv_evac"], 1)
            sp.dma_start(conv_prompt[0, 0], conv_rows[0:2, 0:DC]).then_inc(S["conv_out"], 16)
            sp.dma_start(conv_sample[0, :, 1, :], conv_rows[0:DEC, DC:2 * DC]).then_inc(S["conv_out"], 16)

            def expert(e_a, e_b, s):
                for h, e in ((0, e_a), (1, e_b)):
                    for w, o in ((w_gate, 0), (w_up, F)):
                        sp.dma_start(gate_up[s][h][:, :, o:o + F],
                                     w[0, ds(e, 1)].rearrange("e (k p) f -> p (e k) f", p=P)).then_inc(ew_in[s], 16)
                    sp.dma_start(down[s][h], w_down[0, ds(e, 1)].rearrange("e (k p) n -> p (e k) n", p=P)).then_inc(ew_in[s], 16)

            sp.wait_ge(S["a_turned"], 2 * NT + 1)
            sp.wait_ge(S["a_squared"], NT + 1)
            sp.wait_ge(S["rows_out"], 48)
            sp.wait_ge(S["conv_out"], 48)
            expert(0, 1, 0)
            expert(2, 3, 1)
            sp.wait_ge(S["op_done"], 4 * NT + 2)
            expert(4, 5, 2)
            with sp.Fori(0, 4) as j:
                for s in range(WSLOTS):
                    i = 3 * j + 3 + s
                    sp.wait_ge(S["dn_done"], i - 2)
                    expert(2 * i, 2 * i + 1, s)
            sp.wait_ge(S["dn_done"], 13)
            expert(30, 31, 0)
            sp.wait_ge(S["flag_ready"], 1)
            more = sp.value_load(flag[0:1, 0:1], min_val=0, max_val=1)
            with sp.If(more > 0):
                sp.wait_ge(S["list_done"], 1)
                with sp.Fori(0, OV_PAIRS // 3) as j:
                    for n, s in enumerate((1, 2, 0)):
                        i = 3 * j + 16 + n
                        k = 2 * (3 * j + n)
                        ea = sp.value_load(ov_list[0:1, 0, ds(k, 1)], min_val=0, max_val=E - 1)
                        eb = sp.value_load(ov_list[0:1, 0, ds(k + 1, 1)], min_val=0, max_val=E - 1)
                        sp.wait_ge(S["dn_done"], i - 2)
                        expert(ea, eb, s)
                sp.nop()
            sp.wait_ge(S["y_ready"], 1)
            res_pairs = results.rearrange("(t k) d -> t k d", k=2)
            for t in range(NT + 1):
                n = TILES[t]
                sp.dma_start(back[t][0:n], res_pairs[t * P:t * P + n]).then_inc(back_in[t], 16)
            for t in range(NT + 1):
                sp.wait_ge(S["h_done"], NT + 1 + t + 1)
                sp.dma_start(y_rows[t] if t < NT else ys_rows, x[0:TILES[t], t, :]).then_inc(S["y_out"], 16)
            sp.wait_ge(S["y_out"], 16 * (NT + 1))
            sp.wait_ge(S["rows_out"], 48)
            sp.wait_ge(S["conv_out"], 48)
            sp.wait_ge(rot_out[0], 16 * NT)
            sp.wait_ge(rot_out[1], 16 * NT)

        @block.tensor
        def _(pe):
            pe.wait_ge(S["const_in"], 16)
            pe.wait_ge(S["gains_in"], 80)
            pe.transpose(bank[7][:, 0:30], gain_in[0:30, :], ident[0:30, 0:30]).then_inc(S["gains_turned"], 1)
            for g in range(2 * NT + 1):
                t = g // 2
                pe.wait_ge(S["x_scaled"], t + 1)
                if g >= 3:
                    pe.wait_ge(S["x_evac"], g - 2)
                if t < NT:
                    for k in range(4):
                        o = (4 * (g % 2) + k) * P
                        last = pe.transpose(bank[g % 3][:, k * P:(k + 1) * P], xn[:, t, o:o + P], ident[:, :])
                else:
                    for k in range(KD):
                        last = pe.transpose(bank[g % 3][:, k * DEC:(k + 1) * DEC], xn[0:DEC, t, k * P:(k + 1) * P],
                                            ident[0:DEC, 0:DEC])
                last.then_inc(S["x_turned"], 1)
            pe.wait_ge(S["x_evac"], 2 * NT + 1)
            pe.wait_ge(S["pads_zero"], 1)

            def turn_rot(c, t):
                n = unit(c, t)
                pe.wait_ge(S["rot_done"], n + 1)
                if n >= 1:
                    pe.wait_ge(S["rot_evac"], n)
                for j in range(3):
                    last = pe.transpose(bank[5][:, j * P:(j + 1) * P], rot[n % 2][:, j * P:(j + 1) * P], ident[:, :])
                last.then_inc(S["rot_turned"], 1)

            def combine(c):
                pe.wait_ge(S["part_evac"], c + 1)
                if c >= 1:
                    pe.wait_ge(S["comb_read"], c)
                pe.matmul(bank[4][0:DEC, 0:CW], sm("quad"), partial, start=True, stop=True).then_inc(S["comb_done"], 1)

            def spread_q(b):
                if b >= 1:
                    pe.wait_ge(S["qb_used"], b)
                else:
                    pe.wait_ge(S["rope_ready"], 3)
                for j in range(2):
                    last = pe.matmul(bank[6 + j][:, 0:CW], ident[0:DEC, b:b + 1].to_broadcast([DEC, P]),
                                     qs[0:DEC, j * CW:(j + 1) * CW], start=True, stop=True)
                last.then_inc(S["qb_done"], 1)

            pend = []
            for c in range(QKV_CHUNKS):
                pe.wait_ge(w_in_s[c % WRING], 16 * (c // WRING + 1))
                w = wchunk[c % WRING]
                for t in range(NT):
                    n = unit(c, t)
                    if 3 <= n < QK_CHUNKS * NT + 3:
                        pe.wait_ge(S["z_copied"], n - 2 if n - 3 < QK_CHUNKS * NT else 0)
                    elif n >= 3:
                        pe.wait_ge(S["v_evac"], n - 2 - QK_CHUNKS * NT)
                    for k in range(KD):
                        last = pe.matmul(bank[n % 3][:, 0:CW], xT[:, k, t * P:(t + 1) * P], w[:, k, :],
                                         start=(k == 0), stop=(k == KD - 1))
                    last.then_inc(S["z_done"], 1)
                    if t == 1 and c >= 1:
                        combine(c - 1)
                    if c < QK_CHUNKS:
                        pend.append((c, t))
                    if len(pend) > 2 or (c >= QK_CHUNKS and pend):
                        turn_rot(*pend.pop(0))
                    if c >= QK_CHUNKS and not (c == QK_CHUNKS and t < 2):
                        spread_q((c - QK_CHUNKS) * NT + t - 2)
                if c >= 1:
                    pe.wait_ge(S["part_evac"], c)
                for k in range(KD):
                    q = k % 4
                    last = pe.matmul(bank[3][32 * q:32 * q + 32, 0:CW], xsT[:, k, :], w[:, k, :],
                                     start=(k < 4), stop=(k >= 4))
                last.then_inc(S["part_done"], 1)
            for cb in range(6):
                c = QKV_CHUNKS + cb // 3
                if cb % 3 == 0:
                    pe.wait_ge(w_in_s[c % WRING], 16 * (c // WRING + 1))
                w = wchunk[c % WRING]
                o = (cb % 3) * P
                if cb < 3:
                    pe.wait_ge(S["v_evac"], 2 * NT - 2 + cb)
                if cb >= 2:
                    pe.wait_ge(S["blk_evac"], cb - 1)
                if cb == 0:
                    pe.wait_ge(S["part_evac"], QKV_CHUNKS)
                if cb == 1:
                    pe.wait_ge(S["rot_evac"], QK_CHUNKS * NT)
                for k in range(KD):
                    pe.matmul(bank[cb % 3][:, :], w[:, k, o:o + P], xT[:, k, :], start=(k == 0), stop=(k == KD - 1))
                    last = pe.matmul(bank[3 + 2 * (cb % 2)][:, 0:DEC], w[:, k, o:o + P], xsT[:, k, 0:DEC],
                                     start=(k == 0), stop=(k == KD - 1))
                last.then_inc(S["blk_done"], 1)
                if cb == 0:
                    combine(QKV_CHUNKS - 1)
                    spread_q(6)
                if cb == 1:
                    spread_q(7)
            pe.wait_ge(S["misc_in"], 96)
            pe.wait_ge(S["comb_read"], QKV_CHUNKS)
            for h in range(2):
                last = pe.transpose(bank[4][:, h * 16:h * 16 + 16], state_cols(h), ident[0:16, 0:16])
            last.then_inc(S["state_turned"], 1)

            pe.wait_ge(S["scores_s"], DEC + 1)
            pe.wait_ge(S["qb_used"], DEC)
            for i in range(2):
                last = pe.transpose(bank[6][0:DEC * H, i * P:(i + 1) * P], sc[:, i, :], ident[:, :])
            last.then_inc(S["turned_s"], 1)
            pe.matmul(bank[7][0:DEC * H, 0:H], sm("sampleT")[0:DEC, :], sself[0:DEC, :], start=True, stop=True)\
                .then_inc(S["self_spread"], 1)
            pe.wait_ge(S["conv_done"], 1)
            pe.wait_ge(S["cu_ready"], 2)
            for h in range(2):
                pe.transpose(bank[4][0:2, h * P:(h + 1) * P], cuT[:, h, SEQ:SEQ + 2], ident[:, :])
                last = pe.transpose(bank[4][0:DEC, DC + h * P:DC + (h + 1) * P], cu_s[:, h, 2, :], ident[:, :])
            last.then_inc(S["conv_turned"], 1)
            pe.wait_ge(S["y_squared"], 1)
            pe.wait_ge(S["wr_in"], 80)
            pe.wait_ge(S["cu_ready"], 2)
            for t in range(NT + 1):
                n = TILES[t]
                for h in range(2):
                    last = pe.matmul(bank[3][0:n, 64 + t:65 + t], ysq[:, h, t * P:t * P + n], ones[:, 0:1],
                                     start=(h == 0), stop=(h == 1))
            last.then_inc(S["ssc_done"], 1)
            pe.wait_ge(S["soft_done"], 2)
            for i in range(2):
                last = pe.transpose(bank[5][:, i * 96:(i + 1) * 96], prob_s[0:DEC * H, i * P:(i + 1) * P],
                                    ident[0:DEC * H, 0:DEC * H])
            pe.transpose(bank[5][0:DEC, 192:192 + DEC * H], self8[0:DEC * H, :], ident[0:DEC * H, 0:DEC * H])\
                .then_inc(S["probs_turned"], 1)
            pe.wait_ge(S["probs_placed"], 1)
            for b in range(DEC):
                pe.wait_ge(kv_in[b % 2], 48 * (DEC // 2 + b // 2 + 1))
                for i in range(2):
                    for j in range(2):
                        last = pe.matmul(bank[6 + j][0:DEC * H, 0:CW], probs_s[:, i, b, :], kv[b % 2][:, i, j * CW:(j + 1) * CW],
                                         start=(b == 0 and i == 0), stop=False)
                last.then_inc(S["v_used"], 1)
            for j in range(2):
                last = pe.matmul(bank[6 + j][0:DEC * H, 0:CW], selfT, vs[0:DEC, j * CW:(j + 1) * CW], start=False, stop=True)
            last.then_inc(S["pv_s"], 1)
            pe.wait_ge(S["head_done"], 2)
            for j in range(2):
                last = pe.matmul(bank[3 + j][0:DEC, 0:CW], sm("sample")[0:DEC * H, :],
                                 head_out[0:DEC * H, j * CW:(j + 1) * CW], start=True, stop=True)
            last.then_inc(S["gathered_s"], 1)

            pe.wait_ge(S["attn_s_done"], 1)
            units = [(qt, h) for qt in range(NT) for h in range(H)]
            NU = len(units)
            for s in range(NU + 2):
                if s < NU:
                    qt, h = units[s]
                    n = (qt + 1) * P
                    if s >= 3:
                        pe.wait_ge(S["masked"], s - 2)
                    o = DH * (h % 2)
                    pe.matmul(bank[s % 3][:, 0:n], qT[o:o + DH, h // 2, qt * P:(qt + 1) * P], kT[o:o + DH, h // 2, 0:n],
                              start=True, stop=True).then_inc(S["s_done"], 1)
                if 1 <= s <= NU:
                    u = s - 1
                    qt, h = units[u]
                    pe.wait_ge(S["exp_done"], u + 1)
                    if u >= 2:
                        pe.wait_ge(S["p_evac"], u - 1)
                    for j in range(qt + 1):
                        last = pe.transpose(bank[3 + u % 2][:, j * P:(j + 1) * P], scores_sb[u % 2][:, j * P:(j + 1) * P],
                                            ident[:, :])
                    last.then_inc(S["p_turned"], 1)
                if s >= 2:
                    u = s - 2
                    qt, h = units[u]
                    pe.wait_ge(S["p_evac"], u + 1)
                    if h % 2 == 0 and u >= 4:
                        pe.wait_ge(S["o_evac"], u // 2 - 1)
                    for j in range(qt + 1):
                        last = pe.matmul(bank[5 + (u // 2) % 2][:, (h % 2) * DH:(h % 2 + 1) * DH],
                                         probs_t[u % 2][:, j * P:(j + 1) * P], v_rows[:, j, h * DH:(h + 1) * DH],
                                         start=(j == 0), stop=(j == qt))
                    last.then_inc(S["o_done"], 1)

            for g in range(2 * NT + 1):
                t = g // 2
                if g >= 2:
                    pe.wait_ge(S["a_evac"], g - 1)
                if t < NT:
                    pe.wait_ge(S["o_evac"], NP * NT)
                    for k in range(3):
                        o = (3 * (g % 2) + k) * P
                        last = pe.transpose(bank[g % 2][:, k * P:(k + 1) * P], attn[:, t, o:o + P], ident[:, :])
                else:
                    for k in range(NP):
                        last = pe.transpose(bank[g % 2][:, k * DEC:(k + 1) * DEC], attn_s[0:DEC, k * P:(k + 1) * P],
                                            ident[0:DEC, 0:DEC])
                last.then_inc(S["a_turned"], 1)
            pe.wait_ge(S["wout_in"], 16)
            pe.wait_ge(S["a_evac"], 2 * NT + 1)
            pe.wait_ge(S["y_gained"], 1)

            def turn_h(t):
                pe.wait_ge(S["h_scaled"], t + 1)
                n = TILES[t]
                for g in range(2):
                    if 2 * t + g >= 2:
                        pe.wait_ge(S["h_evac"], 2 * t + g - 1)
                    for k in range(4):
                        o = (4 * g + k) * P
                        last = pe.transpose(bank[4 + g][:, k * P:k * P + n], hn[t % 2][0:n, o:o + P], ident[0:n, 0:n])
                    last.then_inc(S["h_turned"], 1)

            def route(t):
                pe.wait_ge(S["h_evac"], 2 * t + 2)
                if t >= 1:
                    pe.wait_ge(S["r_evac"], t)
                for k in range(KD):
                    last = pe.matmul(bank[6][0:TILES[t], 0:G + E], hnT[t % 2][:, k, 0:TILES[t]], wr[:, k, :],
                                     start=(k == 0), stop=(k == KD - 1))
                last.then_inc(S["r_done"], 1)

            for t in range(NT):
                for g in range(4):
                    u = 4 * t + g
                    if u >= 4:
                        pe.wait_ge(S["op_evac"], u - 3)
                    cols = slice((g % 2) * 512, (g % 2 + 1) * 512)
                    rng = range(NP) if g < 2 else range(NP, KD)
                    for k in rng:
                        src = attnT[:, k, t * P:(t + 1) * P] if k < NP else yT[:, k - NP, t * P:(t + 1) * P]
                        last = pe.matmul(bank[u % 4][:, :], src, wout[:, k, cols], start=(k == rng[0]), stop=(k == rng[-1]))
                    last.then_inc(S["op_done"], 1)
                if t >= 1:
                    turn_h(t - 1)
                if t >= 2:
                    route(t - 2)
            for j in range(2):
                pe.wait_ge(S["op_evac"], 4 * NT - 3 + j)
                for k in (0, 2, 4, 6, 1, 3, 5, 7):
                    q = k // 2
                    last = pe.matmul(bank[j][32 * q:32 * q + 32, :], mixsT[:, k, :], wout[:, k, j * 512:(j + 1) * 512],
                                     start=(k % 2 == 0), stop=(k % 2 == 1))
                last.then_inc(S["op_done"], 1)
            turn_h(NT - 1)
            route(NT - 2)
            pe.wait_ge(S["opp_evac"], 2)
            for g in range(4):
                pe.wait_ge(S["op_evac"], min(4 * NT - 3 + g, 4 * NT) if g >= 2 else 4 * NT)
                part = partial_o[:, (g % 2) * 512:(g % 2 + 1) * 512]
                pe.matmul(bank[g][0:DEC, :], sm("quada" if g < 2 else "quadc"), part, start=True, stop=True)\
                    .then_inc(S["op_done"], 1)
            route(NT - 1)
            turn_h(NT)
            route(NT)

            pe.wait_ge(S["assign"], 1)
            pe.wait_ge(S["r_evac"], NT + 1)
            pe.matmul(bank[6][:, 0:160], tri[:, :], assigned, start=True, stop=True)
            pe.matmul(bank[7][:, 0:160], ones[:, :], assigned, start=True, stop=True).then_inc(S["count_done"], 1)

            def pair(i, s, turn, first):
                if not first:
                    pe.wait_ge(S["silu_done"], i)
                    pe.wait_ge(S["act_done"], i)
                pe.wait_ge(S["xg_evac"], i + 1)
                pe.wait_ge(ew_in[s], turn)
                for k in range(KD):
                    for h in range(2):
                        last = pe.matmul(bank[2][64 * h:64 * h + 64, :], xgT[:, k, 64 * h:64 * h + 64],
                                         gate_up[s][h][:, k, :], start=(k == 0), stop=(k == KD - 1))
                last.then_inc(S["gu_done"], 1)

            def turn_tokens(i, s, turn, first):
                pe.wait_ge(xg_sem[s], turn)
                if not first:
                    pe.wait_ge(S["xg_evac"], i)
                for k in range(KD):
                    last = pe.transpose(bank[k // 4][:, (k % 4) * P:(k % 4 + 1) * P], xg[s][:, k * P:(k + 1) * P], ident[:, :])
                last.then_inc(S["xg_turned"], 1)

            def pair_down(i, s, first):
                pe.wait_ge(S["act_done"], i + 1)
                for c in range(2):
                    last = pe.transpose(bank[3][:, c * P:(c + 1) * P], hgu[:, c * P:(c + 1) * P], ident[:, :])
                last.then_inc(S["ht_done"], 1)
                pe.wait_ge(S["ht_evac"], i + 1)
                if not first:
                    pe.wait_ge(S["dn_evac_a"], i)
                    pe.wait_ge(S["dn_evac_v"], i)
                for j in range(2):
                    for c in range(2):
                        for h in range(2):
                            last = pe.matmul(bank[4 + j][64 * h:64 * h + 64, :], hT[:, c, 64 * h:64 * h + 64],
                                             down[s][h][:, c, j * 512:(j + 1) * 512], start=(c == 0), stop=(c == 1))
                last.then_inc(S["dn_done"], 1)

            turn_tokens(0, 0, 16, True)
            pair(0, 0, 96, True)
            turn_tokens(1, 1, 16, False)
            pair_down(0, 0, True)
            with pe.Fori(0, 4) as j:
                for n, s in enumerate((1, 2, 0)):
                    i = 3 * j + 1 + n
                    pair(i, s, 96 * (j + 1) + (96 if s == 0 else 0), False)
                    turn_tokens(i + 1, (s + 1) % 3, 16 * (j + 1) + (16 if s != 1 else 0), False)
                    pair_down(i, s, False)
            for i in range(13, 16):
                s = i % 3
                pair(i, s, 96 * (i // 3 + 1), False)
                if i < 15:
                    turn_tokens(i + 1, (s + 1) % 3, 16 * ((i + 1) // 3 + 1), False)
                pair_down(i, s, False)
            pe.wait_ge(S["flag_ready"], 1)
            more = pe.value_load(flag[0:1, 0:1], min_val=0, max_val=1)
            with pe.If(more > 0):
                with pe.Fori(0, OV_PAIRS // 3) as j:
                    for n, s in enumerate((1, 2, 0)):
                        i = 3 * j + 16 + n
                        turn = j + 6 + (1 if s == 0 else 0)
                        turn_tokens(i, s, 16 * turn, False)
                        pair(i, s, 96 * turn, False)
                        pair_down(i, s, False)
                pe.nop()
            pe.nop()

        @block.scalar
        def _(act):
            chain = Chain(act, S["act_link"])
            act.wait_ge(S["pads_zero"], 1)
            for t in range(NT + 1):
                n = TILES[t]
                act.wait_ge(x_in[t], 16)
                chain.step(act.activation(junk_x[0:n, :], x[0:n, t, :], ACT.Square, accum_out=ssx[0:n, t:t + 1]))
                act.activation(stdx[0:n, t:t + 1], ssx[0:n, t:t + 1], ACT.Sqrt, bias=eps[0:n, :], scale=1.0 / D)\
                    .then_inc(S["x_std"], 1)

            def part_copy(c):
                act.wait_ge(S["part_done"], c + 1)
                if c >= 1:
                    act.wait_ge(S["comb_done"], c)
                act.activation(partial, bank[3][:, 0:CW], ACT.Copy).then_inc(S["part_evac"], 1)

            def rot_copy(c, t):
                act.wait_ge(S["rot_turned"], unit(c, t) + 1)
                dst = (qT if c < 2 else kT)[:, 3 * (c % 2):3 * (c % 2) + 3, t * P:(t + 1) * P]
                act.activation(dst, bank[5][:, 0:CW].rearrange("p (a b) -> p a b", a=3), ACT.Copy).then_inc(S["rot_evac"], 1)

            def root(src, w, k):
                act.activation(zsq[0:w, :], src, ACT.Square).then_inc(S["z_squared"], 1)
                act.wait_ge(S["z_ssq"], k + 1)
                act.activation(zstd[0:w, :], zss[0:w, :], ACT.Sqrt, bias=eps[0:w, :], scale=1.0 / DH).then_inc(S["z_std"], 1)

            k = 0
            pend = []
            for c in range(QKV_CHUNKS):
                for t in range(NT):
                    n = unit(c, t)
                    act.wait_ge(S["z_done"], n + 1)
                    if c < QK_CHUNKS:
                        root(bank[n % 3][:, 0:CW], P, k)
                        k += 1
                        pend.append((c, t))
                    else:
                        act.activation(v_rows[:, t, (c - 4) * CW:(c - 3) * CW], bank[n % 3][:, 0:CW], ACT.Copy)\
                            .then_inc(S["v_evac"], 1)
                    if t == 1 and c >= 1:
                        cc = c - 1
                        act.wait_ge(S["comb_done"], cc + 1)
                        if cc < QK_CHUNKS:
                            root(bank[4][0:DEC, 0:CW], DEC, k)
                            k += 1
                        else:
                            act.activation(vs[0:DEC, (cc - 4) * CW:(cc - 3) * CW], bank[4][0:DEC, 0:CW], ACT.Copy)\
                                .then_inc(S["comb_read"], 1)
                    if len(pend) > 2 or (c >= QK_CHUNKS and pend):
                        rot_copy(*pend.pop(0))
                    if t == 0 and c >= 1:
                        pass
                part_copy(c)
            for cb in range(4):
                act.wait_ge(S["blk_done"], cb + 1)
                if cb < 2:
                    act.activation(bT[:, cb, 0:SEQ], bank[cb % 3][:, :], ACT.Copy)
                    act.activation(bT[:, cb, SEQ:TOK], bank[3 + 2 * (cb % 2)][:, 0:DEC], ACT.Copy).then_inc(S["blk_evac"], 1)
                else:
                    act.activation(cuT[:, cb - 2, 2:2 + SEQ], bank[cb % 3][:, :], ACT.Copy)
                    act.activation(cu_s[:, cb - 2, 2, :], bank[3 + 2 * (cb % 2)][:, 0:DEC], ACT.Copy).then_inc(S["blk_evac"], 1)
                if cb == 0:
                    act.wait_ge(S["comb_done"], QKV_CHUNKS)
                    act.activation(vs[0:DEC, CW:2 * CW], bank[4][0:DEC, 0:CW], ACT.Copy).then_inc(S["comb_read"], 1)
            act.wait_ge(S["state_turned"], 1)
            for h in range(2):
                act.activation(cu_s[:, h, 0:2, :], bank[4][:, h * 16:h * 16 + 16].rearrange("p (b j) -> p j b", j=2), ACT.Copy)\
                    .then_inc(S["cu_ready"], 1)
            act.wait_ge(S["conv_done"], 1)
            act.activation(ysq, yT, ACT.Square).then_inc(S["y_squared"], 1)
            act.wait_ge(S["conv_turned"], 1)
            act.activation(conv_rows[0:2, 0:DC], bank[4][0:2, 0:DC], ACT.Copy)
            act.activation(conv_rows[0:DEC, DC:2 * DC], bank[4][0:DEC, DC:2 * DC], ACT.Copy).then_inc(S["conv_evac"], 1)
            act.wait_ge(S["ssc_done"], 1)
            act.activation(ssc[:, 0:NT], bank[3][:, 64:64 + NT], ACT.Sqrt, bias=eps, scale=1.0 / DC)
            act.activation(ssc[0:DEC, NT:NT + 1], bank[3][0:DEC, 64 + NT:65 + NT], ACT.Sqrt, bias=eps[0:DEC, :],
                           scale=1.0 / DC).then_inc(S["ssc_std"], 1)
            act.wait_ge(S["soft_in"], 1)
            act.activation(prob_s[0:96, :], neg_s[0:96, :], ACT.Exp, bias=nm_s[0:96, :], scale=-1.0,
                           accum_out=den_s[0:96, :]).then_inc(S["soft_done"], 1)

            units = [(qt, h) for qt in range(NT) for h in range(H)]
            NU = len(units)
            for s in range(NU + 1):
                if s < NU:
                    qt, h = units[s]
                    n = (qt + 1) * P
                    act.wait_ge(S["masked"], s + 1)
                    buf = scores_sb[s % 2][:, 0:n]
                    if qt >= 2 and h == 0:
                        act.wait_ge(S["o_evac"], NP * (qt - 1))
                    act.activation(buf, buf, ACT.Exp, bias=nmax[:, s % 4:s % 4 + 1], scale=-1.0,
                                   accum_out=den[:, s % 24:s % 24 + 1]).then_inc(S["exp_done"], 1)
                if s >= 1:
                    u = s - 1
                    n = (units[u][0] + 1) * P
                    act.wait_ge(S["p_turned"], u + 1)
                    if u >= 2:
                        act.wait_ge(S["o_done"], u - 1)
                    act.activation(probs_t[u % 2][:, 0:n], bank[3 + u % 2][:, 0:n], ACT.Copy).then_inc(S["p_evac"], 1)
            act.wait_ge(S["o_evac"], NP * NT)
            act.wait_ge(S["rows_out"], 48)
            for t in range(NT):
                if t:
                    act.wait_ge(S["a_squared"], t)
                act.activation(junk[:, 0:DA], attn[:, t, :], ACT.Square, accum_out=ssa[:, t:t + 1]).then_inc(S["a_squared"], 1)
            act.wait_ge(S["a_squared"], NT)
            act.activation(junk[0:DEC, 0:DA], attn_s[0:DEC, :], ACT.Square, accum_out=ssa[0:DEC, NT:NT + 1])\
                .then_inc(S["a_squared"], 1)
            act.wait_ge(S["a_squared"], NT + 1)
            act.activation(stda[:, 0:NT], ssa[:, 0:NT], ACT.Sqrt, bias=eps, scale=1.0 / DA)
            act.activation(stda[0:DEC, NT:NT + 1], ssa[0:DEC, NT:NT + 1], ACT.Sqrt, bias=eps[0:DEC, :], scale=1.0 / DA)\
                .then_inc(S["a_std"], 1)
            for t in range(NT + 1):
                n = TILES[t]
                if t == NT:
                    for j in range(2):
                        act.wait_ge(S["op_done"], 4 * NT + 1 + j)
                        act.activation(partial_o[:, j * 512:(j + 1) * 512], bank[j][:, :], ACT.Copy).then_inc(S["opp_evac"], 1)
                act.wait_ge(S["h_done"], t + 1)
                chain.step(act.activation(junk[0:n, :], x[0:n, t, :], ACT.Square, accum_out=ssf[0:n, t:t + 1]))
                act.activation(stdf[0:n, t:t + 1], ssf[0:n, t:t + 1], ACT.Sqrt, bias=eps[0:n, :], scale=1.0 / D)\
                    .then_inc(S["h_std"], 1)
            act.wait_ge(S["r_sub"], 1)
            act.activation(eg, eg, ACT.Exp).then_inc(S["r_exp1"], 1)
            act.wait_ge(S["r_sub2"], 1)
            act.activation(e2, dd, ACT.Exp).then_inc(S["r_exp2"], 1)

            def pair(i, s, turn, first):
                act.wait_ge(S["gu_done"], i + 1)
                if not first:
                    act.wait_ge(S["act_done"], i)
                act.activation(hs, bank[2][:, 0:F], ACT.Silu).then_inc(S["silu_done"], 1)
                act.wait_ge(S["ht_done"], i + 1)
                if not first:
                    act.wait_ge(S["dn_done"], i)
                act.activation(hT, bank[3][:, 0:2 * P].rearrange("p (c n) -> p c n", c=2), ACT.Copy).then_inc(S["ht_evac"], 1)
                if turn is not None:
                    act.wait_ge(res_sem[s], turn)
                act.wait_ge(S["dn_done"], i + 1)
                act.activation(yo[s][:, 0:512], bank[4][:, :], ACT.Copy).then_inc(S["dn_evac_a"], 1)

            act.wait_ge(S["count_done"], 1)
            for i in range(4):
                pair(i, i % 3, 16 * (i // 3) if i >= 3 else None, i == 0)
            with act.Fori(0, 4) as j:
                for n, s in enumerate((1, 2, 0)):
                    pair(3 * j + 4 + n, s, 16 * (j + 1) + (16 if s == 0 else 0), False)
            act.wait_ge(S["flag_ready"], 1)
            more = act.value_load(flag[0:1, 0:1], min_val=0, max_val=1)
            with act.If(more > 0):
                with act.Fori(0, OV_PAIRS // 3) as j:
                    for n, s in enumerate((1, 2, 0)):
                        pair(3 * j + 16 + n, s, 16 * (j + 5) + (16 if s == 0 else 0), False)
                act.nop()
            act.nop()

        @block.vector
        def _(dve):
            chain = Chain(dve, S["dve_link"])

            def tt(out, a, b, op):
                return dve.tensor_tensor(out, a, b, op)

            dve.memset(eps, EPS)
            dve.memset(xsT, 0.0)
            dve.memset(mixsT, 0.0)
            dve.memset(logits[:, :, :], 0.0).then_inc(S["pads_zero"], 1)
            dve.wait_ge(S["pads_zero"], 1)
            dve.wait_ge(S["gains_turned"], 1)
            chain.step(dve.tensor_copy(gains[:, 0:30], bank[7][:, 0:30]))

            def x_scale(t):
                n = TILES[t]
                dve.wait_ge(S["x_std"], t + 1)
                chain.step(dve.reciprocal(rx[0:n, t:t + 1], stdx[0:n, t:t + 1]))
                dve.tensor_scalar(xn[0:n, t, :], x[0:n, t, :], rx[0:n, t:t + 1], None, ALU.mult).then_inc(S["x_scaled"], 1)

            def x_copy(g):
                dve.wait_ge(S["x_turned"], g + 1)
                t = g // 2
                if t < NT:
                    k = 4 * (g % 2)
                    tt(xT[:, k:k + 4, t * P:(t + 1) * P], bank[g % 3][:, :].rearrange("p (a b) -> p a b", a=4),
                       bc(gains[:, k:k + 4], 2, P, [P, 4, P]), ALU.mult).then_inc(S["x_evac"], 1)
                else:
                    tt(xsT[:, :, 0:DEC], bank[g % 3][:, 0:KD * DEC].rearrange("p (a b) -> p a b", a=KD),
                       bc(gains[:, 0:KD], 2, DEC, [P, KD, DEC]), ALU.mult).then_inc(S["x_evac"], 1)

            x_scale(0)
            for t in range(NT + 1):
                if t < NT:
                    x_scale(t + 1)
                x_copy(2 * t)
                if t < NT:
                    x_copy(2 * t + 1)
            dve.wait_ge(S["misc_in"], 96)
            half = DH // 2
            for i, scale in ((0, DH ** -0.5), (1, 1.0)):
                g = gqk[:, i, :]
                dve.scalar_tensor_tensor(rope_g[2 * i], cos, scale, bc(g, 1, T5, [P, T5, DH]), ALU.mult, ALU.mult)
                for a in range(2):
                    b = 1 - a
                    last = dve.scalar_tensor_tensor(rope_g[2 * i + 1][:, :, a * half:(a + 1) * half],
                                                    sin[:, :, a * half:(a + 1) * half], scale,
                                                    bc(g[:, b * half:(b + 1) * half], 1, T5, [P, T5, half]),
                                                    ALU.mult, ALU.mult)
            last.then_inc(S["rope_ready"], 1)
            dve.wait_ge(S["rope_ready"], 1)

            def norm_rope(src, w, c, t, k, dst, out_sem):
                v6 = "p (a b) -> p a b"
                dve.wait_ge(S["z_squared"], k + 1)
                dve.tensor_reduce(zss[0:w, :], zsq[0:w, :].rearrange(v6, a=6), AX.X, ALU.add).then_inc(S["z_ssq"], 1)
                dve.wait_ge(S["z_std"], k + 1)
                chain.step(dve.reciprocal(zr[0:w, :], zstd[0:w, :]))
                if k >= 1:
                    dve.wait_ge(S["z_sin"], k)
                tt(zn[0:w, :].rearrange(v6, a=6), src.rearrange(v6, a=6), bc(zr[0:w, :], 2, DH, [w, 6, DH]), ALU.mult)\
                    .then_inc(S["z_copied" if w == P else "comb_read"], 1)
                if w == P:
                    dve.wait_ge(S["z_copied"], unit(c, t) + 1)
                else:
                    dve.wait_ge(S["comb_read"], c + 1)
                dve.engine_nop().then_inc(S["z_cos"], 1)
                chain.step(tt(zcos[0:w, :].rearrange(v6, a=6), zn[0:w, :].rearrange(v6, a=6),
                              bc(rope_g[2 * (c // 2)][0:w, t, :], 1, 6, [w, 6, DH]), ALU.mult))
                dve.wait_ge(S["z_sin"], k + 1)
                tt(dst, zcos[0:w, :], zsin[0:w, :], ALU.add).then_inc(out_sem, 1)

            k = 0
            for c in range(QK_CHUNKS + 1):
                for t in range(NT):
                    if c < QK_CHUNKS:
                        n = unit(c, t)
                        dve.wait_ge(S["z_done"], n + 1)
                        if n >= 2:
                            dve.wait_ge(S["rot_turned"], n - 1)
                            if n - 2 >= 2 * NT:
                                dve.wait_ge(rot_out[n % 2], 16 * ((n - 2 - 2 * NT) // 2 + 1))
                        norm_rope(bank[n % 3][:, 0:CW], P, c, t, k, rot[n % 2], S["rot_done"])
                        k += 1
                    if t == 1 and c >= 1:
                        cc = c - 1
                        dve.wait_ge(S["comb_done"], cc + 1)
                        norm_rope(bank[4][0:DEC, 0:CW], DEC, cc, NT, k, (qs if cc < 2 else ks)[0:DEC, (cc % 2) * CW:(cc % 2 + 1) * CW],
                                  S["rope_ready"])
                        k += 1
            dve.wait_ge(S["rope_ready"], 1 + QK_CHUNKS)
            for b in range(DEC):
                dve.wait_ge(kv_in[b % 2], 48 * (b // 2 + 1))
                dve.wait_ge(S["qb_done"], b + 1)
                kb = kv[b % 2]
                for j in range(2):
                    last = tt(kb[:, :, j * CW:(j + 1) * CW], kb[:, :, j * CW:(j + 1) * CW],
                              bc(bank[6 + j][:, 0:CW], 1, 2, [P, 2, CW]), ALU.mult)
                last.then_inc(S["qb_used"], 1)
                dve.wait_ge(S["qb_used"], b + 1)
                for i in range(2):
                    last = dve.tensor_reduce(sc[:, i, b * H:(b + 1) * H], kb[:, i, :].rearrange("p (h d) -> p h d", h=H),
                                             AX.X, ALU.add)
                last.then_inc(S["scores_s"], 1)
            chain.step(tt(head_out[0:DEC, :], qs[0:DEC, :], ks[0:DEC, :], ALU.mult))
            dve.tensor_reduce(sself[0:DEC, :], head_out[0:DEC, :].rearrange("p (h d) -> p h d", h=H), AX.X, ALU.add)\
                .then_inc(S["scores_s"], 1)

            for cb in range(4, 6):
                h = cb - 4
                dve.wait_ge(S["blk_done"], cb + 1)
                dve.wait_ge(S["blk_evac"], 4)
                tt(cuT[:, h, 2:2 + SEQ], cuT[:, h, 2:2 + SEQ], bank[cb % 3][:, :], ALU.mult)
                last = tt(cu_s[:, h, 2, :], cu_s[:, h, 2, :], bank[3 + 2 * (cb % 2)][:, 0:DEC], ALU.mult)
            dve.memset(cuT[:, :, 0:2], 0.0)
            chain.step(last) if False else None
            chain.step(dve.memset(nm_s, 0.0))
            dve.wait_ge(S["cu_ready"], 2)
            for j in range(3):
                for h in range(2):
                    tap = gains[:, 24 + 2 * j + h:25 + 2 * j + h]
                    for dst, src in ((yT[:, h, 0:SEQ], cuT[:, h, j:j + SEQ]), (yT[:, h, SEQ:TOK], cu_s[:, h, j, :])):
                        if j == 0:
                            last = dve.tensor_scalar(dst, src, tap, None, ALU.mult)
                        else:
                            last = dve.scalar_tensor_tensor(dst, src, tap, dst, ALU.mult, ALU.add)
                chain.step(last)
            tt(yT, yT, bT, ALU.mult).then_inc(S["conv_done"], 1)

            dve.wait_ge(S["turned_s"], 1)
            dve.wait_ge(S["self_spread"], 1)
            tt(smask[0:96, :], bank[7][0:96, 0:H], sm("head")[0:96, :], ALU.mult)
            chain.step(dve.tensor_copy(raw_s[0:96, 0:256], bank[6][0:96, 0:256]))
            chain.step(dve.tensor_reduce(raw_s[0:96, 256:257], smask[0:96, :], AX.X, ALU.add))
            dve.wait_ge(S["logc_in"], 32)
            dve.tensor_tensor_reduce(neg_s[0:96, :], raw_s[0:96, :], slogc[0:96, :], -1.0, 3.0e38, ALU.add, ALU.min,
                                     nm_s[0:96, :]).then_inc(S["soft_in"], 1)
            dve.wait_ge(S["y_squared"], 1)
            tt(yT, yT, bc(gains[:, 22:24], 2, TOK, [P, 2, TOK]), ALU.mult).then_inc(S["y_gained"], 1)
            dve.wait_ge(S["ssc_std"], 1)
            dve.reciprocal(rc[:, 0:NT], ssc[:, 0:NT])
            dve.reciprocal(rc[0:DEC, NT:NT + 1], ssc[0:DEC, NT:NT + 1]).then_inc(S["conv_std"], 1)
            dve.wait_ge(S["y_gained"], 1)
            dve.tensor_copy(mixsT[:, NP:KD, 0:DEC], yT[:, :, SEQ:TOK])
            dve.wait_ge(S["soft_done"], 1)
            dve.reciprocal(rden_s[0:96, :], den_s[0:96, :])
            dve.tensor_scalar(self8[0:96, :], sm("sample")[0:96, :], prob_s[0:96, 256:257], None, ALU.mult)\
                .then_inc(S["soft_done"], 1)
            dve.wait_ge(S["probs_turned"], 1)
            dve.wait_ge(S["zero_rows"], 1)
            turned = bank[5][:, 0:192].rearrange("p (i q) -> p i q", i=2)
            for b in range(DEC):
                dve.tensor_copy(probs_s[:, :, b, b * H:(b + 1) * H], turned[:, :, b * H:(b + 1) * H])
            dve.tensor_copy(selfT, bank[5][0:DEC, 192:192 + DEC * H]).then_inc(S["probs_placed"], 1)
            dve.wait_ge(S["pv_s"], 1)
            for j in range(2):
                dve.scalar_tensor_tensor(head_out[0:96, j * CW:(j + 1) * CW].rearrange("p (a b) -> p a b", a=6),
                                         bank[6 + j][0:96, 0:CW].rearrange("p (a b) -> p a b", a=6), rden_s[0:96, :],
                                         bc(sm("head")[0:96, 6 * j:6 * j + 6], 2, DH, [96, 6, DH]), ALU.mult, ALU.mult)\
                    .then_inc(S["head_done"], 1)
            dve.wait_ge(S["gathered_s"], 1)
            dve.tensor_copy(attn_s[0:DEC, 0:CW], bank[3][0:DEC, 0:CW])
            dve.tensor_copy(attn_s[0:DEC, CW:DA], bank[4][0:DEC, 0:CW]).then_inc(S["attn_s_done"], 1)

            units = [(qt, h) for qt in range(NT) for h in range(H)]
            NU = len(units)
            dve.wait_ge(S["conv_turned"], 1)
            dve.wait_ge(S["conv_out"], 48)
            dve.wait_ge(S["ssc_done"], 1)
            for s in range(NU + 2):
                if s < NU:
                    qt, h = units[s]
                    n = (qt + 1) * P
                    dve.wait_ge(S["s_done"], s + 1)
                    if s >= 2:
                        dve.wait_ge(S["p_turned"], s - 1)
                    dve.tensor_tensor_reduce(scores_sb[s % 2][:, 0:n], bank[s % 3][:, 0:n], logc[:, SEQ - n:SEQ], -1.0, 3.0e38,
                                             ALU.add, ALU.min, nmax[:, s % 4:s % 4 + 1]).then_inc(S["masked"], 1)
                if s >= 3 and s % 2 == 1:
                    u = s - 2
                    qt, h = units[u]
                    dve.wait_ge(S["o_done"], u + 1)
                    chain.step(dve.reciprocal(rden[(u // 2) % 2], den[:, (u - 1) % 24:(u - 1) % 24 + 2]))
                    tt(attn[:, qt, (h - 1) * DH:(h + 1) * DH].rearrange("p (a b) -> p a b", a=2),
                       bank[5 + (u // 2) % 2][:, 0:P].rearrange("p (a b) -> p a b", a=2),
                       bc(rden[(u // 2) % 2], 2, DH, [P, 2, DH]), ALU.mult).then_inc(S["o_evac"], 1)

            for g in range(2 * NT + 1):
                t = g // 2
                dve.wait_ge(S["a_turned"], g + 1)
                if t < NT:
                    k = 3 * (g % 2)
                    tt(attnT[:, k:k + 3, t * P:(t + 1) * P], bank[g % 2][:, 0:CW].rearrange("p (a b) -> p a b", a=3),
                       bc(gains[:, 16 + k:19 + k], 2, P, [P, 3, P]), ALU.mult).then_inc(S["a_evac"], 1)
                else:
                    tt(mixsT[:, 0:NP, 0:DEC], bank[g % 2][:, 0:NP * DEC].rearrange("p (a b) -> p a b", a=NP),
                       bc(gains[:, 16:16 + NP], 2, DEC, [P, NP, DEC]), ALU.mult).then_inc(S["a_evac"], 1)
            dve.wait_ge(S["a_std"], 1)
            dve.reciprocal(ra[:, 0:NT], stda[:, 0:NT])
            chain.step(dve.reciprocal(ra[0:DEC, NT:NT + 1], stda[0:DEC, NT:NT + 1]))
            dve.wait_ge(S["conv_std"], 1)

            def h_copy(t):
                n = TILES[t]
                for g in range(2):
                    dve.wait_ge(S["h_turned"], 2 * t + g + 1)
                    if t >= 2:
                        dve.wait_ge(S["r_done"], t - 1)
                    tt(hnT[t % 2][:, 4 * g:4 * g + 4, 0:n], bank[4 + g][:, :].rearrange("p (a b) -> p a b", a=4)[:, :, 0:n],
                       bc(gains[:, 8 + 4 * g:12 + 4 * g], 2, n, [P, 4, n]), ALU.mult).then_inc(S["h_evac"], 1)

            def r_copy(t):
                dve.wait_ge(S["r_done"], t + 1)
                dve.tensor_copy(logits[0:TILES[t], t, :], bank[6][0:TILES[t], 0:G + E]).then_inc(S["r_evac"], 1)

            for t in range(NT + 1):
                n = TILES[t]
                for g in range(4):
                    u = 4 * t + g
                    dve.wait_ge(S["op_done"], u + 1 + (2 if t == NT else 0))
                    cols = slice((g % 2) * 512, (g % 2 + 1) * 512)
                    r_ = (ra if g < 2 else rc)[0:n, t:t + 1]
                    if g == 2:
                        dve.wait_ge(S["op_evac"], u)
                    dve.scalar_tensor_tensor(x[0:n, t, cols], bank[u % 4][0:n, :], r_, x[0:n, t, cols], ALU.mult, ALU.add)\
                        .then_inc(S["op_evac"], 1)
                dve.wait_ge(S["op_evac"], 4 * t + 4)
                dve.engine_nop().then_inc(S["h_done"], 1)
                if t >= 1:
                    h_copy(t - 1)
                if t >= 2:
                    r_copy(t - 2)
                dve.wait_ge(S["h_std"], t + 1)
                chain.step(dve.reciprocal(rf[0:n, t:t + 1], stdf[0:n, t:t + 1]))
                if t >= 2:
                    dve.wait_ge(hn_sem[t % 2], 16 * (t // 2))
                dve.tensor_scalar(hn[t % 2][0:n, :], x[0:n, t, :], rf[0:n, t:t + 1], None, ALU.mult).then_inc(S["h_scaled"], 1)
            r_copy(NT - 1)
            h_copy(NT)
            r_copy(NT)
            dve.wait_ge(S["r_evac"], NT + 1)

            lg = logits[:, :, 0:G]
            le = logits[:, :, G:G + E].rearrange("p t (g e) -> p t g e", g=G)
            iota = sm("iota")
            step = chain.step

            def first_max(vals, m, c_, out, n):
                step(dve.tensor_reduce(m, vals, AX.X, ALU.max))
                step(tt(c_, vals, bc(m, 2, n, [P, T5, n]), ALU.is_equal))
                step(dve.scalar_tensor_tensor(c_, c_, -64.0, bc(iota[:, 0:n], 1, T5, [P, T5, n]), ALU.mult, ALU.add))
                step(dve.tensor_reduce(mn, c_, AX.X, ALU.min))
                step(tt(out, c_, bc(mn, 2, n, [P, T5, n]), ALU.is_equal))

            first_max(lg, gm, cg, ohg, G)
            step(tt(eg, lg, bc(gm, 2, G, [P, T5, G]), ALU.subtract))
            dve.engine_nop().then_inc(S["r_sub"], 1)
            step(tt(ohg, ohg, bc(sm("valid"), 2, G, [P, T5, G]), ALU.mult))
            t4 = tmp[:, 0, :, :].rearrange("p t (g e) -> p t g e", g=G)
            step(tt(t4, le, bc(ohg, 3, EG, [P, T5, G, EG]), ALU.mult))
            step(dve.tensor_reduce(leg, t4.rearrange("p t g e -> p t e g"), AX.X, ALU.add))
            first_max(leg, m1, cand, oh1, EG)
            step(dve.scalar_tensor_tensor(cand2, oh1, NEG, leg, ALU.mult, ALU.add))
            first_max(cand2, m2, cand, oh2, EG)
            step(tt(dd, m2, m1, ALU.subtract))
            dve.engine_nop().then_inc(S["r_sub2"], 1)
            for i, oh in enumerate((oh1, oh2)):
                last = tt(e12[:, i, :, :].rearrange("p t (g e) -> p t g e", g=G), bc(ohg, 3, EG, [P, T5, G, EG]),
                          bc(oh, 2, G, [P, T5, G, EG]), ALU.mult)
                step(last)
            tt(assigned.rearrange("p (t e) -> p t e", t=T5), e12[:, 0], e12[:, 1], ALU.add).then_inc(S["assign"], 1)
            dve.wait_ge(S["r_exp1"], 1)
            step(dve.tensor_reduce(gsum, eg, AX.X, ALU.add))
            step(dve.reciprocal(pg, gsum))
            dve.wait_ge(S["r_exp2"], 1)
            step(dve.tensor_scalar(dd, e2, 1.0, None, ALU.add))
            step(dve.reciprocal(dd, dd))
            step(tt(w12[:, 0, :], dd, pg, ALU.mult))
            step(tt(w12[:, 1, :], w12[:, 0, :], e2, ALU.mult))
            dve.wait_ge(S["count_done"], 1)
            step(dve.memset(posn[:, 0, :], 0.0))
            for t in range(NT):
                step(tt(posn[:, t + 1, :], posn[:, t, :], bank[7][:, t * E:(t + 1) * E], ALU.add))
            step(tt(total, posn[:, NT, :], bank[7][:, NT * E:(NT + 1) * E], ALU.add))
            step(tt(posn, posn, bank[6][:, 0:160].rearrange("p (t e) -> p t e", t=T5), ALU.add))
            for dst, src in ((pk, posn), (mr, None), (ov, None)):
                for i in range(2):
                    by = src if src is not None else bc(sm("mainrow" if dst is mr else "ovrow"), 1, T5, [P, T5, E])
                    last = tt(tmp[:, i], e12[:, i], by, ALU.mult)
                    step(last)
                step(dve.tensor_reduce(dst, tmp, AX.X, ALU.add))
            step(tt(ov, ov, pk, ALU.add))
            step(dve.scalar_tensor_tensor(mr, pk, float(PAIRS), mr, ALU.mult, ALU.add))
            step(tt(ov, ov, mr, ALU.subtract))
            step(dve.tensor_scalar(isov, pk, float(SL), None, ALU.is_ge))
            step(tt(ov, ov, isov, ALU.mult))
            step(tt(mr, mr, ov, ALU.add))
            dve.tensor_copy(addr[:, :, :], mr).then_inc(S["addr_done"], 1)
            step(dve.tensor_reduce(gm[:, 0:1], total, AX.X, ALU.max))
            dve.tensor_scalar(flag[:, :], gm[:, 0:1], float(SL), None, ALU.is_gt).then_inc(S["flag_ready"], 1)

            def tokens(i, s):
                dve.wait_ge(S["xg_turned"], i + 1)
                if not isinstance(i, int) or i > 0:
                    dve.wait_ge(S["gu_done"], i)
                for g in range(2):
                    last = tt(xgT[:, 4 * g:4 * g + 4, :], bank[g][:, :].rearrange("p (a b) -> p a b", a=4),
                              bc(gains[:, 8 + 4 * g:12 + 4 * g], 2, P, [P, 4, P]), ALU.mult)
                last.then_inc(S["xg_evac"], 1)

            def hidden(i, first):
                dve.wait_ge(S["silu_done"], i + 1)
                if not first:
                    dve.wait_ge(S["ht_done"], i)
                tt(hgu, hs, bank[2][:, F:2 * F], ALU.mult).then_inc(S["act_done"], 1)

            def result(i, s, turn):
                if turn is not None:
                    dve.wait_ge(res_sem[s], turn)
                dve.wait_ge(S["dn_done"], i + 1)
                dve.tensor_copy(yo[s][:, 512:D], bank[5][:, :]).then_inc(S["dn_evac_v"], 1)

            tokens(0, 0)
            for i in range(4):
                hidden(i, i == 0)
                tokens(i + 1, 0)
                result(i, i % 3, 16 * (i // 3) if i >= 3 else None)
            with dve.Fori(0, 3) as j:
                for n, s in enumerate((1, 2, 0)):
                    i = 3 * j + 4 + n
                    hidden(i, False)
                    tokens(i + 1, 0)
                    result(i, s, 16 * (j + 1) + (16 if s == 0 else 0))
            for i in range(13, 16):
                hidden(i, False)
                if i < 15:
                    tokens(i + 1, 0)
                result(i, i % 3, 16 * (i // 3))
            more = dve.value_load(flag[0:1, 0:1], min_val=0, max_val=1)
            with dve.If(more > 0):
                link = S["rope_ready"]
                at = [1 + QK_CHUNKS]

                def lstep(ins):
                    at[0] += 1
                    ins.then_inc(link, 1)
                    dve.wait_ge(link, at[0])

                big = cut(rt, 0, E, 8)
                lstep(tt(big[0:1], bc(total[0:1, :], 2, 8, [1, E, 8]), bc(sm("limits")[0:1, :], 1, E, [1, E, 8]), ALU.is_gt))
                lstep(dve.tensor_reduce(nb[0:1, :], big[0:1], AX.X, ALU.add))
                lstep(dve.tensor_copy(cum_a[0:1, :], nb[0:1, :]))
                a, b = cum_a, cum_b
                for sh in (1, 2, 4, 8, 16):
                    lstep(dve.tensor_copy(b[0:1, 0:sh], a[0:1, 0:sh]))
                    lstep(tt(b[0:1, sh:E], a[0:1, sh:E], a[0:1, 0:E - sh], ALU.add))
                    a, b = b, a
                for n in range(2 * OV_PAIRS):
                    lstep(dve.tensor_scalar(b[0:1, :], a[0:1, :], float(n), None, ALU.is_le))
                    lstep(dve.tensor_reduce(lst[0:1, n:n + 1], b[0:1, :], AX.X, ALU.add))
                    lstep(tt(b[0:1, :], b[0:1, :], nb[0:1, :], ALU.mult))
                    lstep(dve.tensor_reduce(lst2[0:1, n:n + 1], b[0:1, :], AX.X, ALU.add))
                    lstep(dve.tensor_scalar(lst2[0:1, n:n + 1], lst2[0:1, n:n + 1], -float(SL), OV_BASE + float(n * SL),
                                            ALU.mult, ALU.add))
                lstep(dve.scalar_tensor_tensor(lst2[0:1, :], lst[0:1, :], float(OV_ROWS), lst2[0:1, :], ALU.mult, ALU.add))
                lstep(dve.tensor_scalar(lst[0:1, :], lst[0:1, :], float(E - 1), None, ALU.min))
                lstep(dve.tensor_copy(ov_list[0:1, 0, :], lst[0:1, :]))
                dve.tensor_copy(ov_list[0:1, 1, :], lst2[0:1, :]).then_inc(S["list_done"], 1)
                with dve.Fori(0, OV_PAIRS // 3) as j:
                    for n, s in enumerate((1, 2, 0)):
                        i = 3 * j + 16 + n
                        tokens(i, 0)
                        hidden(i, False)
                        result(i, s, 16 * (j + 5) + (16 if s == 0 else 0))
                dve.nop()
            for t in range(NT + 1):
                n = TILES[t]
                dve.wait_ge(back_in[t], 16)
                for i in range(2):
                    if i == 1:
                        dve.wait_ge(S["x_scaled"], NT + 1 + t + 1)
                    dve.scalar_tensor_tensor(x[0:n, t, :], back[t][0:n, i, :], w12[0:n, i, t:t + 1], x[0:n, t, :],
                                             ALU.mult, ALU.add).then_inc(S["x_scaled" if i == 0 else "h_done"], 1)

        @block.gpsimd
        def _(pool):
            k = 0
            half = DH // 2
            for c in range(QK_CHUNKS + 1):
                todo = []
                for t in range(NT):
                    if c < QK_CHUNKS:
                        todo.append((c, t, P))
                    if t == 1 and c >= 1:
                        todo.append((c - 1, NT, DEC))
                for cc, t, w in todo:
                    pool.wait_ge(S["z_cos"], k + 1)
                    pool.wait_ge(S["rope_ready"], 1)
                    if w == P and unit(cc, t) >= 1 or w == DEC:
                        n_done = unit(cc, t) if w == P else 0
                        if w == P:
                            pool.wait_ge(S["rot_done"], n_done)
                        else:
                            pool.wait_ge(S["rot_done"], min(unit(cc + 1, 1) + 1, QK_CHUNKS * NT))
                    if w == P and t == 2 and cc >= 1:
                        pool.wait_ge(S["rope_ready"], 1 + cc)
                    zv = zn[0:w, :].rearrange("p (a b) -> p a b", a=6)
                    sv = zsin[0:w, :].rearrange("p (a b) -> p a b", a=6)
                    for a in range(2):
                        b = 1 - a
                        last = pool.tensor_tensor(sv[:, :, a * half:(a + 1) * half], zv[:, :, b * half:(b + 1) * half],
                                                  bc(rope_g[2 * (cc // 2) + 1][0:w, t, a * half:(a + 1) * half], 1, 6,
                                                     [w, 6, half]), ALU.mult)
                    last.then_inc(S["z_sin"], 1)
                    k += 1
                    if w == P and cc >= 2:
                        n = unit(cc, t)
                        pool.wait_ge(S["rot_done"], n + 1)
                        pool.dma_start(k_out[t][:, (cc - 2) * CW:(cc - 1) * CW], rot[n % 2]).then_inc(rot_out[n % 2], 16)
            pool.wait_ge(S["part_done"], QKV_CHUNKS)
            pool.memset(probs_s, 0.0).then_inc(S["zero_rows"], 1)

            for t in range(NT + 1):
                pool.wait_ge(S["h_scaled"], t + 1)
                pool.dma_start(hn_rows[t * P:t * P + TILES[t], :], hn[t % 2][0:TILES[t], :]).then_inc(hn_sem[t % 2], 16)
            pool.wait_ge(S["addr_done"], 1)
            pool.wait_ge(S["table_in"], 16)
            pool.wait_ge(S["wr_in"], 80)
            for i in range(2):
                for t in range(NT + 1):
                    n = TILES[t]
                    pool.indirect_dma_start(table, bass.IndirectOffsetOnAxis(addr[0:n, i, t:t + 1], 0),
                                            pay_sb[0:n, t, i, :], None, bounds_check=TABLE - 1, oob_is_err=False)\
                        .then_inc(S["scattered"], 16)
            pool.wait_ge(hn_sem[0], 48)
            pool.wait_ge(hn_sem[1], 32)
            pool.wait_ge(S["h_evac"], 2 * NT + 2)
            pool.wait_ge(S["r_done"], NT + 1)
            for s in range(WSLOTS):
                pool.memset(xg[s], 0.0).then_inc(S["pool_link"], 1)
            pool.wait_ge(S["pool_link"], WSLOTS)
            pool.wait_ge(S["scattered"], 160)
            pool.dma_start(tbl[:, :, :], table[0:E * SL].rearrange("(p i) w -> p i w", i=PAIRS)).then_inc(S["tbl_in"], 16)
            pool.wait_ge(S["tbl_in"], 16)

            def gather(i, s):
                pool.wait_ge(S["idx_ready"], i + 1)
                pool.sem_inc(S["gather_go"], 1)
                pool.indirect_dma_start(xg[s], None, hn_rows, bass.IndirectOffsetOnAxis(idx[:, s, 0:1], 0),
                                        bounds_check=TOK - 1, oob_is_err=False).then_inc(xg_sem[s], 16)

            def scatter(i, s):
                pool.wait_ge(S["dn_evac_a"], i + 1)
                pool.wait_ge(S["dn_evac_v"], i + 1)
                pool.sem_inc(S["scatter_go"], 1)
                pool.indirect_dma_start(results, bass.IndirectOffsetOnAxis(idx[:, s, 1:2], 0), yo[s], None,
                                        bounds_check=CHOICES - 1, oob_is_err=False).then_inc(res_sem[s], 16)

            for i in range(2):
                pool.tensor_copy(idx[:, i, :], tbl[:, i, :]).then_inc(S["idx_ready"], 1)
                gather(i, i)
            for i in range(3):
                if i + 2 == 2:
                    pool.tensor_copy(idx[:, 2, :], tbl[:, 2, :]).then_inc(S["idx_ready"], 1)
                    gather(2, 2)
                    scatter(0, 0)
                    continue
                s = (i + 2) % 3
                pool.wait_ge(res_sem[s], 16)
                pool.tensor_copy(idx[:, s, :], tbl[:, i + 2, :]).then_inc(S["idx_ready"], 1)
                gather(i + 2, s)
                scatter(i, i % 3)
            with pool.Fori(0, 3) as j:
                for n in range(3):
                    i = 3 * j + 3 + n
                    s = (n + 2) % 3
                    pool.wait_ge(res_sem[s], 16 * (j + 1) + (16 if n >= 1 else 0))
                    pool.tensor_copy(idx[:, s, :], tbl[:, ds(i + 2, 1), :].rearrange("p i w -> p (i w)")).then_inc(S["idx_ready"], 1)
                    gather(i + 2, s)
                    scatter(i, n)
            for i in range(12, 16):
                if i + 2 < 16:
                    s = (i + 2) % 3
                    pool.wait_ge(res_sem[s], 16 * ((i + 2) // 3))
                    pool.tensor_copy(idx[:, s, :], tbl[:, i + 2, :]).then_inc(S["idx_ready"], 1)
                    gather(i + 2, s)
                scatter(i, i % 3)
            pool.wait_ge(res_sem[0], 96)
            pool.wait_ge(res_sem[1], 80)
            pool.wait_ge(res_sem[2], 80)
            pool.wait_ge(S["flag_ready"], 1)
            more = pool.value_load(flag[0:1, 0:1], min_val=0, max_val=1)
            with pool.If(more > 0):
                pool.wait_ge(S["list_done"], 1)
                with pool.Fori(0, OV_PAIRS // 3) as j:
                    for n, s in enumerate((1, 2, 0)):
                        i = 3 * j + 16 + n
                        k2 = 2 * (3 * j + n)
                        for h in range(2):
                            row = pool.value_load(ov_list[0:1, 1, ds(k2 + h, 1)], min_val=0, max_val=TABLE - SL)
                            pool.dma_start(idx[h * SL:(h + 1) * SL, s, :], table[ds(row, SL), :]).then_inc(S["ov_in"], 16)
                        pool.wait_ge(S["ov_in"], 32 * (3 * j + n + 1))
                        pool.sem_inc(S["idx_ready"], 1)
                        gather(i, s)
                        scatter(i, s)
                        pool.wait_ge(res_sem[s], 16 * (j + 6) + (16 if s == 0 else 0))
                        pool.sem_inc(S["ov_done"], 1)
                pool.nop()
            pool.engine_nop().then_inc(S["y_ready"], 1)


_INS = ["x_prompt", "x_sample", "cache_k", "cache_v", "state_conv", "g_norm_mix", "w_in", "g_q", "g_k", "w_conv",
        "g_attn_out", "g_conv_out", "w_out", "g_norm_ffn", "w_router_group", "w_router_expert", "w_gate", "w_up", "w_down"]
_OUTS = [(1, SEQ, D), (DEC, 1, D), (1, 1, SEQ, H, DH), (1, 1, SEQ, H, DH), (1, 1, 2, DC), (1, DEC, 1, H, DH),
         (1, DEC, 1, H, DH), (1, DEC, 2, DC)]


def kernel(**inputs):
    import concourse.bacc as _bacc
    from concourse.bass_utils import run_bass_kernel_spmd as _run

    nc = _bacc.Bacc("TRN2", target_bir_lowering=False, num_devices=1)
    arrays, args = {}, []
    given = [(n, inputs[n]) for n in _INS] + [("const", constants()[0]), ("pay", payload()), ("empty", empty_table())]
    for name, a in given:
        a = np.ascontiguousarray(a)
        arrays[f"in_{name}_dram"] = a
        args.append(nc.dram_tensor(f"in_{name}_dram", a.shape, mybir.dt.from_np(a.dtype), kind="ExternalInput").ap())
    for i, shape in enumerate(_OUTS):
        args.append(nc.dram_tensor(f"out_{i}_dram", shape, F32, kind="ExternalOutput").ap())
    build(nc, *args)
    r = _run(nc, [arrays], core_ids=[0])
    return tuple(r.results[0][f"out_{i}_dram"] for i in range(len(_OUTS)))
```

```python
from contextlib import ExitStack

import numpy as np

import concourse.bass as bass
from concourse import mybir
from concourse.alu_op_type import AluOpType as ALU

F32 = mybir.dt.float32
U32 = mybir.dt.uint32
I32 = mybir.dt.int32
ACT = mybir.ActivationFunctionType
AX = mybir.AxisListType

P = 128
SEQ, DEC, D = 512, 8, 1024
NT = SEQ // P
TILES = [P] * NT + [DEC]
KD = D // P
H, DH = 12, 64
DA, DC = H * DH, 256
NP = H // 2
EPS = 1e-6
G, EG, E, F = 4, 8, 32, 256
WBUF = 1024
CW = 384
QK_CHUNKS, QKV_CHUNKS, CHUNKS = 4, 6, 8
WRING = 3
SL = 64
PAIRS = E // 2
WSLOTS = 3
OV_PAIRS = 9
TOK = SEQ + DEC
CHOICES = 2 * TOK
OV_ROWS = 512
OV_BASE = E * SL
TABLE = OV_BASE + E * OV_ROWS + 2 * OV_PAIRS * SL
EMPTY = 1 << 14
NEG = -1.0e30


def ds(i, n):
    return bass.ds(i, n)


def constants():
    f = np.float32
    seg = {}
    p = np.arange(P)
    seg["ident"] = np.eye(P)
    seg["tri"] = (p[:, None] < p[None, :])
    seg["ones"] = np.ones((P, P))
    d = p[:, None] + 3 * P - np.arange(SEQ)[None, :]
    c = ((d >= 0) & (d <= 128)).astype(int) + ((d >= 0) & (d % 4 == 0) & (d <= 512)) + ((d >= 0) & (d % 16 == 0))
    seg["logc"] = np.where(c > 0, np.log(np.maximum(c, 1)), NEG)
    half = DH // 2
    inv = (f(10000.0) ** (-np.arange(half, dtype=f) / f(half))).astype(f)
    pos = np.concatenate([np.arange(SEQ).reshape(NT, P).T, np.full((P, 1), WBUF)], 1).astype(f)
    ang = (pos[:, :, None] * inv[None, None, :]).astype(f)
    cos, sin = np.cos(ang), np.sin(ang)
    seg["cos"] = np.concatenate([cos, cos], 2).reshape(P, -1)
    seg["sin"] = np.concatenate([-sin, sin], 2).reshape(P, -1)
    rows = np.concatenate([896 + p, 512 + 4 * np.arange(96), 16 * np.arange(32)])
    d = np.concatenate([WBUF - rows, [0]])
    c = (d <= 128).astype(int) + ((d % 4 == 0) & (d <= 512)) + (d % 16 == 0)
    seg["slogc"] = np.tile(np.log(c)[None], (P, 1))
    q = np.arange(P)
    seg["head"] = (q[:, None] % H == np.arange(H)[None]) & (q[:, None] < DEC * H)
    seg["sample"] = (q[:, None] // H == np.arange(DEC)[None])
    seg["sampleT"] = (np.arange(DEC * H)[None] // H == q[:, None])
    seg["quad"] = (q[:, None] % 32 == np.arange(DEC)[None])
    seg["quada"] = seg["quad"] & (q[:, None] < 96)
    seg["quadc"] = seg["quad"] & (q[:, None] >= 96)
    seg["valid"] = (np.arange(NT + 1)[None] < NT) | (q[:, None] < DEC)
    seg["iota"] = np.tile(np.arange(EG)[None], (P, 1))
    e = np.arange(E)
    seg["mainrow"] = np.tile(((e % 2) * SL * PAIRS + e // 2)[None], (P, 1))
    seg["ovrow"] = np.tile((OV_BASE + e * OV_ROWS - SL)[None], (P, 1))
    seg["limits"] = np.tile((SL * (1 + np.arange(8)))[None], (P, 1))
    at, n = {}, 0
    for k, v in seg.items():
        at[k] = (n, v.shape[1])
        n += v.shape[1]
    return np.concatenate([v.astype(f) for v in seg.values()], 1), at


def payload():
    t = np.minimum(np.arange(NT + 1)[None, :] * P + np.arange(P)[:, None], TOK - 1)
    pay = np.zeros((P, NT + 1, 2, 2), np.uint32)
    pay[..., 0] = t[:, :, None]
    pay[..., 1] = 2 * t[:, :, None] + np.arange(2)
    return pay.reshape(P, -1)


def empty_table():
    return np.full((P, TABLE // P * 2), EMPTY, np.uint32)


AT = constants()[1]


def build(nc, x_prompt, x_sample, cache_k, cache_v, state_conv, g_norm_mix, w_in, g_q, g_k, w_conv, g_attn_out,
          g_conv_out, w_out, g_norm_ffn, w_router_group, w_router_expert, w_gate, w_up, w_down, const, pay, empty,
          y_prompt, y_sample, k_prompt, v_prompt, conv_prompt, k_sample, v_sample, conv_sample):
    ctx = ExitStack()
    with ctx:
        def sb(name, shape, dt=F32):
            return ctx.enter_context(nc.sbuf_tensor(name, shape, dt))

        def sem(name):
            return ctx.enter_context(nc.semaphore(name))

        hn_rows = nc.dram_tensor("hn_rows", [TOK, D], F32, kind="Internal").ap()
        results = nc.dram_tensor("results", [CHOICES, D], F32, kind="Internal").ap()
        table = nc.dram_tensor("table", [TABLE, 2], U32, kind="Internal").ap()

        bank = [ctx.enter_context(nc.psum_tensor(f"bank{i}", [P, 512], F32)) for i in range(8)]

        SLOT = 12288
        ring = sb("ring", [P, WSLOTS * SLOT])
        work = sb("work", [P, 8192])
        x = sb("x", [P, NT + 1, D])
        rt = sb("rt", [P, 1600])

        def cut(t, off, *dims):
            n = int(np.prod(dims))
            v = t[:, off:off + n]
            if len(dims) == 2:
                return v.rearrange("p (a b) -> p a b", a=dims[0])
            if len(dims) == 3:
                return v.rearrange("p (a b c) -> p a b c", a=dims[0], b=dims[1])
            if len(dims) == 4:
                return v.rearrange("p (a b c d) -> p a b c d", a=dims[0], b=dims[1], c=dims[2])
            return v

        wchunk = [cut(ring, i * 3072, KD, CW) for i in range(WRING)]
        rope_g = [cut(ring, 9216 + i * 320, NT + 1, DH) for i in range(4)]
        zsq = cut(ring, 10496, CW)
        zn = cut(ring, 10880, CW)
        zcos = cut(ring, 11264, CW)
        zsin = cut(ring, 11648, CW)
        probs_s = cut(ring, 10496, 2, DEC, DEC * H)
        attn_s = cut(ring, 9216, DA)
        scores_sb = [[cut(ring, 6160 + (2 * i + h) * 512, 512) for h in range(2)] for i in range(2)]
        probs_t = [[cut(ring, 3072 + (2 * i + h) * 512, 512) for h in range(2)] for i in range(2)]
        ysq = cut(ring, 5120, 2, TOK)
        attn = cut(ring, 0, NT, DA)
        qT = cut(ring, SLOT, NP, SEQ)
        kT = cut(ring, SLOT + 3072, NP, SEQ)
        v_rows = cut(ring, SLOT + 6144, NT, DA)
        xn = cut(ring, SLOT + 6144, NT + 1, D)
        junk_x = cut(ring, SLOT + 11264, D)
        cuT = cut(ring, SLOT + 10256, 2, 2 + SEQ)
        cu_s = cut(ring, SLOT + 11284, 2, 3, DEC)
        conv_rows = cut(ring, SLOT + 11400, 512)
        wout = cut(ring, 2 * SLOT, KD, D)
        xT = cut(ring, 2 * SLOT + 8192, KD, SEQ)
        attnT = cut(ring, 2 * SLOT + 8192, NP, SEQ)
        partial = cut(work, 6656, CW)

        kv = [cut(work, i * 1536, 2, DA) for i in range(2)]
        qs, ks, vs = (cut(work, 3072 + i * DA, DA) for i in range(3))
        rot = [cut(work, 5376 + i * CW, CW) for i in range(2)]
        head_out = cut(work, 5376, DA)
        xsT = cut(work, 6144, KD, 32)
        mixsT = cut(work, 6400, KD, 32)
        yT = cut(work, 7152, 2, TOK)
        cos = cut(work, 7152, NT + 1, DH)
        sin = cut(work, 7472, NT + 1, DH)
        hn = [cut(work, i * D, D) for i in range(2)]
        hnT = [cut(work, 2048 + i * D, KD, P) for i in range(2)]
        junk = cut(work, 4096, D)
        partial_o = cut(work, 5120, D)

        gate_up = [[cut(ring, s * SLOT + h * 4096, KD, 2 * F) for h in range(2)] for s in range(WSLOTS)]
        down = [[cut(ring, s * SLOT + 8192 + h * 2048, 2, D) for h in range(2)] for s in range(WSLOTS)]
        xg = [cut(work, s * D, D) for s in range(WSLOTS)]
        xgT = cut(work, 3072, KD, P)
        yo = [cut(work, 4096 + s * D, D) for s in range(WSLOTS)]
        hs = cut(work, 7168, F)
        hgu = cut(work, 7424, F)
        hT = cut(work, 7680, 2, P)
        back = [cut(ring, i * 2048, 2, D) for i in range(NT + 1)]

        ident = sb("ident", [P, P])
        tri = sb("tri", [P, P])
        ones = sb("ones", [P, P])
        NSMALL = AT["limits"][0] + 8 - AT["head"][0]
        small = sb("small", [P, NSMALL])
        logc = cut(rt, 0, SEQ)
        slogc = cut(rt, 512, 257)
        raw_s, neg_s, prob_s = (cut(rt, 769 + i * 257, 257) for i in range(3))

        def sm(name):
            o, n = AT[name]
            o -= AT["head"][0]
            return small[:, o:o + n]

        gains = sb("gains", [P, 32])
        gain_rows = cut(rt, 1540, 60)
        gain_in = cut(work, 3072, P)
        gqk = cut(work, 3200, 2, DH)
        state_in = cut(rt, 1026, DC)
        wr = sb("wr", [P, KD, G + E])
        logits = sb("logits", [P, NT + 1, G + E])
        st = sb("st", [P, 184])
        pay_sb = sb("pay_sb", [P, NT + 1, 2, 2], U32)
        idx_g = pay_sb[:, 0:2, :, :].rearrange("p t k w -> p (t k w)")[:, 0:WSLOTS]
        tbl = sb("tbl", [P, PAIRS, 2], U32)
        idx = sb("idx", [P, WSLOTS, 2], U32)
        addr = sb("addr", [P, 2, NT + 1], U32)
        flag = sb("flag", [P, 1], I32)
        ov_list = sb("ov_list", [1, 2, 2 * OV_PAIRS], I32)

        ssx, stdx, rx = st[:, 0:5], st[:, 5:10], st[:, 10:15]
        zss, zstd, zr = st[:, 15:21], st[:, 21:27], st[:, 27:33]
        den = st[:, 160:184]
        rden = [st[:, 140 + 2 * i:142 + 2 * i] for i in range(2)]
        nmax = st[:, 47:51]
        ssa, ra = st[:, 51:56], st[:, 56:61]
        ssc, rc = st[:, 61:66], st[:, 66:71]
        stda = st[:, 71:76]
        sself = st[:, 76:88]
        smask = st[:, 88:100]
        nm_s, den_s, rden_s = st[:, 100:101], st[:, 101:102], st[:, 102:103]
        self8 = st[:, 103:111]
        ssf, stdf, rf = st[:, 111:116], st[:, 116:121], st[:, 121:126]
        eps = st[:, 126:127]
        selfT = raw_s[0:DEC, 0:DEC * H]
        sc = cut(rt, 1283, 2, DEC * H)
        w12 = st[:, 130:140].rearrange("p (k t) -> p k t", k=2)

        names = """const_in x_in xs_in gains_in misc_in table_in wr_in wout_in logc_in
            x_squared x_std x_scaled x_turned x_evac gains_turned gains_evac rope_ready pads_zero
            z_done z_squared z_ssq z_std z_copied z_cos z_sin rot_done rot_turned rot_evac v_evac rows_out
            part_done part_evac comb_done comb_read blk_done blk_evac_a blk_evac_v cu_ready conv_done y_squared y_gained ssc_done
            ssc_std conv_std state_turned conv_turned conv_evac conv_out
            qb_done qb_used scores_s turned_s self_spread soft_in soft_done probs_turned probs_placed v_used pv_s head_done
            gathered_s attn_s_done
            s_done masked exp_done p_turned p_evac_a p_evac_v o_done o_evac
            a_squared a_std a_r a_turned a_evac op_done op_evac opp_evac h_done
            h_squared h_std h_scaled h_turned h_evac r_done r_evac hn_out_sem
            r_exp1 r_sub r_sub2 r_exp2 assign count_done addr_done list_done scattered tbl_in idx_ready idx_g_ready ov_in
            xg_in xg_turned xg_evac gu_done silu_done act_done ht_done ht_evac dn_done dn_evac_a dn_evac_v res_out
            y_ready y_out ov_done gather_go scatter_go dve_link act_link pool_link flag_ready zero_rows""".split()
        S = {n: sem(n) for n in names}
        w_in_s = [sem(f"w_loaded{i}") for i in range(WRING)]
        kv_in = [sem(f"kv_loaded{i}") for i in range(2)]
        gu_in = [sem(f"gate_up_loaded{i}") for i in range(WSLOTS)]
        dn_in = [sem(f"down_loaded{i}") for i in range(WSLOTS)]
        xg_sem = [sem(f"xg_in{i}") for i in range(WSLOTS)]
        res_sem = [sem(f"res_out{i}") for i in range(WSLOTS)]
        hn_sem = [sem(f"hn_out{i}") for i in range(2)]
        rot_out = [sem(f"rot_out{i}") for i in range(2)]
        back_in = [sem(f"back_in{i}") for i in range(NT + 1)]
        x_in = [sem(f"x_in{i}") for i in range(NT + 1)]

        w_in_v = w_in[0].rearrange("(k p) n -> p k n", p=P)
        w_out_v = w_out[0].rearrange("(k p) n -> p k n", p=P)
        x_rows = x_prompt[0].rearrange("(t p) d -> t p d", p=P)
        xs_rows = x_sample.rearrange("b t d -> (b t) d")
        k_out = k_prompt[0, 0].rearrange("(t p) h d -> t p (h d)", p=P)
        v_out = v_prompt[0, 0].rearrange("(t p) h d -> p t (h d)", p=P)
        y_rows = y_prompt[0].rearrange("(t p) d -> t p d", p=P)
        ys_rows = y_sample.rearrange("b t d -> (b t) d")
        ck = cache_k[0].rearrange("b r h d -> b r (h d)")
        cv = cache_v[0].rearrange("b r h d -> b r (h d)")

        def bc(ap, axis, n, shape):
            return ap.unsqueeze(axis).to_broadcast(shape)

        class Chain:
            def __init__(self, eng, s):
                self.eng, self.s, self.n = eng, s, 0

            def step(self, ins):
                self.n += 1
                ins.then_inc(self.s, 1)
                self.eng.wait_ge(self.s, self.n)

        BLOCKS = [2, 4, 3, 5, 0, 1]
        pair_units = [(qt, hp) for qt in reversed(range(NT)) for hp in range(NP)]
        NU = len(pair_units)
        score_bank = [[bank[0], bank[4]], [bank[1], bank[2]]]
        turn_bank = [bank[3], bank[5]]

        block = ctx.enter_context(nc.Block())
        def unit(c, t):
            return c * NT + t

        def state_cols(h):
            return state_in[0:16, h * P:(h + 1) * P]

        def r(off, *dims):
            return cut(rt, off, *dims)

        T5 = NT + 1
        assigned = r(0, 160)
        e12 = r(160, 2, T5, E)
        tmp = r(480, 2, T5, E)
        posn = r(800, T5, E)
        total = r(960, E)
        leg, cand, cand2 = r(992, T5, EG), r(1032, T5, EG), r(1072, T5, EG)
        oh1, oh2 = r(1112, T5, EG), r(1152, T5, EG)
        ohg, cg, eg = r(1192, T5, G), r(1212, T5, G), r(1232, T5, G)
        gm, gsum, pg, m1, m2, dd, e2, mn = (r(1252 + 5 * i, T5) for i in range(8))
        pk, mr, ov, isov = (r(1292 + 10 * i, 2, T5) for i in range(4))
        nb, cum_a, cum_b = r(1332, E), r(1364, E), r(1396, E)
        lst, lst2 = r(1428, 2 * OV_PAIRS), r(1446, 2 * OV_PAIRS)

        @block.sync
        def _(sp):
            def cseg(name, dst):
                o, n = AT[name]
                return sp.dma_start(dst, const[:, o:o + n])

            for t in range(NT):
                sp.dma_start(x[:, t, :], x_rows[t]).then_inc(x_in[t], 16)
                if t == 0:
                    cseg("ident", ident[:, :]).then_inc(S["const_in"], 16)
                    for r, (g, n) in enumerate(((g_norm_mix, 8), (g_norm_ffn, 8), (g_attn_out, 6), (g_conv_out, 2))):
                        r0 = (0, 8, 16, 22)[r]
                        sp.dma_start(gain_in[r0:r0 + n, :], g[0].rearrange("(k p) -> k p", p=P)).then_inc(S["gains_in"], 16)
                    sp.dma_start(gain_in[24:30, :], w_conv[0].rearrange("j (k p) -> (j k) p", p=P)).then_inc(S["gains_in"], 16)
            sp.dma_start(x[0:DEC, NT, :], xs_rows).then_inc(x_in[NT], 16)
            for c in range(WRING):
                sp.dma_start(wchunk[c], w_in_v[:, :, c * CW:(c + 1) * CW]).then_inc(w_in_s[c], 16)
            cseg("cos", cos.rearrange("p a b -> p (a b)")).then_inc(S["misc_in"], 16)
            cseg("sin", sin.rearrange("p a b -> p (a b)")).then_inc(S["misc_in"], 16)
            sp.dma_start(gqk[:, 0, :], g_q[0].partition_broadcast(P)).then_inc(S["misc_in"], 16)
            sp.dma_start(gqk[:, 1, :], g_k[0].partition_broadcast(P)).then_inc(S["misc_in"], 16)
            sp.dma_start(state_in[0:2 * DEC, :], state_conv[0].rearrange("b j c -> (b j) c")).then_inc(S["misc_in"], 16)
            sp.dma_start(small[:, :], const[:, AT["head"][0]:AT["head"][0] + NSMALL]).then_inc(S["misc_in"], 16)
            cseg("logc", logc).then_inc(S["logc_in"], 16)
            cseg("slogc", slogc).then_inc(S["logc_in"], 16)
            cseg("tri", tri[:, :]).then_inc(S["wr_in"], 16)
            cseg("ones", ones[:, :]).then_inc(S["wr_in"], 16)
            sp.dma_start(wr[:, :, 0:G], w_router_group[0].rearrange("(k p) n -> p k n", p=P)).then_inc(S["wr_in"], 16)
            sp.dma_start(wr[:, :, G:G + E], w_router_expert[0].rearrange("(k p) n -> p k n", p=P)).then_inc(S["wr_in"], 16)
            sp.dma_start(pay_sb[:, :, :, :].rearrange("p t k w -> p (t k w)"), pay).then_inc(S["wr_in"], 16)
            sp.dma_start(table.rearrange("(p n) w -> p (n w)", p=P), empty).then_inc(S["table_in"], 16)
            sp.dma_start(conv_sample[0, :, 0, :], state_conv[0, :, 1, :]).then_inc(S["conv_out"], 16)

            def cached(b, src, s):
                sp.dma_start(kv[b % 2][:, 0, :], src[b, WBUF - P:WBUF, :]).then_inc(s, 16)
                sp.dma_start(kv[b % 2][0:96, 1, :], src[b, 512:896:4, :]).then_inc(s, 16)
                sp.dma_start(kv[b % 2][96:128, 1, :], src[b, 0:512:16, :]).then_inc(s, 16)

            def wload(c):
                if c - WRING < QKV_CHUNKS:
                    sp.wait_ge(S["part_done"], c - WRING + 1)
                sp.dma_start(wchunk[c % WRING], w_in_v[:, :, c * CW:(c + 1) * CW]).then_inc(w_in_s[c % WRING], 16)

            def keys(b):
                if b >= 2:
                    sp.wait_ge(S["scores_s"], b - 1)
                cached(b, ck, kv_in[b % 2])

            def values(b):
                if b < 2:
                    sp.wait_ge(S["scores_s"], DEC - 1 + b)
                else:
                    sp.wait_ge(S["v_used"], b - 1)
                cached(b, cv, kv_in[b % 2])

            keys(0)
            keys(1)
            wload(3)
            wload(4)
            sp.dma_start(wout, w_out_v).then_inc(S["wout_in"], 16)
            wload(5)
            keys(2)
            keys(3)
            wload(6)
            for b in range(4, DEC):
                keys(b)
            values(0)
            wload(7)
            for b in range(1, 4):
                values(b)
            sp.wait_ge(S["v_evac"], 2 * NT)
            sp.dma_start(v_out, v_rows).then_inc(S["rows_out"], 16)
            sp.wait_ge(S["comb_read"], QKV_CHUNKS)
            sp.dma_start(k_sample[0].rearrange("b t h d -> (b t) (h d)"), ks[0:DEC, :]).then_inc(S["rows_out"], 16)
            sp.dma_start(v_sample[0].rearrange("b t h d -> (b t) (h d)"), vs[0:DEC, :]).then_inc(S["rows_out"], 16)
            for b in range(4, DEC):
                values(b)
            sp.wait_ge(S["conv_evac"], 1)
            sp.dma_start(conv_prompt[0, 0], conv_rows[0:2, 0:DC]).then_inc(S["conv_out"], 16)
            sp.dma_start(conv_sample[0, :, 1, :], conv_rows[0:DEC, DC:2 * DC]).then_inc(S["conv_out"], 16)

            def gates(experts, s):
                for h, e in enumerate(experts):
                    for w, o in ((w_gate, 0), (w_up, F)):
                        sp.dma_start(gate_up[s][h][:, :, o:o + F],
                                     w[0, ds(e, 1)].rearrange("e (k p) f -> p (e k) f", p=P)).then_inc(gu_in[s], 16)

            def downs(experts, s):
                for h, e in enumerate(experts):
                    sp.dma_start(down[s][h], w_down[0, ds(e, 1)].rearrange("e (k p) n -> p (e k) n", p=P)).then_inc(dn_in[s], 16)

            def expert(a, b, s, i=None):
                if i is not None:
                    sp.wait_ge(S["gu_done"], i - 2)
                gates((a, b), s)
                if i is not None:
                    sp.wait_ge(S["dn_done"], i - 2)
                downs((a, b), s)

            sp.wait_ge(S["a_turned"], 2 * NT + 1)
            sp.wait_ge(S["a_squared"], NT + 1)
            sp.wait_ge(S["rows_out"], 48)
            sp.wait_ge(S["conv_out"], 48)
            expert(0, 1, 0)
            expert(2, 3, 1)
            sp.wait_ge(S["op_done"], 4 * NT + 2)
            expert(4, 5, 2)
            with sp.Fori(0, 4) as j:
                for s in range(WSLOTS):
                    i = 3 * j + 3 + s
                    expert(2 * i, 2 * i + 1, s, i)
            expert(30, 31, 0, PAIRS - 1)
            sp.wait_ge(S["flag_ready"], 1)
            more = sp.value_load(flag[0:1, 0:1], min_val=0, max_val=1)
            with sp.If(more > 0):
                sp.wait_ge(S["list_done"], 1)
                with sp.Fori(0, OV_PAIRS // 3) as j:
                    for n, s in enumerate((1, 2, 0)):
                        i = 3 * j + 16 + n
                        k = 2 * (3 * j + n)
                        ea = sp.value_load(ov_list[0:1, 0, ds(k, 1)], min_val=0, max_val=E - 1)
                        eb = sp.value_load(ov_list[0:1, 0, ds(k + 1, 1)], min_val=0, max_val=E - 1)
                        expert(ea, eb, s, i)
                sp.nop()
            sp.wait_ge(S["y_ready"], 1)
            res_pairs = results.rearrange("(t k) d -> t k d", k=2)
            for t in range(NT + 1):
                n = TILES[t]
                sp.dma_start(back[t][0:n], res_pairs[t * P:t * P + n]).then_inc(back_in[t], 16)
            for t in range(NT + 1):
                sp.wait_ge(S["h_done"], NT + 1 + t + 1)
                sp.dma_start(y_rows[t] if t < NT else ys_rows, x[0:TILES[t], t, :]).then_inc(S["y_out"], 16)
            sp.wait_ge(S["y_out"], 16 * (NT + 1))
            sp.wait_ge(S["rows_out"], 48)
            sp.wait_ge(S["conv_out"], 48)
            sp.wait_ge(rot_out[0], 16 * NT)
            sp.wait_ge(rot_out[1], 16 * NT)

        @block.tensor
        def _(pe):
            pe.wait_ge(S["const_in"], 16)
            pe.wait_ge(S["gains_in"], 80)
            pe.transpose(bank[7][:, 0:30], gain_in[0:30, :], ident[0:30, 0:30]).then_inc(S["gains_turned"], 1)
            for g in range(2 * NT + 1):
                t = g // 2
                pe.wait_ge(S["x_scaled"], t + 1)
                if g >= 3:
                    pe.wait_ge(S["x_evac"], g - 2)
                if t < NT:
                    for k in range(4):
                        o = (4 * (g % 2) + k) * P
                        last = pe.transpose(bank[g % 3][:, k * P:(k + 1) * P], xn[:, t, o:o + P], ident[:, :])
                else:
                    for k in range(KD):
                        last = pe.transpose(bank[g % 3][:, k * DEC:(k + 1) * DEC], xn[0:DEC, t, k * P:(k + 1) * P],
                                            ident[0:DEC, 0:DEC])
                last.then_inc(S["x_turned"], 1)
            pe.wait_ge(S["x_evac"], 2 * NT + 1)
            pe.wait_ge(S["pads_zero"], 1)

            def turn_rot(c, t):
                n = unit(c, t)
                pe.wait_ge(S["rot_done"], n + 1)
                if n >= 1:
                    pe.wait_ge(S["rot_evac"], n)
                for j in range(3):
                    last = pe.transpose(bank[5][:, j * P:(j + 1) * P], rot[n % 2][:, j * P:(j + 1) * P], ident[:, :])
                last.then_inc(S["rot_turned"], 1)

            def combine(c):
                pe.wait_ge(S["part_evac"], c + 1)
                if c >= 1:
                    pe.wait_ge(S["comb_read"], c)
                else:
                    pe.wait_ge(S["cu_ready"], 2)
                pe.matmul(bank[4][0:DEC, 0:CW], sm("quad"), partial, start=True, stop=True).then_inc(S["comb_done"], 1)

            def spread_q(b):
                if b >= 1:
                    pe.wait_ge(S["qb_used"], b)
                else:
                    pe.wait_ge(S["rope_ready"], 3)
                for j in range(2):
                    last = pe.matmul(bank[6 + j][:, 0:CW], ident[0:DEC, b:b + 1].to_broadcast([DEC, P]),
                                     qs[0:DEC, j * CW:(j + 1) * CW], start=True, stop=True)
                last.then_inc(S["qb_done"], 1)

            def turn_state():
                pe.wait_ge(S["misc_in"], 96)
                for h in range(2):
                    last = pe.transpose(bank[4][:, h * 16:h * 16 + 16], state_cols(h), ident[0:16, 0:16])
                last.then_inc(S["state_turned"], 1)

            def turn_scores():
                pe.wait_ge(S["scores_s"], DEC + 1)
                pe.wait_ge(S["qb_used"], DEC)
                for i in range(2):
                    last = pe.transpose(bank[6][0:DEC * H, i * P:(i + 1) * P], sc[:, i, :], ident[:, :])
                last.then_inc(S["turned_s"], 1)
                pe.matmul(bank[7][0:DEC * H, 0:H], sm("sampleT")[0:DEC, :], sself[0:DEC, :], start=True, stop=True)\
                    .then_inc(S["self_spread"], 1)

            def turn_probs():
                pe.wait_ge(S["soft_done"], 2)
                pe.wait_ge(S["rot_evac"], QK_CHUNKS * NT)
                for i in range(2):
                    pe.transpose(bank[5][:, i * 96:(i + 1) * 96], prob_s[0:DEC * H, i * P:(i + 1) * P],
                                 ident[0:DEC * H, 0:DEC * H])
                pe.transpose(bank[5][0:DEC, 192:192 + DEC * H], self8[0:DEC * H, :], ident[0:DEC * H, 0:DEC * H])\
                    .then_inc(S["probs_turned"], 1)

            def sample_values(b):
                if b == 0:
                    pe.wait_ge(S["probs_placed"], 1)
                pe.wait_ge(kv_in[b % 2], 48 * (DEC // 2 + b // 2 + 1))
                for i in range(2):
                    for j in range(2):
                        last = pe.matmul(bank[6 + j][0:DEC * H, 0:CW], probs_s[:, i, b, :], kv[b % 2][:, i, j * CW:(j + 1) * CW],
                                         start=(b == 0 and i == 0), stop=False)
                last.then_inc(S["v_used"], 1)

            spread_at = {(2, 3): 0, (3, 1): 1, (3, 3): 2, (4, 0): 3, (4, 1): 4, (4, 2): 5, (4, 3): 6, (5, 0): 7}
            pend = []
            for c in range(QKV_CHUNKS):
                pe.wait_ge(w_in_s[c % WRING], 16 * (c // WRING + 1))
                w = wchunk[c % WRING]
                for t in range(NT):
                    n = unit(c, t)
                    if 3 <= n < QK_CHUNKS * NT + 3:
                        pe.wait_ge(S["z_copied"], n - 2 if n - 3 < QK_CHUNKS * NT else 0)
                    elif n >= 3:
                        pe.wait_ge(S["v_evac"], n - 2 - QK_CHUNKS * NT)
                    for k in range(KD):
                        last = pe.matmul(bank[n % 3][:, 0:CW], xT[:, k, t * P:(t + 1) * P], w[:, k, :],
                                         start=(k == 0), stop=(k == KD - 1))
                    last.then_inc(S["z_done"], 1)
                    if (c, t) == (1, 0):
                        turn_state()
                    if t == 1 and c >= 1:
                        combine(c - 1)
                    if c < QK_CHUNKS:
                        pend.append((c, t))
                    if len(pend) > 2 or (c >= QK_CHUNKS and pend):
                        turn_rot(*pend.pop(0))
                    if (c, t) in spread_at:
                        spread_q(spread_at[c, t])
                    if (c, t) == (5, 1):
                        turn_scores()
                if c >= 1:
                    pe.wait_ge(S["part_evac"], c)
                for k in range(KD):
                    q = k % 4
                    last = pe.matmul(bank[3][32 * q:32 * q + 32, 0:CW], xsT[:, k, :], w[:, k, :],
                                     start=(k < 4), stop=(k >= 4))
                last.then_inc(S["part_done"], 1)
            def prompt_scores(p):
                qt, hp = pair_units[p]
                n = (qt + 1) * P
                if p == 0:
                    pe.wait_ge(S["blk_evac_v"], 2)
                    pe.wait_ge(S["comb_read"], QKV_CHUNKS)
                elif p == 1:
                    pe.wait_ge(S["blk_evac_v"], 4)
                else:
                    pe.wait_ge(S["masked"], 2 * p - 2)
                for h in range(2):
                    o = DH * h
                    pe.matmul(score_bank[p % 2][h][:, 0:n], qT[o:o + DH, hp, qt * P:(qt + 1) * P], kT[o:o + DH, hp, 0:n],
                              start=True, stop=True).then_inc(S["s_done"], 1)

            turn_probs()
            for i, cb in enumerate(BLOCKS):
                c = QKV_CHUNKS + cb // 3
                if i < 2:
                    pe.wait_ge(w_in_s[c % WRING], 16 * (c // WRING + 1))
                w = wchunk[c % WRING]
                o = (cb % 3) * P
                if i < 3:
                    pe.wait_ge(S["v_evac"], 2 * NT - 2 + i)
                if i == 0:
                    pe.wait_ge(S["part_evac"], QKV_CHUNKS)
                if i == 1:
                    pe.wait_ge(S["probs_placed"], 1)
                if i in (2, 4):
                    pe.wait_ge(S["blk_evac_a"], i // 2)
                if i in (3, 5):
                    pe.wait_ge(S["blk_evac_v"], i // 2)
                for k in range(KD):
                    pe.matmul(bank[i % 3][:, :], w[:, k, o:o + P], xT[:, k, :], start=(k == 0), stop=(k == KD - 1))
                    last = pe.matmul(bank[3 + 2 * (i % 2)][:, 0:DEC], w[:, k, o:o + P], xsT[:, k, 0:DEC],
                                     start=(k == 0), stop=(k == KD - 1))
                last.then_inc(S["blk_done"], 1)
                if i == 0:
                    combine(QKV_CHUNKS - 1)
                for b in ((0,), (1, 2), (3, 4), (5, 6), (7,), ())[i]:
                    sample_values(b)
                if i == 4:
                    prompt_scores(0)
                if i == 4:
                    pe.wait_ge(S["comb_read"], QKV_CHUNKS)
                    for j in range(2):
                        last = pe.matmul(bank[6 + j][0:DEC * H, 0:CW], selfT, vs[0:DEC, j * CW:(j + 1) * CW],
                                         start=False, stop=True)
                    last.then_inc(S["pv_s"], 1)
            pe.wait_ge(S["head_done"], 2)
            for j in range(2):
                last = pe.matmul(bank[6 + j][0:DEC, 0:CW], sm("sample")[0:DEC * H, :],
                                 head_out[0:DEC * H, j * CW:(j + 1) * CW], start=True, stop=True)
            last.then_inc(S["gathered_s"], 1)

            for p in range(NU + 2):
                if 1 <= p < NU:
                    prompt_scores(p)
                if 1 <= p <= NU:
                    u = p - 1
                    qt, hp = pair_units[u]
                    for h in range(2):
                        pe.wait_ge(S["exp_done"], 2 * u + h + 1)
                        if u >= 1:
                            pe.wait_ge(S["p_evac_v" if h else "p_evac_a"], u)
                        for j in range(qt + 1):
                            last = pe.transpose(turn_bank[h][:, j * P:(j + 1) * P], scores_sb[u % 2][h][:, j * P:(j + 1) * P],
                                                ident[:, :])
                        last.then_inc(S["p_turned"], 1)
                if p >= 2:
                    u = p - 2
                    qt, hp = pair_units[u]
                    if u >= 2:
                        pe.wait_ge(S["o_evac"], u - 1)
                    else:
                        pe.wait_ge(S["attn_s_done"], 1)
                    for h in range(2):
                        pe.wait_ge(S["p_evac_v" if h else "p_evac_a"], u + 1)
                        for j in range(qt + 1):
                            last = pe.matmul(bank[6 + u % 2][:, h * DH:(h + 1) * DH], probs_t[u % 2][h][:, j * P:(j + 1) * P],
                                             v_rows[:, j, (2 * hp + h) * DH:(2 * hp + h + 1) * DH],
                                             start=(j == 0), stop=(j == qt))
                    last.then_inc(S["o_done"], 1)

            pe.wait_ge(S["conv_done"], 1)
            for h in range(2):
                pe.transpose(bank[4][0:2, h * P:(h + 1) * P], cuT[:, h, SEQ:SEQ + 2], ident[:, :])
                last = pe.transpose(bank[4][0:DEC, DC + h * P:DC + (h + 1) * P], cu_s[:, h, 2, :], ident[:, :])
            last.then_inc(S["conv_turned"], 1)
            pe.wait_ge(S["y_squared"], 1)
            pe.wait_ge(S["wr_in"], 80)
            for t in range(NT + 1):
                n = TILES[t]
                for h in range(2):
                    last = pe.matmul(bank[3][0:n, 64 + t:65 + t], ysq[:, h, t * P:t * P + n], ones[:, 0:1],
                                     start=(h == 0), stop=(h == 1))
            last.then_inc(S["ssc_done"], 1)

            for g in range(2 * NT + 1):
                t = g // 2
                if g >= 2:
                    pe.wait_ge(S["a_evac"], g - 1)
                if t < NT:
                    pe.wait_ge(S["o_evac"], NP * NT)
                    for k in range(3):
                        o = (3 * (g % 2) + k) * P
                        last = pe.transpose(bank[g % 2][:, k * P:(k + 1) * P], attn[:, t, o:o + P], ident[:, :])
                else:
                    for k in range(NP):
                        last = pe.transpose(bank[g % 2][:, k * DEC:(k + 1) * DEC], attn_s[0:DEC, k * P:(k + 1) * P],
                                            ident[0:DEC, 0:DEC])
                last.then_inc(S["a_turned"], 1)
            pe.wait_ge(S["wout_in"], 16)
            pe.wait_ge(S["a_evac"], 2 * NT + 1)
            pe.wait_ge(S["y_gained"], 1)

            def turn_h(t):
                pe.wait_ge(S["h_scaled"], t + 1)
                pe.wait_ge(S["conv_evac"], 1)
                n = TILES[t]
                for g in range(2):
                    if 2 * t + g >= 2:
                        pe.wait_ge(S["h_evac"], 2 * t + g - 1)
                    for k in range(4):
                        o = (4 * g + k) * P
                        last = pe.transpose(bank[4 + g][:, k * P:k * P + n], hn[t % 2][0:n, o:o + P], ident[0:n, 0:n])
                    last.then_inc(S["h_turned"], 1)

            def route(t):
                pe.wait_ge(S["h_evac"], 2 * t + 2)
                if t >= 1:
                    pe.wait_ge(S["r_evac"], t)
                for k in range(KD):
                    last = pe.matmul(bank[6][0:TILES[t], 0:G + E], hnT[t % 2][:, k, 0:TILES[t]], wr[:, k, :],
                                     start=(k == 0), stop=(k == KD - 1))
                last.then_inc(S["r_done"], 1)

            for t in range(NT):
                for g in range(4):
                    u = 4 * t + g
                    if u >= 4:
                        pe.wait_ge(S["op_evac"], u - 3)
                    cols = slice((g % 2) * 512, (g % 2 + 1) * 512)
                    rng = range(NP) if g < 2 else range(NP, KD)
                    for k in rng:
                        src = attnT[:, k, t * P:(t + 1) * P] if k < NP else yT[:, k - NP, t * P:(t + 1) * P]
                        last = pe.matmul(bank[u % 4][:, :], src, wout[:, k, cols], start=(k == rng[0]), stop=(k == rng[-1]))
                    last.then_inc(S["op_done"], 1)
                if t >= 1:
                    turn_h(t - 1)
                if t >= 2:
                    route(t - 2)
            for j in range(2):
                pe.wait_ge(S["op_evac"], 4 * NT - 3 + j)
                for k in (0, 2, 4, 6, 1, 3, 5, 7):
                    q = k // 2
                    last = pe.matmul(bank[j][32 * q:32 * q + 32, :], mixsT[:, k, :], wout[:, k, j * 512:(j + 1) * 512],
                                     start=(k % 2 == 0), stop=(k % 2 == 1))
                last.then_inc(S["op_done"], 1)
            turn_h(NT - 1)
            route(NT - 2)
            pe.wait_ge(S["opp_evac"], 2)
            for g in range(4):
                pe.wait_ge(S["op_evac"], min(4 * NT - 3 + g, 4 * NT) if g >= 2 else 4 * NT)
                part = partial_o[:, (g % 2) * 512:(g % 2 + 1) * 512]
                pe.matmul(bank[g][0:DEC, :], sm("quada" if g < 2 else "quadc"), part, start=True, stop=True)\
                    .then_inc(S["op_done"], 1)
            route(NT - 1)
            turn_h(NT)
            route(NT)

            pe.wait_ge(S["assign"], 1)
            pe.wait_ge(S["r_evac"], NT + 1)
            pe.matmul(bank[6][:, 0:160], tri[:, :], assigned, start=True, stop=True)
            pe.matmul(bank[7][:, 0:160], ones[:, :], assigned, start=True, stop=True).then_inc(S["count_done"], 1)

            def pair(i, s, turn, first):
                if not first:
                    pe.wait_ge(S["silu_done"], i)
                    pe.wait_ge(S["act_done"], i)
                pe.wait_ge(S["xg_evac"], i + 1)
                pe.wait_ge(gu_in[s], 64 * turn)
                for k in range(KD):
                    for h in range(2):
                        last = pe.matmul(bank[2][64 * h:64 * h + 64, :], xgT[:, k, 64 * h:64 * h + 64],
                                         gate_up[s][h][:, k, :], start=(k == 0), stop=(k == KD - 1))
                last.then_inc(S["gu_done"], 1)

            def turn_tokens(i, s, turn, first):
                pe.wait_ge(xg_sem[s], turn)
                if not first:
                    pe.wait_ge(S["xg_evac"], i)
                for k in range(KD):
                    last = pe.transpose(bank[k // 4][:, (k % 4) * P:(k % 4 + 1) * P], xg[s][:, k * P:(k + 1) * P], ident[:, :])
                last.then_inc(S["xg_turned"], 1)

            def pair_down(i, s, turn, first):
                pe.wait_ge(dn_in[s], 32 * turn)
                pe.wait_ge(S["act_done"], i + 1)
                for c in range(2):
                    last = pe.transpose(bank[3][:, c * P:(c + 1) * P], hgu[:, c * P:(c + 1) * P], ident[:, :])
                last.then_inc(S["ht_done"], 1)
                pe.wait_ge(S["ht_evac"], i + 1)
                if not first:
                    pe.wait_ge(S["dn_evac_a"], i)
                    pe.wait_ge(S["dn_evac_v"], i)
                for j in range(2):
                    for c in range(2):
                        for h in range(2):
                            last = pe.matmul(bank[4 + j][64 * h:64 * h + 64, :], hT[:, c, 64 * h:64 * h + 64],
                                             down[s][h][:, c, j * 512:(j + 1) * 512], start=(c == 0), stop=(c == 1))
                last.then_inc(S["dn_done"], 1)

            turn_tokens(0, 0, 16, True)
            pair(0, 0, 1, True)
            turn_tokens(1, 1, 16, False)
            pair_down(0, 0, 1, True)
            with pe.Fori(0, 4) as j:
                for n, s in enumerate((1, 2, 0)):
                    i = 3 * j + 1 + n
                    turn = j + 1 + (1 if s == 0 else 0)
                    pair(i, s, turn, False)
                    turn_tokens(i + 1, (s + 1) % 3, 16 * (j + 1) + (16 if s != 1 else 0), False)
                    pair_down(i, s, turn, False)
            for i in range(13, 16):
                s = i % 3
                pair(i, s, i // 3 + 1, False)
                if i < 15:
                    turn_tokens(i + 1, (s + 1) % 3, 16 * ((i + 1) // 3 + 1), False)
                pair_down(i, s, i // 3 + 1, False)
            pe.wait_ge(S["flag_ready"], 1)
            more = pe.value_load(flag[0:1, 0:1], min_val=0, max_val=1)
            with pe.If(more > 0):
                with pe.Fori(0, OV_PAIRS // 3) as j:
                    for n, s in enumerate((1, 2, 0)):
                        i = 3 * j + 16 + n
                        turn = j + 6 + (1 if s == 0 else 0)
                        turn_tokens(i, s, 16 * turn, False)
                        pair(i, s, turn, False)
                        pair_down(i, s, turn, False)
                pe.nop()
            pe.nop()

        @block.scalar
        def _(act):
            chain = Chain(act, S["act_link"])
            act.wait_ge(S["pads_zero"], 1)
            for t in range(NT + 1):
                n = TILES[t]
                act.wait_ge(x_in[t], 16)
                chain.step(act.activation(junk_x[0:n, :], x[0:n, t, :], ACT.Square, accum_out=ssx[0:n, t:t + 1]))
                act.activation(stdx[0:n, t:t + 1], ssx[0:n, t:t + 1], ACT.Sqrt, bias=eps[0:n, :], scale=1.0 / D)\
                    .then_inc(S["x_std"], 1)

            def part_copy(c):
                act.wait_ge(S["part_done"], c + 1)
                if c >= 1:
                    act.wait_ge(S["comb_done"], c)
                act.activation(partial, bank[3][:, 0:CW], ACT.Copy).then_inc(S["part_evac"], 1)

            def rot_copy(c, t):
                act.wait_ge(S["rot_turned"], unit(c, t) + 1)
                dst = (qT if c < 2 else kT)[:, 3 * (c % 2):3 * (c % 2) + 3, t * P:(t + 1) * P]
                act.activation(dst, bank[5][:, 0:CW].rearrange("p (a b) -> p a b", a=3), ACT.Copy).then_inc(S["rot_evac"], 1)

            def root(src, w, k):
                act.activation(zsq[0:w, :], src, ACT.Square).then_inc(S["z_squared"], 1)
                act.wait_ge(S["z_ssq"], k + 1)
                act.activation(zstd[0:w, :], zss[0:w, :], ACT.Sqrt, bias=eps[0:w, :], scale=1.0 / DH).then_inc(S["z_std"], 1)

            k = 0
            pend = []
            for c in range(QKV_CHUNKS):
                for t in range(NT):
                    n = unit(c, t)
                    act.wait_ge(S["z_done"], n + 1)
                    if c < QK_CHUNKS:
                        root(bank[n % 3][:, 0:CW], P, k)
                        k += 1
                        pend.append((c, t))
                    else:
                        act.activation(v_rows[:, t, (c - 4) * CW:(c - 3) * CW], bank[n % 3][:, 0:CW], ACT.Copy)\
                            .then_inc(S["v_evac"], 1)
                    if t == 1 and c >= 1:
                        cc = c - 1
                        act.wait_ge(S["comb_done"], cc + 1)
                        if cc < QK_CHUNKS:
                            root(bank[4][0:DEC, 0:CW], DEC, k)
                            k += 1
                        else:
                            act.activation(vs[0:DEC, (cc - 4) * CW:(cc - 3) * CW], bank[4][0:DEC, 0:CW], ACT.Copy)\
                                .then_inc(S["comb_read"], 1)
                    if len(pend) > 2 or (c >= QK_CHUNKS and pend):
                        rot_copy(*pend.pop(0))
                    if (c, t) == (1, 0):
                        act.wait_ge(S["state_turned"], 1)
                        for h in range(2):
                            act.activation(cu_s[:, h, 0:2, :], bank[4][:, h * 16:h * 16 + 16]
                                           .rearrange("p (b j) -> p j b", j=2), ACT.Copy).then_inc(S["cu_ready"], 1)
                    if (c, t) == (5, 2):
                        act.wait_ge(S["soft_in"], 1)
                        act.activation(prob_s[0:96, :], neg_s[0:96, :], ACT.Exp, bias=nm_s[0:96, :], scale=-1.0,
                                       accum_out=den_s[0:96, :]).then_inc(S["soft_done"], 1)
                part_copy(c)
            for h in range(2):
                i = 2 * h
                act.wait_ge(S["blk_done"], i + 1)
                act.activation(cuT[:, h, 2:2 + SEQ], bank[i % 3][:, :], ACT.Copy)
                act.activation(cu_s[:, h, 2, :], bank[3][:, 0:DEC], ACT.Copy).then_inc(S["blk_evac_a"], 1)
                if h == 0:
                    act.wait_ge(S["comb_done"], QKV_CHUNKS)
                    act.activation(vs[0:DEC, CW:2 * CW], bank[4][0:DEC, 0:CW], ACT.Copy).then_inc(S["comb_read"], 1)

            for p in range(NU + 1):
                if p < NU:
                    qt, hp = pair_units[p]
                    n = (qt + 1) * P
                    if p // NP >= 2 and hp == 0:
                        act.wait_ge(S["o_evac"], NP * (p // NP - 1))
                    for h in range(2):
                        u = 2 * p + h
                        act.wait_ge(S["masked"], u + 1)
                        buf = scores_sb[p % 2][h][:, 0:n]
                        act.activation(buf, buf, ACT.Exp, bias=nmax[:, u % 4:u % 4 + 1], scale=-1.0,
                                       accum_out=den[:, u % 24:u % 24 + 1]).then_inc(S["exp_done"], 1)
                if p >= 1:
                    u = p - 1
                    n = (pair_units[u][0] + 1) * P
                    act.wait_ge(S["p_turned"], 2 * u + 1)
                    if u >= 2:
                        act.wait_ge(S["o_done"], u - 1)
                    act.activation(probs_t[u % 2][0][:, 0:n], turn_bank[0][:, 0:n], ACT.Copy).then_inc(S["p_evac_a"], 1)
                if p == 1:
                    act.wait_ge(S["conv_done"], 1)
                    act.activation(ysq, yT, ACT.Square).then_inc(S["y_squared"], 1)
            act.wait_ge(S["conv_turned"], 1)
            act.activation(conv_rows[0:2, 0:DC], bank[4][0:2, 0:DC], ACT.Copy)
            act.activation(conv_rows[0:DEC, DC:2 * DC], bank[4][0:DEC, DC:2 * DC], ACT.Copy).then_inc(S["conv_evac"], 1)
            act.wait_ge(S["ssc_done"], 1)
            act.activation(ssc[:, 0:NT], bank[3][:, 64:64 + NT], ACT.Sqrt, bias=eps, scale=1.0 / DC)
            act.activation(ssc[0:DEC, NT:NT + 1], bank[3][0:DEC, 64 + NT:65 + NT], ACT.Sqrt, bias=eps[0:DEC, :],
                           scale=1.0 / DC).then_inc(S["ssc_std"], 1)
            act.wait_ge(S["o_evac"], NP * NT)
            act.wait_ge(S["rows_out"], 48)
            for t in range(NT):
                if t:
                    act.wait_ge(S["a_squared"], t)
                act.activation(junk[:, 0:DA], attn[:, t, :], ACT.Square, accum_out=ssa[:, t:t + 1]).then_inc(S["a_squared"], 1)
            act.wait_ge(S["a_squared"], NT)
            act.activation(junk[0:DEC, 0:DA], attn_s[0:DEC, :], ACT.Square, accum_out=ssa[0:DEC, NT:NT + 1])\
                .then_inc(S["a_squared"], 1)
            act.wait_ge(S["a_squared"], NT + 1)
            act.activation(stda[:, 0:NT], ssa[:, 0:NT], ACT.Sqrt, bias=eps, scale=1.0 / DA)
            act.activation(stda[0:DEC, NT:NT + 1], ssa[0:DEC, NT:NT + 1], ACT.Sqrt, bias=eps[0:DEC, :], scale=1.0 / DA)\
                .then_inc(S["a_std"], 1)
            for t in range(NT + 1):
                n = TILES[t]
                if t == NT:
                    for j in range(2):
                        act.wait_ge(S["op_done"], 4 * NT + 1 + j)
                        act.activation(partial_o[:, j * 512:(j + 1) * 512], bank[j][:, :], ACT.Copy).then_inc(S["opp_evac"], 1)
                act.wait_ge(S["h_done"], t + 1)
                chain.step(act.activation(junk[0:n, :], x[0:n, t, :], ACT.Square, accum_out=ssf[0:n, t:t + 1]))
                act.activation(stdf[0:n, t:t + 1], ssf[0:n, t:t + 1], ACT.Sqrt, bias=eps[0:n, :], scale=1.0 / D)\
                    .then_inc(S["h_std"], 1)
            act.wait_ge(S["r_sub"], 1)
            act.activation(eg, eg, ACT.Exp).then_inc(S["r_exp1"], 1)
            act.wait_ge(S["r_sub2"], 1)
            act.activation(e2, dd, ACT.Exp).then_inc(S["r_exp2"], 1)

            def pair(i, s, turn, first):
                act.wait_ge(S["gu_done"], i + 1)
                if not first:
                    act.wait_ge(S["act_done"], i)
                act.activation(hs, bank[2][:, 0:F], ACT.Silu).then_inc(S["silu_done"], 1)
                act.wait_ge(S["ht_done"], i + 1)
                if not first:
                    act.wait_ge(S["dn_done"], i)
                act.activation(hT, bank[3][:, 0:2 * P].rearrange("p (c n) -> p c n", c=2), ACT.Copy).then_inc(S["ht_evac"], 1)
                if turn is not None:
                    act.wait_ge(res_sem[s], turn)
                act.wait_ge(S["dn_done"], i + 1)
                act.activation(yo[s][:, 0:512], bank[4][:, :], ACT.Copy).then_inc(S["dn_evac_a"], 1)

            act.wait_ge(S["count_done"], 1)
            for i in range(4):
                pair(i, i % 3, 16 * (i // 3) if i >= 3 else None, i == 0)
            with act.Fori(0, 4) as j:
                for n, s in enumerate((1, 2, 0)):
                    pair(3 * j + 4 + n, s, 16 * (j + 1) + (16 if s == 0 else 0), False)
            act.wait_ge(S["flag_ready"], 1)
            more = act.value_load(flag[0:1, 0:1], min_val=0, max_val=1)
            with act.If(more > 0):
                with act.Fori(0, OV_PAIRS // 3) as j:
                    for n, s in enumerate((1, 2, 0)):
                        pair(3 * j + 16 + n, s, 16 * (j + 5) + (16 if s == 0 else 0), False)
                act.nop()
            act.nop()

        @block.vector
        def _(dve):
            chain = Chain(dve, S["dve_link"])

            def tt(out, a, b, op):
                return dve.tensor_tensor(out, a, b, op)

            dve.memset(eps, EPS)
            dve.memset(xsT, 0.0)
            dve.memset(mixsT, 0.0)
            dve.memset(logits[:, :, :], 0.0).then_inc(S["pads_zero"], 1)
            dve.wait_ge(S["pads_zero"], 1)
            dve.wait_ge(S["gains_turned"], 1)
            chain.step(dve.tensor_copy(gains[:, 0:30], bank[7][:, 0:30]))

            def x_scale(t):
                n = TILES[t]
                dve.wait_ge(S["x_std"], t + 1)
                chain.step(dve.reciprocal(rx[0:n, t:t + 1], stdx[0:n, t:t + 1]))
                dve.tensor_scalar(xn[0:n, t, :], x[0:n, t, :], rx[0:n, t:t + 1], None, ALU.mult).then_inc(S["x_scaled"], 1)

            def x_copy(g):
                dve.wait_ge(S["x_turned"], g + 1)
                t = g // 2
                if t < NT:
                    k = 4 * (g % 2)
                    tt(xT[:, k:k + 4, t * P:(t + 1) * P], bank[g % 3][:, :].rearrange("p (a b) -> p a b", a=4),
                       bc(gains[:, k:k + 4], 2, P, [P, 4, P]), ALU.mult).then_inc(S["x_evac"], 1)
                else:
                    tt(xsT[:, :, 0:DEC], bank[g % 3][:, 0:KD * DEC].rearrange("p (a b) -> p a b", a=KD),
                       bc(gains[:, 0:KD], 2, DEC, [P, KD, DEC]), ALU.mult).then_inc(S["x_evac"], 1)

            x_scale(0)
            for t in range(NT + 1):
                if t < NT:
                    x_scale(t + 1)
                x_copy(2 * t)
                if t < NT:
                    x_copy(2 * t + 1)
            dve.wait_ge(S["misc_in"], 96)
            half = DH // 2
            for i, scale in ((0, DH ** -0.5), (1, 1.0)):
                g = gqk[:, i, :]
                dve.scalar_tensor_tensor(rope_g[2 * i], cos, scale, bc(g, 1, T5, [P, T5, DH]), ALU.mult, ALU.mult)
                for a in range(2):
                    b = 1 - a
                    last = dve.scalar_tensor_tensor(rope_g[2 * i + 1][:, :, a * half:(a + 1) * half],
                                                    sin[:, :, a * half:(a + 1) * half], scale,
                                                    bc(g[:, b * half:(b + 1) * half], 1, T5, [P, T5, half]),
                                                    ALU.mult, ALU.mult)
            last.then_inc(S["rope_ready"], 1)
            dve.wait_ge(S["rope_ready"], 1)

            def norm_rope(src, w, c, t, k, dst, out_sem):
                v6 = "p (a b) -> p a b"
                dve.wait_ge(S["z_squared"], k + 1)
                dve.tensor_reduce(zss[0:w, :], zsq[0:w, :].rearrange(v6, a=6), AX.X, ALU.add).then_inc(S["z_ssq"], 1)
                dve.wait_ge(S["z_std"], k + 1)
                chain.step(dve.reciprocal(zr[0:w, :], zstd[0:w, :]))
                if k >= 1:
                    dve.wait_ge(S["z_sin"], k)
                tt(zn[0:w, :].rearrange(v6, a=6), src.rearrange(v6, a=6), bc(zr[0:w, :], 2, DH, [w, 6, DH]), ALU.mult)\
                    .then_inc(S["z_copied" if w == P else "comb_read"], 1)
                if w == P:
                    dve.wait_ge(S["z_copied"], unit(c, t) + 1)
                else:
                    dve.wait_ge(S["comb_read"], c + 1)
                dve.engine_nop().then_inc(S["z_cos"], 1)
                chain.step(tt(zcos[0:w, :].rearrange(v6, a=6), zn[0:w, :].rearrange(v6, a=6),
                              bc(rope_g[2 * (c // 2)][0:w, t, :], 1, 6, [w, 6, DH]), ALU.mult))
                dve.wait_ge(S["z_sin"], k + 1)
                tt(dst, zcos[0:w, :], zsin[0:w, :], ALU.add).then_inc(out_sem, 1)

            def sample_scores(b):
                dve.wait_ge(kv_in[b % 2], 48 * (b // 2 + 1))
                dve.wait_ge(S["qb_done"], b + 1)
                kb = kv[b % 2]
                for j in range(2):
                    last = tt(kb[:, :, j * CW:(j + 1) * CW], kb[:, :, j * CW:(j + 1) * CW],
                              bc(bank[6 + j][:, 0:CW], 1, 2, [P, 2, CW]), ALU.mult)
                last.then_inc(S["qb_used"], 1)
                dve.wait_ge(S["qb_used"], b + 1)
                for i in range(2):
                    last = dve.tensor_reduce(sc[:, i, b * H:(b + 1) * H], kb[:, i, :].rearrange("p (h d) -> p h d", h=H),
                                             AX.X, ALU.add)
                last.then_inc(S["scores_s"], 1)

            k = 0
            scores_at = {(3, 0): 0, (3, 2): 1, (3, 3): 2, (4, 0): 3}
            for c in range(QK_CHUNKS + 1):
                for t in range(NT):
                    if c < QK_CHUNKS:
                        n = unit(c, t)
                        dve.wait_ge(S["z_done"], n + 1)
                        if n >= 2:
                            dve.wait_ge(S["rot_turned"], n - 1)
                            if n - 2 >= 2 * NT:
                                dve.wait_ge(rot_out[n % 2], 16 * ((n - 2 - 2 * NT) // 2 + 1))
                        norm_rope(bank[n % 3][:, 0:CW], P, c, t, k, rot[n % 2], S["rot_done"])
                        k += 1
                    if t == 1 and c >= 1:
                        cc = c - 1
                        dve.wait_ge(S["comb_done"], cc + 1)
                        norm_rope(bank[4][0:DEC, 0:CW], DEC, cc, NT, k, (qs if cc < 2 else ks)[0:DEC, (cc % 2) * CW:(cc % 2 + 1) * CW],
                                  S["rope_ready"])
                        k += 1
                    if (c, t) in scores_at:
                        sample_scores(scores_at[c, t])
            for b in range(4, DEC):
                sample_scores(b)
            dve.wait_ge(S["rope_ready"], 1 + QK_CHUNKS)
            chain.step(tt(qs[0:DEC, :], qs[0:DEC, :], ks[0:DEC, :], ALU.mult))
            dve.tensor_reduce(sself[0:DEC, :], qs[0:DEC, :].rearrange("p (h d) -> p h d", h=H), AX.X, ALU.add)\
                .then_inc(S["scores_s"], 1)
            chain.step(dve.memset(nm_s, 0.0))
            dve.wait_ge(S["turned_s"], 1)
            dve.wait_ge(S["self_spread"], 1)
            tt(smask[0:96, :], bank[7][0:96, 0:H], sm("head")[0:96, :], ALU.mult)
            chain.step(dve.tensor_copy(raw_s[0:96, 0:256], bank[6][0:96, 0:256]))
            chain.step(dve.tensor_reduce(raw_s[0:96, 256:257], smask[0:96, :], AX.X, ALU.add))
            dve.wait_ge(S["logc_in"], 32)
            dve.wait_ge(S["state_turned"], 1)
            dve.tensor_tensor_reduce(neg_s[0:96, :], raw_s[0:96, :], slogc[0:96, :], -1.0, 3.0e38, ALU.add, ALU.min,
                                     nm_s[0:96, :]).then_inc(S["soft_in"], 1)
            dve.wait_ge(S["soft_done"], 1)
            dve.reciprocal(rden_s[0:96, :], den_s[0:96, :])
            dve.tensor_scalar(self8[0:96, :], sm("sample")[0:96, :], prob_s[0:96, 256:257], None, ALU.mult)\
                .then_inc(S["soft_done"], 1)
            dve.wait_ge(S["probs_turned"], 1)
            dve.wait_ge(S["zero_rows"], 1)
            turned = bank[5][:, 0:192].rearrange("p (i q) -> p i q", i=2)
            for b in range(DEC):
                dve.tensor_copy(probs_s[:, :, b, b * H:(b + 1) * H], turned[:, :, b * H:(b + 1) * H])
            dve.tensor_copy(selfT, bank[5][0:DEC, 192:192 + DEC * H]).then_inc(S["probs_placed"], 1)

            def masked_scores(p):
                n = (pair_units[p][0] + 1) * P
                for h in range(2):
                    u = 2 * p + h
                    dve.wait_ge(S["s_done"], u + 1)
                    if p >= 2:
                        dve.wait_ge(S["p_turned"], u - 3)
                    dve.tensor_tensor_reduce(scores_sb[p % 2][h][:, 0:n], score_bank[p % 2][h][:, 0:n],
                                             logc[:, SEQ - n:SEQ], -1.0, 3.0e38, ALU.add, ALU.min,
                                             nmax[:, u % 4:u % 4 + 1]).then_inc(S["masked"], 1)

            chain.step(dve.memset(cuT[:, :, 0:2], 0.0))
            for h in range(2):
                i = 2 * h + 1
                dve.wait_ge(S["blk_done"], i + 1)
                dve.wait_ge(S["blk_evac_a"], h + 1)
                tt(cuT[:, h, 2:2 + SEQ], cuT[:, h, 2:2 + SEQ], bank[i % 3][:, :], ALU.mult)
                tt(cu_s[:, h, 2, :], cu_s[:, h, 2, :], bank[5][:, 0:DEC], ALU.mult).then_inc(S["blk_evac_v"], 1)
                dve.wait_ge(S["blk_evac_v"], h + 1)
                dve.wait_ge(S["cu_ready"], 2)
                for j in range(3):
                    tap = gains[:, 24 + 2 * j + h:25 + 2 * j + h]
                    for dst, src in ((yT[:, h, 0:SEQ], cuT[:, h, j:j + SEQ]), (yT[:, h, SEQ:TOK], cu_s[:, h, j, :])):
                        if j == 0:
                            last = dve.tensor_scalar(dst, src, tap, None, ALU.mult)
                        else:
                            last = dve.scalar_tensor_tensor(dst, src, tap, dst, ALU.mult, ALU.add)
                    chain.step(last)
            for h in range(2):
                i = 4 + h
                dve.wait_ge(S["blk_done"], i + 1)
                tt(yT[:, h, 0:SEQ], yT[:, h, 0:SEQ], bank[i % 3][:, :], ALU.mult)
                tt(yT[:, h, SEQ:TOK], yT[:, h, SEQ:TOK], bank[3 + 2 * (i % 2)][:, 0:DEC], ALU.mult).then_inc(S["blk_evac_v"], 1)
                if h == 0:
                    masked_scores(0)
                    dve.wait_ge(S["pv_s"], 1)
                    for i in range(2):
                        dve.wait_ge(rot_out[i], 16 * NT)
                    for j in range(2):
                        dve.scalar_tensor_tensor(head_out[0:96, j * CW:(j + 1) * CW].rearrange("p (a b) -> p a b", a=6),
                                                 bank[6 + j][0:96, 0:CW].rearrange("p (a b) -> p a b", a=6), rden_s[0:96, :],
                                                 bc(sm("head")[0:96, 6 * j:6 * j + 6], 2, DH, [96, 6, DH]), ALU.mult, ALU.mult)\
                            .then_inc(S["head_done"], 1)
            dve.wait_ge(S["blk_evac_v"], 4)
            dve.engine_nop().then_inc(S["conv_done"], 1)

            for p in range(NU + 3):
                if 1 <= p < NU:
                    masked_scores(p)
                if p == 0:
                    dve.wait_ge(S["gathered_s"], 1)
                    dve.tensor_copy(attn_s[0:DEC, 0:CW], bank[6][0:DEC, 0:CW])
                    dve.tensor_copy(attn_s[0:DEC, CW:DA], bank[7][0:DEC, 0:CW]).then_inc(S["attn_s_done"], 1)
                if p == 3:
                    dve.wait_ge(S["y_squared"], 1)
                    tt(yT, yT, bc(gains[:, 22:24], 2, TOK, [P, 2, TOK]), ALU.mult).then_inc(S["y_gained"], 1)
                    dve.wait_ge(S["y_gained"], 1)
                    dve.tensor_copy(mixsT[:, NP:KD, 0:DEC], yT[:, :, SEQ:TOK])
                if 1 <= p <= NU:
                    u = p - 1
                    n = (pair_units[u][0] + 1) * P
                    dve.wait_ge(S["p_turned"], 2 * u + 2)
                    if u >= 2:
                        dve.wait_ge(S["o_done"], u - 1)
                    dve.tensor_copy(probs_t[u % 2][1][:, 0:n], turn_bank[1][:, 0:n]).then_inc(S["p_evac_v"], 1)
                if p >= 3:
                    u = p - 3
                    qt, hp = pair_units[u]
                    dve.wait_ge(S["o_done"], u + 1)
                    chain.step(dve.reciprocal(rden[u % 2], den[:, (2 * u) % 24:(2 * u) % 24 + 2]))
                    tt(attn[:, qt, 2 * hp * DH:2 * (hp + 1) * DH].rearrange("p (a b) -> p a b", a=2),
                       bank[6 + u % 2][:, 0:P].rearrange("p (a b) -> p a b", a=2),
                       bc(rden[u % 2], 2, DH, [P, 2, DH]), ALU.mult).then_inc(S["o_evac"], 1)
            dve.wait_ge(S["ssc_std"], 1)
            dve.reciprocal(rc[:, 0:NT], ssc[:, 0:NT])
            dve.reciprocal(rc[0:DEC, NT:NT + 1], ssc[0:DEC, NT:NT + 1]).then_inc(S["conv_std"], 1)

            for g in range(2 * NT + 1):
                t = g // 2
                dve.wait_ge(S["a_turned"], g + 1)
                if t < NT:
                    k = 3 * (g % 2)
                    tt(attnT[:, k:k + 3, t * P:(t + 1) * P], bank[g % 2][:, 0:CW].rearrange("p (a b) -> p a b", a=3),
                       bc(gains[:, 16 + k:19 + k], 2, P, [P, 3, P]), ALU.mult).then_inc(S["a_evac"], 1)
                else:
                    tt(mixsT[:, 0:NP, 0:DEC], bank[g % 2][:, 0:NP * DEC].rearrange("p (a b) -> p a b", a=NP),
                       bc(gains[:, 16:16 + NP], 2, DEC, [P, NP, DEC]), ALU.mult).then_inc(S["a_evac"], 1)
            dve.wait_ge(S["a_std"], 1)
            dve.reciprocal(ra[:, 0:NT], stda[:, 0:NT])
            chain.step(dve.reciprocal(ra[0:DEC, NT:NT + 1], stda[0:DEC, NT:NT + 1]))
            dve.wait_ge(S["conv_std"], 1)

            def h_copy(t):
                n = TILES[t]
                for g in range(2):
                    dve.wait_ge(S["h_turned"], 2 * t + g + 1)
                    if t >= 2:
                        dve.wait_ge(S["r_done"], t - 1)
                    tt(hnT[t % 2][:, 4 * g:4 * g + 4, 0:n], bank[4 + g][:, :].rearrange("p (a b) -> p a b", a=4)[:, :, 0:n],
                       bc(gains[:, 8 + 4 * g:12 + 4 * g], 2, n, [P, 4, n]), ALU.mult).then_inc(S["h_evac"], 1)

            def r_copy(t):
                dve.wait_ge(S["r_done"], t + 1)
                dve.tensor_copy(logits[0:TILES[t], t, :], bank[6][0:TILES[t], 0:G + E]).then_inc(S["r_evac"], 1)

            for t in range(NT + 1):
                n = TILES[t]
                for g in range(4):
                    u = 4 * t + g
                    dve.wait_ge(S["op_done"], u + 1 + (2 if t == NT else 0))
                    cols = slice((g % 2) * 512, (g % 2 + 1) * 512)
                    r_ = (ra if g < 2 else rc)[0:n, t:t + 1]
                    if g == 2:
                        dve.wait_ge(S["op_evac"], u)
                    dve.scalar_tensor_tensor(x[0:n, t, cols], bank[u % 4][0:n, :], r_, x[0:n, t, cols], ALU.mult, ALU.add)\
                        .then_inc(S["op_evac"], 1)
                dve.wait_ge(S["op_evac"], 4 * t + 4)
                dve.engine_nop().then_inc(S["h_done"], 1)
                if t >= 1:
                    h_copy(t - 1)
                if t >= 2:
                    r_copy(t - 2)
                dve.wait_ge(S["h_std"], t + 1)
                chain.step(dve.reciprocal(rf[0:n, t:t + 1], stdf[0:n, t:t + 1]))
                if t >= 2:
                    dve.wait_ge(hn_sem[t % 2], 16 * (t // 2))
                dve.tensor_scalar(hn[t % 2][0:n, :], x[0:n, t, :], rf[0:n, t:t + 1], None, ALU.mult).then_inc(S["h_scaled"], 1)
            r_copy(NT - 1)
            h_copy(NT)
            r_copy(NT)
            dve.wait_ge(S["r_evac"], NT + 1)

            lg = logits[:, :, 0:G]
            le = logits[:, :, G:G + E].rearrange("p t (g e) -> p t g e", g=G)
            iota = sm("iota")
            step = chain.step

            def first_max(vals, m, c_, out, n):
                step(dve.tensor_reduce(m, vals, AX.X, ALU.max))
                step(tt(c_, vals, bc(m, 2, n, [P, T5, n]), ALU.is_equal))
                step(dve.scalar_tensor_tensor(c_, c_, -64.0, bc(iota[:, 0:n], 1, T5, [P, T5, n]), ALU.mult, ALU.add))
                step(dve.tensor_reduce(mn, c_, AX.X, ALU.min))
                step(tt(out, c_, bc(mn, 2, n, [P, T5, n]), ALU.is_equal))

            first_max(lg, gm, cg, ohg, G)
            step(tt(eg, lg, bc(gm, 2, G, [P, T5, G]), ALU.subtract))
            dve.engine_nop().then_inc(S["r_sub"], 1)
            step(tt(ohg, ohg, bc(sm("valid"), 2, G, [P, T5, G]), ALU.mult))
            t4 = tmp[:, 0, :, :].rearrange("p t (g e) -> p t g e", g=G)
            step(tt(t4, le, bc(ohg, 3, EG, [P, T5, G, EG]), ALU.mult))
            step(dve.tensor_reduce(leg, t4.rearrange("p t g e -> p t e g"), AX.X, ALU.add))
            first_max(leg, m1, cand, oh1, EG)
            step(dve.scalar_tensor_tensor(cand2, oh1, NEG, leg, ALU.mult, ALU.add))
            first_max(cand2, m2, cand, oh2, EG)
            step(tt(dd, m2, m1, ALU.subtract))
            dve.engine_nop().then_inc(S["r_sub2"], 1)
            for i, oh in enumerate((oh1, oh2)):
                last = tt(e12[:, i, :, :].rearrange("p t (g e) -> p t g e", g=G), bc(ohg, 3, EG, [P, T5, G, EG]),
                          bc(oh, 2, G, [P, T5, G, EG]), ALU.mult)
                step(last)
            tt(assigned.rearrange("p (t e) -> p t e", t=T5), e12[:, 0], e12[:, 1], ALU.add).then_inc(S["assign"], 1)
            dve.wait_ge(S["r_exp1"], 1)
            step(dve.tensor_reduce(gsum, eg, AX.X, ALU.add))
            step(dve.reciprocal(pg, gsum))
            dve.wait_ge(S["r_exp2"], 1)
            step(dve.tensor_scalar(dd, e2, 1.0, None, ALU.add))
            step(dve.reciprocal(dd, dd))
            step(tt(w12[:, 0, :], dd, pg, ALU.mult))
            step(tt(w12[:, 1, :], w12[:, 0, :], e2, ALU.mult))
            dve.wait_ge(S["count_done"], 1)
            step(dve.memset(posn[:, 0, :], 0.0))
            for t in range(NT):
                step(tt(posn[:, t + 1, :], posn[:, t, :], bank[7][:, t * E:(t + 1) * E], ALU.add))
            step(tt(total, posn[:, NT, :], bank[7][:, NT * E:(NT + 1) * E], ALU.add))
            step(tt(posn, posn, bank[6][:, 0:160].rearrange("p (t e) -> p t e", t=T5), ALU.add))
            for dst, src in ((pk, posn), (mr, None), (ov, None)):
                for i in range(2):
                    by = src if src is not None else bc(sm("mainrow" if dst is mr else "ovrow"), 1, T5, [P, T5, E])
                    last = tt(tmp[:, i], e12[:, i], by, ALU.mult)
                    step(last)
                step(dve.tensor_reduce(dst, tmp, AX.X, ALU.add))
            step(tt(ov, ov, pk, ALU.add))
            step(dve.scalar_tensor_tensor(mr, pk, float(PAIRS), mr, ALU.mult, ALU.add))
            step(tt(ov, ov, mr, ALU.subtract))
            step(dve.tensor_scalar(isov, pk, float(SL), None, ALU.is_ge))
            step(tt(ov, ov, isov, ALU.mult))
            step(tt(mr, mr, ov, ALU.add))
            dve.tensor_copy(addr[:, :, :], mr).then_inc(S["addr_done"], 1)
            step(dve.tensor_reduce(gm[:, 0:1], total, AX.X, ALU.max))
            dve.tensor_scalar(flag[:, :], gm[:, 0:1], float(SL), None, ALU.is_gt).then_inc(S["flag_ready"], 1)

            def tokens(i, s):
                dve.wait_ge(S["xg_turned"], i + 1)
                if not isinstance(i, int) or i > 0:
                    dve.wait_ge(S["gu_done"], i)
                for g in range(2):
                    last = tt(xgT[:, 4 * g:4 * g + 4, :], bank[g][:, :].rearrange("p (a b) -> p a b", a=4),
                              bc(gains[:, 8 + 4 * g:12 + 4 * g], 2, P, [P, 4, P]), ALU.mult)
                last.then_inc(S["xg_evac"], 1)

            def hidden(i, first):
                dve.wait_ge(S["silu_done"], i + 1)
                if not first:
                    dve.wait_ge(S["ht_done"], i)
                tt(hgu, hs, bank[2][:, F:2 * F], ALU.mult).then_inc(S["act_done"], 1)

            def result(i, s, turn):
                if turn is not None:
                    dve.wait_ge(res_sem[s], turn)
                dve.wait_ge(S["dn_done"], i + 1)
                dve.tensor_copy(yo[s][:, 512:D], bank[5][:, :]).then_inc(S["dn_evac_v"], 1)

            tokens(0, 0)
            for i in range(4):
                hidden(i, i == 0)
                tokens(i + 1, 0)
                result(i, i % 3, 16 * (i // 3) if i >= 3 else None)
            with dve.Fori(0, 3) as j:
                for n, s in enumerate((1, 2, 0)):
                    i = 3 * j + 4 + n
                    hidden(i, False)
                    tokens(i + 1, 0)
                    result(i, s, 16 * (j + 1) + (16 if s == 0 else 0))
            for i in range(13, 16):
                hidden(i, False)
                if i < 15:
                    tokens(i + 1, 0)
                result(i, i % 3, 16 * (i // 3))
            more = dve.value_load(flag[0:1, 0:1], min_val=0, max_val=1)
            with dve.If(more > 0):
                link = S["rope_ready"]
                at = [1 + QK_CHUNKS]

                def lstep(ins):
                    at[0] += 1
                    ins.then_inc(link, 1)
                    dve.wait_ge(link, at[0])

                big = cut(rt, 0, E, 8)
                lstep(tt(big[0:1], bc(total[0:1, :], 2, 8, [1, E, 8]), bc(sm("limits")[0:1, :], 1, E, [1, E, 8]), ALU.is_gt))
                lstep(dve.tensor_reduce(nb[0:1, :], big[0:1], AX.X, ALU.add))
                lstep(dve.tensor_copy(cum_a[0:1, :], nb[0:1, :]))
                a, b = cum_a, cum_b
                for sh in (1, 2, 4, 8, 16):
                    lstep(dve.tensor_copy(b[0:1, 0:sh], a[0:1, 0:sh]))
                    lstep(tt(b[0:1, sh:E], a[0:1, sh:E], a[0:1, 0:E - sh], ALU.add))
                    a, b = b, a
                for n in range(2 * OV_PAIRS):
                    lstep(dve.tensor_scalar(b[0:1, :], a[0:1, :], float(n), None, ALU.is_le))
                    lstep(dve.tensor_reduce(lst[0:1, n:n + 1], b[0:1, :], AX.X, ALU.add))
                    lstep(tt(b[0:1, :], b[0:1, :], nb[0:1, :], ALU.mult))
                    lstep(dve.tensor_reduce(lst2[0:1, n:n + 1], b[0:1, :], AX.X, ALU.add))
                    lstep(dve.tensor_scalar(lst2[0:1, n:n + 1], lst2[0:1, n:n + 1], -float(SL), OV_BASE + float(n * SL),
                                            ALU.mult, ALU.add))
                lstep(dve.scalar_tensor_tensor(lst2[0:1, :], lst[0:1, :], float(OV_ROWS), lst2[0:1, :], ALU.mult, ALU.add))
                lstep(dve.tensor_scalar(lst[0:1, :], lst[0:1, :], float(E - 1), None, ALU.min))
                lstep(dve.tensor_copy(ov_list[0:1, 0, :], lst[0:1, :]))
                dve.tensor_copy(ov_list[0:1, 1, :], lst2[0:1, :]).then_inc(S["list_done"], 1)
                with dve.Fori(0, OV_PAIRS // 3) as j:
                    for n, s in enumerate((1, 2, 0)):
                        i = 3 * j + 16 + n
                        tokens(i, 0)
                        hidden(i, False)
                        result(i, s, 16 * (j + 5) + (16 if s == 0 else 0))
                dve.nop()
            for t in range(NT + 1):
                n = TILES[t]
                dve.wait_ge(back_in[t], 16)
                for i in range(2):
                    if i == 1:
                        dve.wait_ge(S["x_scaled"], NT + 1 + t + 1)
                    dve.scalar_tensor_tensor(x[0:n, t, :], back[t][0:n, i, :], w12[0:n, i, t:t + 1], x[0:n, t, :],
                                             ALU.mult, ALU.add).then_inc(S["x_scaled" if i == 0 else "h_done"], 1)

        @block.gpsimd
        def _(pool):
            k = 0
            half = DH // 2
            for c in range(QK_CHUNKS + 1):
                todo = []
                for t in range(NT):
                    if c < QK_CHUNKS:
                        todo.append((c, t, P))
                    if t == 1 and c >= 1:
                        todo.append((c - 1, NT, DEC))
                for cc, t, w in todo:
                    pool.wait_ge(S["z_cos"], k + 1)
                    pool.wait_ge(S["rope_ready"], 1)
                    if w == P and unit(cc, t) >= 1 or w == DEC:
                        n_done = unit(cc, t) if w == P else 0
                        if w == P:
                            pool.wait_ge(S["rot_done"], n_done)
                        else:
                            pool.wait_ge(S["rot_done"], min(unit(cc + 1, 1) + 1, QK_CHUNKS * NT))
                    if w == P and t == 2 and cc >= 1:
                        pool.wait_ge(S["rope_ready"], 1 + cc)
                    zv = zn[0:w, :].rearrange("p (a b) -> p a b", a=6)
                    sv = zsin[0:w, :].rearrange("p (a b) -> p a b", a=6)
                    for a in range(2):
                        b = 1 - a
                        last = pool.tensor_tensor(sv[:, :, a * half:(a + 1) * half], zv[:, :, b * half:(b + 1) * half],
                                                  bc(rope_g[2 * (cc // 2) + 1][0:w, t, a * half:(a + 1) * half], 1, 6,
                                                     [w, 6, half]), ALU.mult)
                    last.then_inc(S["z_sin"], 1)
                    k += 1
                    if w == P and cc >= 2:
                        n = unit(cc, t)
                        pool.wait_ge(S["rot_done"], n + 1)
                        pool.dma_start(k_out[t][:, (cc - 2) * CW:(cc - 1) * CW], rot[n % 2]).then_inc(rot_out[n % 2], 16)
            pool.wait_ge(S["rope_ready"], 1 + QK_CHUNKS)
            pool.memset(probs_s, 0.0).then_inc(S["zero_rows"], 1)

            for t in range(NT + 1):
                pool.wait_ge(S["h_scaled"], t + 1)
                pool.dma_start(hn_rows[t * P:t * P + TILES[t], :], hn[t % 2][0:TILES[t], :]).then_inc(hn_sem[t % 2], 16)
            pool.wait_ge(S["addr_done"], 1)
            pool.wait_ge(S["table_in"], 16)
            pool.wait_ge(S["wr_in"], 80)
            for i in range(2):
                for t in range(NT + 1):
                    n = TILES[t]
                    pool.indirect_dma_start(table, bass.IndirectOffsetOnAxis(addr[0:n, i, t:t + 1], 0),
                                            pay_sb[0:n, t, i, :], None, bounds_check=TABLE - 1, oob_is_err=False)\
                        .then_inc(S["scattered"], 16)
            pool.wait_ge(hn_sem[0], 48)
            pool.wait_ge(hn_sem[1], 32)
            pool.wait_ge(S["h_evac"], 2 * NT + 2)
            pool.wait_ge(S["r_done"], NT + 1)
            for s in range(WSLOTS):
                pool.memset(xg[s], 0.0).then_inc(S["pool_link"], 1)
            pool.wait_ge(S["pool_link"], WSLOTS)
            pool.wait_ge(S["scattered"], 160)
            pool.dma_start(tbl[:, :, :], table[0:E * SL].rearrange("(p i) w -> p i w", i=PAIRS)).then_inc(S["tbl_in"], 16)
            pool.wait_ge(S["tbl_in"], 16)

            def gather(s, tokens):
                pool.sem_inc(S["gather_go"], 1)
                pool.indirect_dma_start(xg[s], None, hn_rows, bass.IndirectOffsetOnAxis(tokens, 0),
                                        bounds_check=TOK - 1, oob_is_err=False).then_inc(xg_sem[s], 16)

            def next_tokens(i, s):
                pool.tensor_copy(idx_g[:, s:s + 1], tbl[:, ds(i, 1), 0:1].rearrange("p i w -> p (i w)"))\
                    .then_inc(S["idx_g_ready"], 1)
                pool.wait_ge(S["idx_g_ready"], i + 1)
                gather(s, idx_g[:, s:s + 1])

            def scatter(i, s, of_table=True):
                pool.wait_ge(S["dn_evac_a"], i + 1)
                if of_table:
                    pool.tensor_copy(idx[:, s, :], tbl[:, ds(i, 1), :].rearrange("p i w -> p (i w)")).then_inc(S["idx_ready"], 1)
                    pool.wait_ge(S["idx_ready"], i + 1)
                    pool.sem_inc(S["scatter_go"], 1)
                pool.wait_ge(S["dn_evac_v"], i + 1)
                pool.sem_inc(S["scatter_go"], 1)
                pool.indirect_dma_start(results, bass.IndirectOffsetOnAxis(idx[:, s, 1:2], 0), yo[s], None,
                                        bounds_check=CHOICES - 1, oob_is_err=False).then_inc(res_sem[s], 16)

            for i in range(WSLOTS):
                next_tokens(i, i)
            pool.wait_ge(S["xg_turned"], 1)
            next_tokens(WSLOTS, 0)
            with pool.Fori(0, (PAIRS - 4) // 3) as j:
                for n in range(3):
                    i = 3 * j + n
                    pool.wait_ge(S["xg_turned"], i + 2)
                    next_tokens(i + 4, (n + 1) % 3)
                    scatter(i, n)
            for i in range(PAIRS - 4, PAIRS):
                scatter(i, i % 3)
            pool.wait_ge(res_sem[0], 96)
            pool.wait_ge(res_sem[1], 80)
            pool.wait_ge(res_sem[2], 80)
            pool.wait_ge(S["flag_ready"], 1)
            more = pool.value_load(flag[0:1, 0:1], min_val=0, max_val=1)
            with pool.If(more > 0):
                pool.wait_ge(S["list_done"], 1)
                with pool.Fori(0, OV_PAIRS // 3) as j:
                    for n, s in enumerate((1, 2, 0)):
                        i = 3 * j + 16 + n
                        k2 = 2 * (3 * j + n)
                        for h in range(2):
                            row = pool.value_load(ov_list[0:1, 1, ds(k2 + h, 1)], min_val=0, max_val=TABLE - SL)
                            pool.dma_start(idx[h * SL:(h + 1) * SL, s, :], table[ds(row, SL), :]).then_inc(S["ov_in"], 16)
                        pool.wait_ge(S["ov_in"], 32 * (3 * j + n + 1))
                        gather(s, idx[:, s, 0:1])
                        scatter(i, s, False)
                        pool.wait_ge(res_sem[s], 16 * (j + 6) + (16 if s == 0 else 0))
                        pool.sem_inc(S["ov_done"], 1)
                pool.nop()
            pool.engine_nop().then_inc(S["y_ready"], 1)


_INS = ["x_prompt", "x_sample", "cache_k", "cache_v", "state_conv", "g_norm_mix", "w_in", "g_q", "g_k", "w_conv",
        "g_attn_out", "g_conv_out", "w_out", "g_norm_ffn", "w_router_group", "w_router_expert", "w_gate", "w_up", "w_down"]
_OUTS = [(1, SEQ, D), (DEC, 1, D), (1, 1, SEQ, H, DH), (1, 1, SEQ, H, DH), (1, 1, 2, DC), (1, DEC, 1, H, DH),
         (1, DEC, 1, H, DH), (1, DEC, 2, DC)]


def kernel(**inputs):
    import concourse.bacc as _bacc
    from concourse.bass_utils import run_bass_kernel_spmd as _run

    nc = _bacc.Bacc("TRN2", target_bir_lowering=False, num_devices=1)
    arrays, args = {}, []
    given = [(n, inputs[n]) for n in _INS] + [("const", constants()[0]), ("pay", payload()), ("empty", empty_table())]
    for name, a in given:
        a = np.ascontiguousarray(a)
        arrays[f"in_{name}_dram"] = a
        args.append(nc.dram_tensor(f"in_{name}_dram", a.shape, mybir.dt.from_np(a.dtype), kind="ExternalInput").ap())
    for i, shape in enumerate(_OUTS):
        args.append(nc.dram_tensor(f"out_{i}_dram", shape, F32, kind="ExternalOutput").ap())
    build(nc, *args)
    r = _run(nc, [arrays], core_ids=[0])
    return tuple(r.results[0][f"out_{i}_dram"] for i in range(len(_OUTS)))
```

```python
from contextlib import ExitStack

import numpy as np

import concourse.bass as bass
from concourse import mybir
from concourse.alu_op_type import AluOpType as ALU

F32 = mybir.dt.float32
U32 = mybir.dt.uint32
I32 = mybir.dt.int32
ACT = mybir.ActivationFunctionType
AX = mybir.AxisListType

P = 128
SEQ, DEC, D = 512, 8, 1024
NT = SEQ // P
TILES = [P] * NT + [DEC]
KD = D // P
H, DH = 12, 64
DA, DC = H * DH, 256
NP = H // 2
EPS = 1e-6
G, EG, E, F = 4, 8, 32, 256
WBUF = 1024
CW = 384
QK_CHUNKS, QKV_CHUNKS, CHUNKS = 4, 6, 8
WRING = 3
SL = 64
PAIRS = E // 2
WSLOTS = 3
OV_PAIRS = 9
TOK = SEQ + DEC
CHOICES = 2 * TOK
OV_ROWS = 512
OV_BASE = E * SL
TABLE = OV_BASE + E * OV_ROWS + 2 * OV_PAIRS * SL
EMPTY = 1 << 14
NEG = -1.0e30


def ds(i, n):
    return bass.ds(i, n)


def constants():
    f = np.float32
    seg = {}
    p = np.arange(P)
    seg["ident"] = np.eye(P)
    seg["tri"] = (p[:, None] < p[None, :])
    seg["ones"] = np.ones((P, P))
    d = p[:, None] + 3 * P - np.arange(SEQ)[None, :]
    c = ((d >= 0) & (d <= 128)).astype(int) + ((d >= 0) & (d % 4 == 0) & (d <= 512)) + ((d >= 0) & (d % 16 == 0))
    seg["logc"] = np.where(c > 0, np.log(np.maximum(c, 1)), NEG)
    half = DH // 2
    inv = (f(10000.0) ** (-np.arange(half, dtype=f) / f(half))).astype(f)
    pos = np.concatenate([np.arange(SEQ).reshape(NT, P).T, np.full((P, 1), WBUF)], 1).astype(f)
    ang = (pos[:, :, None] * inv[None, None, :]).astype(f)
    cos, sin = np.cos(ang), np.sin(ang)
    seg["cos"] = np.concatenate([cos, cos], 2).reshape(P, -1)
    seg["sin"] = np.concatenate([-sin, sin], 2).reshape(P, -1)
    rows = np.concatenate([896 + p, 512 + 4 * np.arange(96), 16 * np.arange(32)])
    d = np.concatenate([WBUF - rows, [0]])
    c = (d <= 128).astype(int) + ((d % 4 == 0) & (d <= 512)) + (d % 16 == 0)
    seg["slogc"] = np.tile(np.log(c)[None], (P, 1))
    q = np.arange(P)
    seg["head"] = (q[:, None] % H == np.arange(H)[None]) & (q[:, None] < DEC * H)
    seg["sample"] = (q[:, None] // H == np.arange(DEC)[None])
    seg["sampleT"] = (np.arange(DEC * H)[None] // H == q[:, None])
    seg["quad"] = (q[:, None] % 32 == np.arange(DEC)[None])
    seg["quada"] = seg["quad"] & (q[:, None] < 96)
    seg["quadc"] = seg["quad"] & (q[:, None] >= 96)
    seg["valid"] = np.tile(q[:, None] < DEC, (1, 2)) | (np.arange(2)[None] == 0)
    seg["iota"] = np.tile(np.arange(EG)[None] - 64, (P, 1))
    e = np.arange(E)
    seg["mainrow"] = np.tile(((e % 2) * SL * PAIRS + e // 2)[None], (P, 1))
    seg["ovrow"] = np.tile((OV_BASE + e * OV_ROWS - SL)[None], (P, 1)) - seg["mainrow"]
    seg["limits"] = np.tile((SL * (1 + np.arange(8)))[None], (P, 1))
    at, n = {}, 0
    for k, v in seg.items():
        at[k] = (n, v.shape[1])
        n += v.shape[1]
    return np.concatenate([v.astype(f) for v in seg.values()], 1), at


def payload():
    t = np.minimum(np.arange(NT + 1)[None, :] * P + np.arange(P)[:, None], TOK - 1)
    pay = np.zeros((P, NT + 1, 2, 2), np.uint32)
    pay[..., 0] = t[:, :, None]
    pay[..., 1] = 2 * t[:, :, None] + np.arange(2)
    return pay.reshape(P, -1)


def empty_table():
    return np.full((P, TABLE // P * 2), EMPTY, np.uint32)


AT = constants()[1]


def build(nc, x_prompt, x_sample, cache_k, cache_v, state_conv, g_norm_mix, w_in, g_q, g_k, w_conv, g_attn_out,
          g_conv_out, w_out, g_norm_ffn, w_router_group, w_router_expert, w_gate, w_up, w_down, const, pay, empty,
          y_prompt, y_sample, k_prompt, v_prompt, conv_prompt, k_sample, v_sample, conv_sample):
    ctx = ExitStack()
    with ctx:
        def sb(name, shape, dt=F32):
            return ctx.enter_context(nc.sbuf_tensor(name, shape, dt))

        def sem(name):
            return ctx.enter_context(nc.semaphore(name))

        hn_rows = nc.dram_tensor("hn_rows", [TOK, D], F32, kind="Internal").ap()
        results = nc.dram_tensor("results", [CHOICES, D], F32, kind="Internal").ap()
        table = nc.dram_tensor("table", [TABLE, 2], U32, kind="Internal").ap()

        bank = [ctx.enter_context(nc.psum_tensor(f"bank{i}", [P, 512], F32)) for i in range(8)]

        SLOT = 12288
        ring = sb("ring", [P, WSLOTS * SLOT])
        work = sb("work", [P, 8192])
        x = sb("x", [P, NT + 1, D])
        rt = sb("rt", [P, 1600])

        def cut(t, off, *dims):
            n = int(np.prod(dims))
            v = t[:, off:off + n]
            if len(dims) == 2:
                return v.rearrange("p (a b) -> p a b", a=dims[0])
            if len(dims) == 3:
                return v.rearrange("p (a b c) -> p a b c", a=dims[0], b=dims[1])
            if len(dims) == 4:
                return v.rearrange("p (a b c d) -> p a b c d", a=dims[0], b=dims[1], c=dims[2])
            return v

        wchunk = [cut(ring, i * 3072, KD, CW) for i in range(WRING)]
        rope_g = [cut(ring, 9216 + i * 320, NT + 1, DH) for i in range(4)]
        zsq = cut(ring, 10496, CW)
        zn = cut(ring, 10880, CW)
        zcos = cut(ring, 11264, CW)
        zsin = cut(ring, 11648, CW)
        probs_s = cut(ring, 10496, 2, DEC, DEC * H)
        attn_s = cut(ring, 9216, DA)
        scores_sb = [[cut(ring, 6160 + (2 * i + h) * 512, 512) for h in range(2)] for i in range(2)]
        probs_t = [[cut(ring, 3072 + (2 * i + h) * 512, 512) for h in range(2)] for i in range(2)]
        ysq = cut(ring, 5120, 2, TOK)
        attn = cut(ring, 0, NT, DA)
        qT = cut(ring, SLOT, NP, SEQ)
        kT = cut(ring, SLOT + 3072, NP, SEQ)
        v_rows = cut(ring, SLOT + 6144, NT, DA)
        xn = cut(ring, SLOT + 6144, NT + 1, D)
        junk_x = cut(ring, SLOT + 11264, D)
        cuT = cut(ring, SLOT + 10256, 2, 2 + SEQ)
        cu_s = cut(ring, SLOT + 11284, 2, 3, DEC)
        conv_rows = cut(ring, SLOT + 11400, 512)
        wout = cut(ring, 2 * SLOT, KD, D)
        xT = cut(ring, 2 * SLOT + 8192, KD, SEQ)
        attnT = cut(ring, 2 * SLOT + 8192, NP, SEQ)
        partial = cut(work, 6656, CW)

        kv = [cut(work, i * 1536, 2, DA) for i in range(2)]
        qs, ks, vs = (cut(work, 3072 + i * DA, DA) for i in range(3))
        rot = [cut(work, 5376 + i * CW, CW) for i in range(2)]
        head_out = cut(work, 5376, DA)
        xsT = cut(work, 6144, KD, 32)
        mixsT = cut(work, 6400, KD, 32)
        yT = cut(work, 7152, 2, TOK)
        cos = cut(work, 7152, NT + 1, DH)
        sin = cut(work, 7472, NT + 1, DH)
        hn = [cut(work, i * D, D) for i in range(2)]
        hnT = [cut(work, 2048 + i * D, KD, P) for i in range(2)]
        junk = cut(work, 4096, D)
        partial_o = cut(work, 5120, D)

        gate_up = [[cut(ring, s * SLOT + h * 4096, KD, 2 * F) for h in range(2)] for s in range(WSLOTS)]
        down = [[cut(ring, s * SLOT + 8192 + h * 2048, 2, D) for h in range(2)] for s in range(WSLOTS)]
        xg = [cut(work, s * D, D) for s in range(WSLOTS)]
        xgT = cut(work, 3072, KD, P)
        yo = [cut(work, 4096 + s * D, D) for s in range(WSLOTS)]
        hs = cut(work, 7168, F)
        hgu = cut(work, 7424, F)
        hT = cut(work, 7680, 2, P)
        back = [cut(ring, i * 2048, 2, D) for i in range(NT + 1)]

        ident = sb("ident", [P, P])
        tri = sb("tri", [P, P])
        ones = sb("ones", [P, P])
        NSMALL = AT["limits"][0] + 8 - AT["head"][0]
        small = sb("small", [P, NSMALL])
        logc = cut(rt, 0, SEQ)
        slogc = cut(rt, 512, 257)
        raw_s, neg_s, prob_s = (cut(rt, 769 + i * 257, 257) for i in range(3))

        def sm(name):
            o, n = AT[name]
            o -= AT["head"][0]
            return small[:, o:o + n]

        gains = sb("gains", [P, 32])
        gain_rows = cut(rt, 1540, 60)
        gain_in = cut(work, 3072, P)
        gqk = cut(work, 3200, 2, DH)
        state_in = cut(rt, 1026, DC)
        wr = sb("wr", [P, KD, G + E])
        logits = sb("logits", [P, NT + 1, G + E])
        st = sb("st", [P, 184])
        pay_sb = sb("pay_sb", [P, NT + 1, 2, 2], U32)
        idx_g = pay_sb[:, 0:2, :, :].rearrange("p t k w -> p (t k w)")[:, 0:WSLOTS]
        tbl = sb("tbl", [P, PAIRS, 2], U32)
        idx = sb("idx", [P, WSLOTS, 2], U32)
        addr = sb("addr", [P, 2, NT + 1], U32)
        flag = sb("flag", [P, 1], I32)
        ov_list = sb("ov_list", [1, 2, 2 * OV_PAIRS], I32)

        ssx, stdx, rx = st[:, 0:5], st[:, 5:10], st[:, 10:15]
        zss, zstd, zr = st[:, 15:21], st[:, 21:27], st[:, 27:33]
        den = st[:, 160:184]
        rden = [st[:, 140 + 2 * i:142 + 2 * i] for i in range(2)]
        nmax = st[:, 47:51]
        ssa, ra = st[:, 51:56], st[:, 56:61]
        ssc, rc = st[:, 61:66], st[:, 66:71]
        stda = st[:, 71:76]
        sself = st[:, 76:88]
        smask = st[:, 88:100]
        nm_s, den_s, rden_s = st[:, 100:101], st[:, 101:102], st[:, 102:103]
        self8 = st[:, 103:111]
        ssf, stdf, rf = st[:, 111:116], st[:, 116:121], st[:, 121:126]
        eps = st[:, 126:127]
        selfT = raw_s[0:DEC, 0:DEC * H]
        sc = cut(rt, 1283, 2, DEC * H)
        w12 = st[:, 130:140].rearrange("p (k t) -> p k t", k=2)

        names = """const_in x_in xs_in gains_in misc_in table_in wr_in wout_in logc_in
            x_squared x_std x_scaled x_turned x_evac gains_turned gains_evac rope_ready pads_zero
            z_done z_squared z_ssq z_std z_copied z_cos z_sin rot_done rot_turned rot_evac v_evac rows_out
            part_done part_evac comb_done comb_read blk_done blk_evac_a blk_evac_v cu_ready conv_done y_squared y_gained ssc_done
            ssc_std conv_std state_turned conv_turned conv_evac conv_out
            qb_done qb_used scores_s turned_s self_spread soft_in soft_done probs_turned probs_placed v_used pv_s head_done
            gathered_s attn_s_done
            s_done masked exp_done p_turned p_evac_a p_evac_v o_done o_evac
            a_squared a_std a_r a_turned a_evac opp_done op_done op_evac opp_evac h_done
            h_squared h_std h_scaled h_turned h_evac r_done r_evac hn_out_sem
            r_exp1 r_sub r_sub2 r_exp2 assign count_done count_read addr_done counts_ready list_done scattered tbl_in idx_ready idx_g_ready ov_in
            xg_in xg_turned xg_evac gu_done silu_done act_done ht_done ht_evac dn_done dn_evac_a dn_evac_v res_out
            y_ready y_out ov_done gather_go scatter_go dve_link act_link pool_link flag_ready zero_rows""".split()
        S = {n: sem(n) for n in names}
        w_in_s = [sem(f"w_loaded{i}") for i in range(WRING)]
        kv_in = [sem(f"kv_loaded{i}") for i in range(2)]
        gu_in = [sem(f"gate_up_loaded{i}") for i in range(WSLOTS)]
        dn_in = [sem(f"down_loaded{i}") for i in range(WSLOTS)]
        xg_sem = [sem(f"xg_in{i}") for i in range(WSLOTS)]
        res_sem = [sem(f"res_out{i}") for i in range(WSLOTS)]
        hn_sem = [sem(f"hn_out{i}") for i in range(2)]
        rot_out = [sem(f"rot_out{i}") for i in range(2)]
        back_in = [sem(f"back_in{i}") for i in range(NT + 1)]
        x_in = [sem(f"x_in{i}") for i in range(NT + 1)]

        w_in_v = w_in[0].rearrange("(k p) n -> p k n", p=P)
        w_out_v = w_out[0].rearrange("(k p) n -> p k n", p=P)
        x_rows = x_prompt[0].rearrange("(t p) d -> t p d", p=P)
        xs_rows = x_sample.rearrange("b t d -> (b t) d")
        k_out = k_prompt[0, 0].rearrange("(t p) h d -> t p (h d)", p=P)
        v_out = v_prompt[0, 0].rearrange("(t p) h d -> p t (h d)", p=P)
        y_rows = y_prompt[0].rearrange("(t p) d -> t p d", p=P)
        ys_rows = y_sample.rearrange("b t d -> (b t) d")
        ck = cache_k[0].rearrange("b r h d -> b r (h d)")
        cv = cache_v[0].rearrange("b r h d -> b r (h d)")

        def bc(ap, axis, n, shape):
            return ap.unsqueeze(axis).to_broadcast(shape)

        class Chain:
            def __init__(self, eng, s):
                self.eng, self.s, self.n = eng, s, 0

            def step(self, ins):
                self.n += 1
                ins.then_inc(self.s, 1)
                self.eng.wait_ge(self.s, self.n)

        ORDER = [0, NT] + list(range(1, NT))
        GROUPS = [(0, 2), (2, 3), (3, 5)]
        BLOCKS = [2, 4, 3, 5, 0, 1]
        pair_units = [(qt, hp) for qt in reversed(range(NT)) for hp in range(NP)]
        NU = len(pair_units)
        score_bank = [[bank[0], bank[4]], [bank[1], bank[2]]]
        turn_bank = [bank[3], bank[5]]

        block = ctx.enter_context(nc.Block())
        def unit(c, t):
            return c * NT + t

        def state_cols(h):
            return state_in[0:16, h * P:(h + 1) * P]

        def r(off, *dims):
            return cut(rt, off, *dims)

        T5 = NT + 1
        assigned = r(0, 160)
        e12 = r(160, 2, T5, E)
        tmp = r(480, 2, T5, E)
        posn = r(800, T5, E)
        total = r(960, E)
        leg, cand, cand2 = r(992, T5, EG), r(1032, T5, EG), r(1072, T5, EG)
        oh1, oh2 = r(1112, T5, EG), r(1152, T5, EG)
        ohg, cg, eg = r(1192, T5, G), r(1212, T5, G), r(1232, T5, G)
        gm, gsum, pg, m1_, m2_, dd, e2, mn = (r(1252 + 5 * i, T5) for i in range(8))
        pk, mr, ov, isov = (r(1292 + 10 * i, 2, T5) for i in range(4))
        gm_max = r(1464, 1)
        nb, cum_a, cum_b = r(1332, E), r(1364, E), r(1396, E)
        lst, lst2 = r(1428, 2 * OV_PAIRS), r(1446, 2 * OV_PAIRS)

        @block.sync
        def _(sp):
            def cseg(name, dst):
                o, n = AT[name]
                return sp.dma_start(dst, const[:, o:o + n])

            for t in range(NT):
                sp.dma_start(x[:, t, :], x_rows[t]).then_inc(x_in[t], 16)
                if t == 0:
                    cseg("ident", ident[:, :]).then_inc(S["const_in"], 16)
                    for r, (g, n) in enumerate(((g_norm_mix, 8), (g_norm_ffn, 8), (g_attn_out, 6), (g_conv_out, 2))):
                        r0 = (0, 8, 16, 22)[r]
                        sp.dma_start(gain_in[r0:r0 + n, :], g[0].rearrange("(k p) -> k p", p=P)).then_inc(S["gains_in"], 16)
                    sp.dma_start(gain_in[24:30, :], w_conv[0].rearrange("j (k p) -> (j k) p", p=P)).then_inc(S["gains_in"], 16)
            sp.dma_start(x[0:DEC, NT, :], xs_rows).then_inc(x_in[NT], 16)
            for c in range(WRING):
                sp.dma_start(wchunk[c], w_in_v[:, :, c * CW:(c + 1) * CW]).then_inc(w_in_s[c], 16)
            cseg("cos", cos.rearrange("p a b -> p (a b)")).then_inc(S["misc_in"], 16)
            cseg("sin", sin.rearrange("p a b -> p (a b)")).then_inc(S["misc_in"], 16)
            sp.dma_start(gqk[:, 0, :], g_q[0].partition_broadcast(P)).then_inc(S["misc_in"], 16)
            sp.dma_start(gqk[:, 1, :], g_k[0].partition_broadcast(P)).then_inc(S["misc_in"], 16)
            sp.dma_start(state_in[0:2 * DEC, :], state_conv[0].rearrange("b j c -> (b j) c")).then_inc(S["misc_in"], 16)
            sp.dma_start(small[:, :], const[:, AT["head"][0]:AT["head"][0] + NSMALL]).then_inc(S["misc_in"], 16)
            cseg("logc", logc).then_inc(S["logc_in"], 16)
            cseg("slogc", slogc).then_inc(S["logc_in"], 16)
            cseg("tri", tri[:, :]).then_inc(S["wr_in"], 16)
            cseg("ones", ones[:, :]).then_inc(S["wr_in"], 16)
            sp.dma_start(wr[:, :, 0:G], w_router_group[0].rearrange("(k p) n -> p k n", p=P)).then_inc(S["wr_in"], 16)
            sp.dma_start(wr[:, :, G:G + E], w_router_expert[0].rearrange("(k p) n -> p k n", p=P)).then_inc(S["wr_in"], 16)
            sp.dma_start(pay_sb[:, :, :, :].rearrange("p t k w -> p (t k w)"), pay).then_inc(S["wr_in"], 16)
            sp.dma_start(table.rearrange("(p n) w -> p (n w)", p=P), empty).then_inc(S["table_in"], 16)
            sp.dma_start(conv_sample[0, :, 0, :], state_conv[0, :, 1, :]).then_inc(S["conv_out"], 16)

            def cached(b, src, s):
                sp.dma_start(kv[b % 2][:, 0, :], src[b, WBUF - P:WBUF, :]).then_inc(s, 16)
                sp.dma_start(kv[b % 2][0:96, 1, :], src[b, 512:896:4, :]).then_inc(s, 16)
                sp.dma_start(kv[b % 2][96:128, 1, :], src[b, 0:512:16, :]).then_inc(s, 16)

            def wload(c):
                if c - WRING < QKV_CHUNKS:
                    sp.wait_ge(S["part_done"], c - WRING + 1)
                sp.dma_start(wchunk[c % WRING], w_in_v[:, :, c * CW:(c + 1) * CW]).then_inc(w_in_s[c % WRING], 16)

            def keys(b):
                if b >= 2:
                    sp.wait_ge(S["scores_s"], b - 1)
                cached(b, ck, kv_in[b % 2])

            def values(b):
                if b < 2:
                    sp.wait_ge(S["scores_s"], DEC - 1 + b)
                else:
                    sp.wait_ge(S["v_used"], b - 1)
                cached(b, cv, kv_in[b % 2])

            keys(0)
            keys(1)
            wload(3)
            wload(4)
            sp.dma_start(wout, w_out_v).then_inc(S["wout_in"], 16)
            wload(5)
            keys(2)
            keys(3)
            wload(6)
            for b in range(4, DEC):
                keys(b)
            values(0)
            wload(7)
            for b in range(1, 4):
                values(b)
            sp.wait_ge(S["v_evac"], 2 * NT)
            sp.dma_start(v_out, v_rows).then_inc(S["rows_out"], 16)
            sp.wait_ge(S["comb_read"], QKV_CHUNKS)
            sp.dma_start(k_sample[0].rearrange("b t h d -> (b t) (h d)"), ks[0:DEC, :]).then_inc(S["rows_out"], 16)
            sp.dma_start(v_sample[0].rearrange("b t h d -> (b t) (h d)"), vs[0:DEC, :]).then_inc(S["rows_out"], 16)
            for b in range(4, DEC):
                values(b)
            sp.wait_ge(S["conv_evac"], 1)
            sp.dma_start(conv_prompt[0, 0], conv_rows[0:2, 0:DC]).then_inc(S["conv_out"], 16)
            sp.dma_start(conv_sample[0, :, 1, :], conv_rows[0:DEC, DC:2 * DC]).then_inc(S["conv_out"], 16)

            def gates(experts, s, which=(0, 1)):
                for h in which:
                    e = experts[h]
                    for w, o in ((w_gate, 0), (w_up, F)):
                        sp.dma_start(gate_up[s][h][:, :, o:o + F],
                                     w[0, ds(e, 1)].rearrange("e (k p) f -> p (e k) f", p=P)).then_inc(gu_in[s], 16)

            def downs(experts, s):
                for h, e in enumerate(experts):
                    sp.dma_start(down[s][h], w_down[0, ds(e, 1)].rearrange("e (k p) n -> p (e k) n", p=P)).then_inc(dn_in[s], 16)

            def expert(a, b, s, i=None):
                if i is not None:
                    sp.wait_ge(S["gu_done"], i - 2)
                gates((a, b), s)
                if i is not None:
                    sp.wait_ge(S["dn_done"], i - 2)
                downs((a, b), s)

            sp.wait_ge(S["a_turned"], 2 * NT + 1)
            sp.wait_ge(S["a_squared"], NT + 1)
            sp.wait_ge(S["rows_out"], 48)
            sp.wait_ge(S["conv_out"], 48)
            expert(0, 1, 0)
            expert(2, 3, 1)
            sp.wait_ge(S["op_done"], 4 * NT + 2)
            gates((4, 5), 2, (0,))
            downs((4, 5), 2)
            sp.wait_ge(S["op_done"], 4 * NT + 4)
            gates((4, 5), 2, (1,))
            with sp.Fori(0, 4) as j:
                for s in range(WSLOTS):
                    i = 3 * j + 3 + s
                    expert(2 * i, 2 * i + 1, s, i)
            expert(30, 31, 0, PAIRS - 1)
            sp.wait_ge(S["flag_ready"], 1)
            more = sp.value_load(flag[0:1, 0:1], min_val=0, max_val=1)
            with sp.If(more > 0):
                sp.wait_ge(S["list_done"], 1)
                with sp.Fori(0, OV_PAIRS // 3) as j:
                    for n, s in enumerate((1, 2, 0)):
                        i = 3 * j + 16 + n
                        k = 2 * (3 * j + n)
                        ea = sp.value_load(ov_list[0:1, 0, ds(k, 1)], min_val=0, max_val=E - 1)
                        eb = sp.value_load(ov_list[0:1, 0, ds(k + 1, 1)], min_val=0, max_val=E - 1)
                        expert(ea, eb, s, i)
                sp.nop()
            sp.wait_ge(S["y_ready"], 1)
            res_pairs = results.rearrange("(t k) d -> t k d", k=2)
            for t in range(NT + 1):
                n = TILES[t]
                sp.dma_start(back[t][0:n], res_pairs[t * P:t * P + n]).then_inc(back_in[t], 16)
            for t in range(NT + 1):
                sp.wait_ge(S["h_done"], NT + 1 + t + 1)
                sp.dma_start(y_rows[t] if t < NT else ys_rows, x[0:TILES[t], t, :]).then_inc(S["y_out"], 16)
            sp.wait_ge(S["y_out"], 16 * (NT + 1))
            sp.wait_ge(S["rows_out"], 48)
            sp.wait_ge(S["conv_out"], 48)
            sp.wait_ge(rot_out[0], 16 * NT)
            sp.wait_ge(rot_out[1], 16 * NT)

        @block.tensor
        def _(pe):
            pe.wait_ge(S["const_in"], 16)
            pe.wait_ge(S["gains_in"], 80)
            pe.transpose(bank[7][:, 0:30], gain_in[0:30, :], ident[0:30, 0:30]).then_inc(S["gains_turned"], 1)
            for g in range(2 * NT + 1):
                t = g // 2
                pe.wait_ge(S["x_scaled"], t + 1)
                if g >= 3:
                    pe.wait_ge(S["x_evac"], g - 2)
                if t < NT:
                    for k in range(4):
                        o = (4 * (g % 2) + k) * P
                        last = pe.transpose(bank[g % 3][:, k * P:(k + 1) * P], xn[:, t, o:o + P], ident[:, :])
                else:
                    for k in range(KD):
                        last = pe.transpose(bank[g % 3][:, k * DEC:(k + 1) * DEC], xn[0:DEC, t, k * P:(k + 1) * P],
                                            ident[0:DEC, 0:DEC])
                last.then_inc(S["x_turned"], 1)
            pe.wait_ge(S["x_evac"], 2 * NT + 1)
            pe.wait_ge(S["pads_zero"], 1)

            def turn_rot(c, t):
                n = unit(c, t)
                pe.wait_ge(S["rot_done"], n + 1)
                if n >= 1:
                    pe.wait_ge(S["rot_evac"], n)
                for j in range(3):
                    last = pe.transpose(bank[5][:, j * P:(j + 1) * P], rot[n % 2][:, j * P:(j + 1) * P], ident[:, :])
                last.then_inc(S["rot_turned"], 1)

            def combine(c):
                pe.wait_ge(S["part_evac"], c + 1)
                if c >= 1:
                    pe.wait_ge(S["comb_read"], c)
                else:
                    pe.wait_ge(S["cu_ready"], 2)
                pe.matmul(bank[4][0:DEC, 0:CW], sm("quad"), partial, start=True, stop=True).then_inc(S["comb_done"], 1)

            def spread_q(b):
                if b >= 1:
                    pe.wait_ge(S["qb_used"], b)
                else:
                    pe.wait_ge(S["rope_ready"], 3)
                for j in range(2):
                    last = pe.matmul(bank[6 + j][:, 0:CW], ident[0:DEC, b:b + 1].to_broadcast([DEC, P]),
                                     qs[0:DEC, j * CW:(j + 1) * CW], start=True, stop=True)
                last.then_inc(S["qb_done"], 1)

            def turn_state():
                pe.wait_ge(S["misc_in"], 96)
                for h in range(2):
                    last = pe.transpose(bank[4][:, h * 16:h * 16 + 16], state_cols(h), ident[0:16, 0:16])
                last.then_inc(S["state_turned"], 1)

            def turn_scores():
                pe.wait_ge(S["scores_s"], DEC + 1)
                pe.wait_ge(S["qb_used"], DEC)
                for i in range(2):
                    last = pe.transpose(bank[6][0:DEC * H, i * P:(i + 1) * P], sc[:, i, :], ident[:, :])
                last.then_inc(S["turned_s"], 1)
                pe.matmul(bank[7][0:DEC * H, 0:H], sm("sampleT")[0:DEC, :], sself[0:DEC, :], start=True, stop=True)\
                    .then_inc(S["self_spread"], 1)

            def turn_probs():
                pe.wait_ge(S["soft_done"], 2)
                pe.wait_ge(S["rot_evac"], QK_CHUNKS * NT)
                for i in range(2):
                    pe.transpose(bank[5][:, i * 96:(i + 1) * 96], prob_s[0:DEC * H, i * P:(i + 1) * P],
                                 ident[0:DEC * H, 0:DEC * H])
                pe.transpose(bank[5][0:DEC, 192:192 + DEC * H], self8[0:DEC * H, :], ident[0:DEC * H, 0:DEC * H])\
                    .then_inc(S["probs_turned"], 1)

            def sample_values(b):
                if b == 0:
                    pe.wait_ge(S["probs_placed"], 1)
                pe.wait_ge(kv_in[b % 2], 48 * (DEC // 2 + b // 2 + 1))
                for i in range(2):
                    for j in range(2):
                        last = pe.matmul(bank[6 + j][0:DEC * H, 0:CW], probs_s[:, i, b, :], kv[b % 2][:, i, j * CW:(j + 1) * CW],
                                         start=(b == 0 and i == 0), stop=False)
                last.then_inc(S["v_used"], 1)

            spread_at = {(2, 3): 0, (3, 1): 1, (3, 3): 2, (4, 0): 3, (4, 1): 4, (4, 2): 5, (4, 3): 6, (5, 0): 7}
            pend = []
            for c in range(QKV_CHUNKS):
                pe.wait_ge(w_in_s[c % WRING], 16 * (c // WRING + 1))
                w = wchunk[c % WRING]
                for t in range(NT):
                    n = unit(c, t)
                    if 3 <= n < QK_CHUNKS * NT + 3:
                        pe.wait_ge(S["z_copied"], n - 2 if n - 3 < QK_CHUNKS * NT else 0)
                    elif n >= 3:
                        pe.wait_ge(S["v_evac"], n - 2 - QK_CHUNKS * NT)
                    for k in range(KD):
                        last = pe.matmul(bank[n % 3][:, 0:CW], xT[:, k, t * P:(t + 1) * P], w[:, k, :],
                                         start=(k == 0), stop=(k == KD - 1))
                    last.then_inc(S["z_done"], 1)
                    if (c, t) == (1, 0):
                        turn_state()
                    if t == 1 and c >= 1:
                        combine(c - 1)
                    if c < QK_CHUNKS:
                        pend.append((c, t))
                    if len(pend) > 2 or (c >= QK_CHUNKS and pend):
                        turn_rot(*pend.pop(0))
                    if (c, t) in spread_at:
                        spread_q(spread_at[c, t])
                    if (c, t) == (5, 1):
                        turn_scores()
                if c >= 1:
                    pe.wait_ge(S["part_evac"], c)
                for k in range(KD):
                    q = k % 4
                    last = pe.matmul(bank[3][32 * q:32 * q + 32, 0:CW], xsT[:, k, :], w[:, k, :],
                                     start=(k < 4), stop=(k >= 4))
                last.then_inc(S["part_done"], 1)
            def prompt_scores(p):
                qt, hp = pair_units[p]
                n = (qt + 1) * P
                if p == 0:
                    pe.wait_ge(S["blk_evac_v"], 2)
                    pe.wait_ge(S["comb_read"], QKV_CHUNKS)
                elif p == 1:
                    pe.wait_ge(S["blk_evac_v"], 4)
                else:
                    pe.wait_ge(S["masked"], 2 * p - 2)
                for h in range(2):
                    o = DH * h
                    pe.matmul(score_bank[p % 2][h][:, 0:n], qT[o:o + DH, hp, qt * P:(qt + 1) * P], kT[o:o + DH, hp, 0:n],
                              start=True, stop=True).then_inc(S["s_done"], 1)

            turn_probs()
            for i, cb in enumerate(BLOCKS):
                c = QKV_CHUNKS + cb // 3
                if i < 2:
                    pe.wait_ge(w_in_s[c % WRING], 16 * (c // WRING + 1))
                w = wchunk[c % WRING]
                o = (cb % 3) * P
                if i < 3:
                    pe.wait_ge(S["v_evac"], 2 * NT - 2 + i)
                if i == 0:
                    pe.wait_ge(S["part_evac"], QKV_CHUNKS)
                if i == 1:
                    pe.wait_ge(S["probs_placed"], 1)
                if i in (2, 4):
                    pe.wait_ge(S["blk_evac_a"], i // 2)
                if i in (3, 5):
                    pe.wait_ge(S["blk_evac_v"], i // 2)
                for k in range(KD):
                    pe.matmul(bank[i % 3][:, :], w[:, k, o:o + P], xT[:, k, :], start=(k == 0), stop=(k == KD - 1))
                    last = pe.matmul(bank[3 + 2 * (i % 2)][:, 0:DEC], w[:, k, o:o + P], xsT[:, k, 0:DEC],
                                     start=(k == 0), stop=(k == KD - 1))
                last.then_inc(S["blk_done"], 1)
                if i == 0:
                    combine(QKV_CHUNKS - 1)
                for b in ((0,), (1, 2), (3, 4), (5, 6), (7,), ())[i]:
                    sample_values(b)
                if i == 4:
                    prompt_scores(0)
                if i == 4:
                    pe.wait_ge(S["comb_read"], QKV_CHUNKS)
                    for j in range(2):
                        last = pe.matmul(bank[6 + j][0:DEC * H, 0:CW], selfT, vs[0:DEC, j * CW:(j + 1) * CW],
                                         start=False, stop=True)
                    last.then_inc(S["pv_s"], 1)
            pe.wait_ge(S["head_done"], 2)
            for j in range(2):
                last = pe.matmul(bank[6 + j][0:DEC, 0:CW], sm("sample")[0:DEC * H, :],
                                 head_out[0:DEC * H, j * CW:(j + 1) * CW], start=True, stop=True)
            last.then_inc(S["gathered_s"], 1)

            for p in range(NU + 2):
                if 1 <= p < NU:
                    prompt_scores(p)
                if 1 <= p <= NU:
                    u = p - 1
                    qt, hp = pair_units[u]
                    for h in range(2):
                        pe.wait_ge(S["exp_done"], 2 * u + h + 1)
                        if u >= 1:
                            pe.wait_ge(S["p_evac_v" if h else "p_evac_a"], u)
                        for j in range(qt + 1):
                            last = pe.transpose(turn_bank[h][:, j * P:(j + 1) * P], scores_sb[u % 2][h][:, j * P:(j + 1) * P],
                                                ident[:, :])
                        last.then_inc(S["p_turned"], 1)
                if p >= 2:
                    u = p - 2
                    qt, hp = pair_units[u]
                    if u >= 2:
                        pe.wait_ge(S["o_evac"], u - 1)
                    else:
                        pe.wait_ge(S["attn_s_done"], 1)
                    for h in range(2):
                        pe.wait_ge(S["p_evac_v" if h else "p_evac_a"], u + 1)
                        for j in range(qt + 1):
                            last = pe.matmul(bank[6 + u % 2][:, h * DH:(h + 1) * DH], probs_t[u % 2][h][:, j * P:(j + 1) * P],
                                             v_rows[:, j, (2 * hp + h) * DH:(2 * hp + h + 1) * DH],
                                             start=(j == 0), stop=(j == qt))
                    last.then_inc(S["o_done"], 1)

            pe.wait_ge(S["conv_done"], 1)
            for h in range(2):
                pe.transpose(bank[4][0:2, h * P:(h + 1) * P], cuT[:, h, SEQ:SEQ + 2], ident[:, :])
                last = pe.transpose(bank[4][0:DEC, DC + h * P:DC + (h + 1) * P], cu_s[:, h, 2, :], ident[:, :])
            last.then_inc(S["conv_turned"], 1)
            pe.wait_ge(S["y_squared"], 1)
            pe.wait_ge(S["wr_in"], 80)
            for t in range(NT + 1):
                n = TILES[t]
                for h in range(2):
                    last = pe.matmul(bank[3][0:n, 64 + t:65 + t], ysq[:, h, t * P:t * P + n], ones[:, 0:1],
                                     start=(h == 0), stop=(h == 1))
            last.then_inc(S["ssc_done"], 1)

            for g in range(2 * NT + 1):
                t = g // 2
                if g >= 2:
                    pe.wait_ge(S["a_evac"], g - 1)
                if t < NT:
                    pe.wait_ge(S["o_evac"], NP * NT)
                    for k in range(3):
                        o = (3 * (g % 2) + k) * P
                        last = pe.transpose(bank[g % 2][:, k * P:(k + 1) * P], attn[:, t, o:o + P], ident[:, :])
                else:
                    for k in range(NP):
                        last = pe.transpose(bank[g % 2][:, k * DEC:(k + 1) * DEC], attn_s[0:DEC, k * P:(k + 1) * P],
                                            ident[0:DEC, 0:DEC])
                last.then_inc(S["a_turned"], 1)
            pe.wait_ge(S["wout_in"], 16)
            pe.wait_ge(S["a_evac"], 2 * NT + 1)
            pe.wait_ge(S["y_gained"], 1)

            def turn_h(m):
                n = TILES[ORDER[m]]
                pe.wait_ge(S["h_scaled"], m + 1)
                pe.wait_ge(S["conv_evac"], 1)
                for g in range(2):
                    if m >= 1:
                        pe.wait_ge(S["h_evac"], 2 * m + g - 1)
                    for k in range(4):
                        o = (4 * g + k) * P
                        last = pe.transpose(bank[4 + g][:, k * P:k * P + n], hn[m % 2][0:n, o:o + P], ident[0:n, 0:n])
                    last.then_inc(S["h_turned"], 1)

            def route(m):
                n = TILES[ORDER[m]]
                pe.wait_ge(S["h_evac"], 2 * m + 2)
                if m >= 1:
                    pe.wait_ge(S["r_evac"], m)
                else:
                    pe.wait_ge(S["opp_evac"], 2)
                for k in range(KD):
                    last = pe.matmul(bank[6][0:n, 0:G + E], hnT[m % 2][:, k, 0:n], wr[:, k, :],
                                     start=(k == 0), stop=(k == KD - 1))
                last.then_inc(S["r_done"], 1)

            def count(b):
                pe.wait_ge(S["assign"], b + 1)
                if b >= 1:
                    pe.wait_ge(S["count_read"], b)
                m0, m1 = GROUPS[b]
                for m in range(m0, m1):
                    here = assigned[:, m * E:(m + 1) * E]
                    o = (m - m0) * 2 * E
                    pe.matmul(bank[7][:, o:o + E], tri[:, :], here, start=True, stop=True)
                    last = pe.matmul(bank[7][:, o + E:o + 2 * E], ones[:, :], here, start=True, stop=True)
                last.then_inc(S["count_done"], 1)

            for j in range(2):
                for k in (0, 2, 4, 6, 1, 3, 5, 7):
                    q = k // 2
                    last = pe.matmul(bank[6 + j][32 * q:32 * q + 32, :], mixsT[:, k, :], wout[:, k, j * 512:(j + 1) * 512],
                                     start=(k % 2 == 0), stop=(k % 2 == 1))
                last.then_inc(S["opp_done"], 1)
            def out_group(m, g):
                t, u = ORDER[m], 4 * m + g
                cols = slice((g % 2) * 512, (g % 2 + 1) * 512)
                if u >= 4:
                    pe.wait_ge(S["op_evac"], u - 3)
                if t == NT:
                    pe.wait_ge(S["opp_evac"], 2)
                    last = pe.matmul(bank[g][0:DEC, :], sm("quada" if g < 2 else "quadc"), partial_o[:, cols],
                                     start=True, stop=True)
                else:
                    rng = range(NP) if g < 2 else range(NP, KD)
                    for k in rng:
                        src = attnT[:, k, t * P:(t + 1) * P] if k < NP else yT[:, k - NP, t * P:(t + 1) * P]
                        last = pe.matmul(bank[g][:, :], src, wout[:, k, cols], start=(k == rng[0]), stop=(k == rng[-1]))
                last.then_inc(S["op_done"], 1)

            for m in (0, 1):
                for g in range(4):
                    out_group(m, g)
            turn_h(0)
            out_group(2, 0)
            turn_h(1)
            out_group(2, 1)
            route(0)
            out_group(2, 2)
            route(1)
            out_group(2, 3)
            out_group(3, 0)
            turn_h(2)
            out_group(3, 1)
            route(2)
            out_group(3, 2)
            count(0)
            out_group(3, 3)
            out_group(4, 0)
            turn_h(3)
            out_group(4, 1)
            route(3)
            out_group(4, 2)
            count(1)
            out_group(4, 3)
            turn_h(4)
            route(4)
            count(2)

            def pair(i, s, turn, first):
                if not first:
                    pe.wait_ge(S["silu_done"], i)
                    pe.wait_ge(S["act_done"], i)
                pe.wait_ge(S["xg_evac"], i + 1)
                pe.wait_ge(gu_in[s], 64 * turn)
                for k in range(KD):
                    for h in range(2):
                        last = pe.matmul(bank[2][64 * h:64 * h + 64, :], xgT[:, k, 64 * h:64 * h + 64],
                                         gate_up[s][h][:, k, :], start=(k == 0), stop=(k == KD - 1))
                last.then_inc(S["gu_done"], 1)

            def turn_tokens(i, s, turn, first):
                pe.wait_ge(xg_sem[s], turn)
                if not first:
                    pe.wait_ge(S["xg_evac"], i)
                for k in range(KD):
                    last = pe.transpose(bank[k // 4][:, (k % 4) * P:(k % 4 + 1) * P], xg[s][:, k * P:(k + 1) * P], ident[:, :])
                last.then_inc(S["xg_turned"], 1)

            def pair_down(i, s, turn, first):
                pe.wait_ge(dn_in[s], 32 * turn)
                pe.wait_ge(S["act_done"], i + 1)
                for c in range(2):
                    last = pe.transpose(bank[3][:, c * P:(c + 1) * P], hgu[:, c * P:(c + 1) * P], ident[:, :])
                last.then_inc(S["ht_done"], 1)
                pe.wait_ge(S["ht_evac"], i + 1)
                if not first:
                    pe.wait_ge(S["dn_evac_a"], i)
                    pe.wait_ge(S["dn_evac_v"], i)
                for j in range(2):
                    for c in range(2):
                        for h in range(2):
                            last = pe.matmul(bank[4 + j][64 * h:64 * h + 64, :], hT[:, c, 64 * h:64 * h + 64],
                                             down[s][h][:, c, j * 512:(j + 1) * 512], start=(c == 0), stop=(c == 1))
                last.then_inc(S["dn_done"], 1)

            turn_tokens(0, 0, 16, True)
            pair(0, 0, 1, True)
            turn_tokens(1, 1, 16, False)
            pair_down(0, 0, 1, True)
            with pe.Fori(0, 4) as j:
                for n, s in enumerate((1, 2, 0)):
                    i = 3 * j + 1 + n
                    turn = j + 1 + (1 if s == 0 else 0)
                    pair(i, s, turn, False)
                    turn_tokens(i + 1, (s + 1) % 3, 16 * (j + 1) + (16 if s != 1 else 0), False)
                    pair_down(i, s, turn, False)
            for i in range(13, 16):
                s = i % 3
                pair(i, s, i // 3 + 1, False)
                if i < 15:
                    turn_tokens(i + 1, (s + 1) % 3, 16 * ((i + 1) // 3 + 1), False)
                pair_down(i, s, i // 3 + 1, False)
            pe.wait_ge(S["flag_ready"], 1)
            more = pe.value_load(flag[0:1, 0:1], min_val=0, max_val=1)
            with pe.If(more > 0):
                with pe.Fori(0, OV_PAIRS // 3) as j:
                    for n, s in enumerate((1, 2, 0)):
                        i = 3 * j + 16 + n
                        turn = j + 6 + (1 if s == 0 else 0)
                        turn_tokens(i, s, 16 * turn, False)
                        pair(i, s, turn, False)
                        pair_down(i, s, turn, False)
                pe.nop()
            pe.nop()

        @block.scalar
        def _(act):
            chain = Chain(act, S["act_link"])
            act.wait_ge(S["pads_zero"], 1)
            for t in range(NT + 1):
                n = TILES[t]
                act.wait_ge(x_in[t], 16)
                chain.step(act.activation(junk_x[0:n, :], x[0:n, t, :], ACT.Square, accum_out=ssx[0:n, t:t + 1]))
                act.activation(stdx[0:n, t:t + 1], ssx[0:n, t:t + 1], ACT.Sqrt, bias=eps[0:n, :], scale=1.0 / D)\
                    .then_inc(S["x_std"], 1)

            def part_copy(c):
                act.wait_ge(S["part_done"], c + 1)
                if c >= 1:
                    act.wait_ge(S["comb_done"], c)
                act.activation(partial, bank[3][:, 0:CW], ACT.Copy).then_inc(S["part_evac"], 1)

            def rot_copy(c, t):
                act.wait_ge(S["rot_turned"], unit(c, t) + 1)
                dst = (qT if c < 2 else kT)[:, 3 * (c % 2):3 * (c % 2) + 3, t * P:(t + 1) * P]
                act.activation(dst, bank[5][:, 0:CW].rearrange("p (a b) -> p a b", a=3), ACT.Copy).then_inc(S["rot_evac"], 1)

            def root(src, w, k):
                act.activation(zsq[0:w, :], src, ACT.Square).then_inc(S["z_squared"], 1)
                act.wait_ge(S["z_ssq"], k + 1)
                act.activation(zstd[0:w, :], zss[0:w, :], ACT.Sqrt, bias=eps[0:w, :], scale=1.0 / DH).then_inc(S["z_std"], 1)

            k = 0
            pend = []
            for c in range(QKV_CHUNKS):
                for t in range(NT):
                    n = unit(c, t)
                    act.wait_ge(S["z_done"], n + 1)
                    if c < QK_CHUNKS:
                        root(bank[n % 3][:, 0:CW], P, k)
                        k += 1
                        pend.append((c, t))
                    else:
                        act.activation(v_rows[:, t, (c - 4) * CW:(c - 3) * CW], bank[n % 3][:, 0:CW], ACT.Copy)\
                            .then_inc(S["v_evac"], 1)
                    if t == 1 and c >= 1:
                        cc = c - 1
                        act.wait_ge(S["comb_done"], cc + 1)
                        if cc < QK_CHUNKS:
                            root(bank[4][0:DEC, 0:CW], DEC, k)
                            k += 1
                        else:
                            act.activation(vs[0:DEC, (cc - 4) * CW:(cc - 3) * CW], bank[4][0:DEC, 0:CW], ACT.Copy)\
                                .then_inc(S["comb_read"], 1)
                    if len(pend) > 2 or (c >= QK_CHUNKS and pend):
                        rot_copy(*pend.pop(0))
                    if (c, t) == (1, 0):
                        act.wait_ge(S["state_turned"], 1)
                        for h in range(2):
                            act.activation(cu_s[:, h, 0:2, :], bank[4][:, h * 16:h * 16 + 16]
                                           .rearrange("p (b j) -> p j b", j=2), ACT.Copy).then_inc(S["cu_ready"], 1)
                    if (c, t) == (5, 2):
                        act.wait_ge(S["soft_in"], 1)
                        act.activation(prob_s[0:96, :], neg_s[0:96, :], ACT.Exp, bias=nm_s[0:96, :], scale=-1.0,
                                       accum_out=den_s[0:96, :]).then_inc(S["soft_done"], 1)
                part_copy(c)
            for h in range(2):
                i = 2 * h
                act.wait_ge(S["blk_done"], i + 1)
                act.activation(cuT[:, h, 2:2 + SEQ], bank[i % 3][:, :], ACT.Copy)
                act.activation(cu_s[:, h, 2, :], bank[3][:, 0:DEC], ACT.Copy).then_inc(S["blk_evac_a"], 1)
                if h == 0:
                    act.wait_ge(S["comb_done"], QKV_CHUNKS)
                    act.activation(vs[0:DEC, CW:2 * CW], bank[4][0:DEC, 0:CW], ACT.Copy).then_inc(S["comb_read"], 1)

            def square_tile(i):
                if i:
                    act.wait_ge(S["a_squared"], i)
                else:
                    act.wait_ge(S["rows_out"], 48)
                if i < NT:
                    act.wait_ge(S["o_evac"], NP * (i + 1))
                    t = NT - 1 - i
                    act.activation(junk[:, 0:DA], attn[:, t, :], ACT.Square, accum_out=ssa[:, t:t + 1])\
                        .then_inc(S["a_squared"], 1)
                else:
                    act.activation(junk[0:DEC, 0:DA], attn_s[0:DEC, :], ACT.Square, accum_out=ssa[0:DEC, NT:NT + 1])\
                        .then_inc(S["a_squared"], 1)

            for p in range(NU + 1):
                if p < NU:
                    qt, hp = pair_units[p]
                    n = (qt + 1) * P
                    if p // NP >= 2 and hp == 0:
                        act.wait_ge(S["o_evac"], NP * (p // NP - 1))
                    for h in range(2):
                        u = 2 * p + h
                        act.wait_ge(S["masked"], u + 1)
                        buf = scores_sb[p % 2][h][:, 0:n]
                        act.activation(buf, buf, ACT.Exp, bias=nmax[:, u % 4:u % 4 + 1], scale=-1.0,
                                       accum_out=den[:, u % 24:u % 24 + 1]).then_inc(S["exp_done"], 1)
                if p >= 1:
                    u = p - 1
                    n = (pair_units[u][0] + 1) * P
                    act.wait_ge(S["p_turned"], 2 * u + 1)
                    if u >= 2:
                        act.wait_ge(S["o_done"], u - 1)
                    act.activation(probs_t[u % 2][0][:, 0:n], turn_bank[0][:, 0:n], ACT.Copy).then_inc(S["p_evac_a"], 1)
                if p % NP == 4 and p > NP:
                    square_tile(p // NP - 1)
                if p == 1:
                    act.wait_ge(S["conv_done"], 1)
                    act.activation(ysq, yT, ACT.Square).then_inc(S["y_squared"], 1)
            act.wait_ge(S["conv_turned"], 1)
            act.activation(conv_rows[0:2, 0:DC], bank[4][0:2, 0:DC], ACT.Copy)
            act.activation(conv_rows[0:DEC, DC:2 * DC], bank[4][0:DEC, DC:2 * DC], ACT.Copy).then_inc(S["conv_evac"], 1)
            act.wait_ge(S["ssc_done"], 1)
            act.activation(ssc[:, 0:NT], bank[3][:, 64:64 + NT], ACT.Sqrt, bias=eps, scale=1.0 / DC)
            act.activation(ssc[0:DEC, NT:NT + 1], bank[3][0:DEC, 64 + NT:65 + NT], ACT.Sqrt, bias=eps[0:DEC, :],
                           scale=1.0 / DC).then_inc(S["ssc_std"], 1)
            square_tile(NT - 1)
            square_tile(NT)
            act.wait_ge(S["a_squared"], NT + 1)
            act.activation(stda[:, 0:NT], ssa[:, 0:NT], ACT.Sqrt, bias=eps, scale=1.0 / DA)
            act.activation(stda[0:DEC, NT:NT + 1], ssa[0:DEC, NT:NT + 1], ACT.Sqrt, bias=eps[0:DEC, :], scale=1.0 / DA)\
                .then_inc(S["a_std"], 1)
            for j in range(2):
                act.wait_ge(S["opp_done"], 1 + j)
                act.activation(partial_o[:, j * 512:(j + 1) * 512], bank[6 + j][:, :], ACT.Copy).then_inc(S["opp_evac"], 1)
            for m, t in enumerate(ORDER):
                n = TILES[t]
                act.wait_ge(S["h_done"], m + 1)
                chain.step(act.activation(junk[0:n, :], x[0:n, t, :], ACT.Square, accum_out=ssf[0:n, t:t + 1]))
                act.activation(stdf[0:n, t:t + 1], ssf[0:n, t:t + 1], ACT.Sqrt, bias=eps[0:n, :], scale=1.0 / D)\
                    .then_inc(S["h_std"], 1)
            act.wait_ge(S["r_sub"], 1)
            act.activation(eg, eg, ACT.Exp).then_inc(S["r_exp1"], 1)
            act.wait_ge(S["r_sub2"], 1)
            act.activation(e2, dd, ACT.Exp).then_inc(S["r_exp2"], 1)

            def pair(i, s, turn, first):
                act.wait_ge(S["gu_done"], i + 1)
                if not first:
                    act.wait_ge(S["act_done"], i)
                act.activation(hs, bank[2][:, 0:F], ACT.Silu).then_inc(S["silu_done"], 1)
                act.wait_ge(S["ht_done"], i + 1)
                if not first:
                    act.wait_ge(S["dn_done"], i)
                act.activation(hT, bank[3][:, 0:2 * P].rearrange("p (c n) -> p c n", c=2), ACT.Copy).then_inc(S["ht_evac"], 1)
                if turn is not None:
                    act.wait_ge(res_sem[s], turn)
                act.wait_ge(S["dn_done"], i + 1)
                act.activation(yo[s][:, 0:512], bank[4][:, :], ACT.Copy).then_inc(S["dn_evac_a"], 1)

            act.wait_ge(S["count_done"], len(GROUPS))
            for i in range(4):
                pair(i, i % 3, 16 * (i // 3) if i >= 3 else None, i == 0)
            with act.Fori(0, 4) as j:
                for n, s in enumerate((1, 2, 0)):
                    pair(3 * j + 4 + n, s, 16 * (j + 1) + (16 if s == 0 else 0), False)
            act.wait_ge(S["flag_ready"], 1)
            more = act.value_load(flag[0:1, 0:1], min_val=0, max_val=1)
            with act.If(more > 0):
                with act.Fori(0, OV_PAIRS // 3) as j:
                    for n, s in enumerate((1, 2, 0)):
                        pair(3 * j + 16 + n, s, 16 * (j + 5) + (16 if s == 0 else 0), False)
                act.nop()
            act.nop()

        @block.vector
        def _(dve):
            chain = Chain(dve, S["dve_link"])

            def tt(out, a, b, op):
                return dve.tensor_tensor(out, a, b, op)

            dve.memset(eps, EPS)
            dve.memset(xsT, 0.0)
            dve.memset(mixsT, 0.0)
            dve.memset(logits[:, :, :], 0.0).then_inc(S["pads_zero"], 1)
            dve.wait_ge(S["pads_zero"], 1)
            dve.wait_ge(S["gains_turned"], 1)
            chain.step(dve.tensor_copy(gains[:, 0:30], bank[7][:, 0:30]))

            def x_scale(t):
                n = TILES[t]
                dve.wait_ge(S["x_std"], t + 1)
                chain.step(dve.reciprocal(rx[0:n, t:t + 1], stdx[0:n, t:t + 1]))
                dve.tensor_scalar(xn[0:n, t, :], x[0:n, t, :], rx[0:n, t:t + 1], None, ALU.mult).then_inc(S["x_scaled"], 1)

            def x_copy(g):
                dve.wait_ge(S["x_turned"], g + 1)
                t = g // 2
                if t < NT:
                    k = 4 * (g % 2)
                    tt(xT[:, k:k + 4, t * P:(t + 1) * P], bank[g % 3][:, :].rearrange("p (a b) -> p a b", a=4),
                       bc(gains[:, k:k + 4], 2, P, [P, 4, P]), ALU.mult).then_inc(S["x_evac"], 1)
                else:
                    tt(xsT[:, :, 0:DEC], bank[g % 3][:, 0:KD * DEC].rearrange("p (a b) -> p a b", a=KD),
                       bc(gains[:, 0:KD], 2, DEC, [P, KD, DEC]), ALU.mult).then_inc(S["x_evac"], 1)

            x_scale(0)
            for t in range(NT + 1):
                if t < NT:
                    x_scale(t + 1)
                x_copy(2 * t)
                if t < NT:
                    x_copy(2 * t + 1)
            dve.wait_ge(S["misc_in"], 96)
            half = DH // 2
            for i, scale in ((0, DH ** -0.5), (1, 1.0)):
                g = gqk[:, i, :]
                dve.scalar_tensor_tensor(rope_g[2 * i], cos, scale, bc(g, 1, T5, [P, T5, DH]), ALU.mult, ALU.mult)
                for a in range(2):
                    b = 1 - a
                    last = dve.scalar_tensor_tensor(rope_g[2 * i + 1][:, :, a * half:(a + 1) * half],
                                                    sin[:, :, a * half:(a + 1) * half], scale,
                                                    bc(g[:, b * half:(b + 1) * half], 1, T5, [P, T5, half]),
                                                    ALU.mult, ALU.mult)
            last.then_inc(S["rope_ready"], 1)
            dve.wait_ge(S["rope_ready"], 1)

            def norm_rope(src, w, c, t, k, dst, out_sem):
                v6 = "p (a b) -> p a b"
                dve.wait_ge(S["z_squared"], k + 1)
                dve.tensor_reduce(zss[0:w, :], zsq[0:w, :].rearrange(v6, a=6), AX.X, ALU.add).then_inc(S["z_ssq"], 1)
                dve.wait_ge(S["z_std"], k + 1)
                chain.step(dve.reciprocal(zr[0:w, :], zstd[0:w, :]))
                if k >= 1:
                    dve.wait_ge(S["z_sin"], k)
                tt(zn[0:w, :].rearrange(v6, a=6), src.rearrange(v6, a=6), bc(zr[0:w, :], 2, DH, [w, 6, DH]), ALU.mult)\
                    .then_inc(S["z_copied" if w == P else "comb_read"], 1)
                if w == P:
                    dve.wait_ge(S["z_copied"], unit(c, t) + 1)
                else:
                    dve.wait_ge(S["comb_read"], c + 1)
                dve.engine_nop().then_inc(S["z_cos"], 1)
                chain.step(tt(zcos[0:w, :].rearrange(v6, a=6), zn[0:w, :].rearrange(v6, a=6),
                              bc(rope_g[2 * (c // 2)][0:w, t, :], 1, 6, [w, 6, DH]), ALU.mult))
                dve.wait_ge(S["z_sin"], k + 1)
                tt(dst, zcos[0:w, :], zsin[0:w, :], ALU.add).then_inc(out_sem, 1)

            def sample_scores(b):
                dve.wait_ge(kv_in[b % 2], 48 * (b // 2 + 1))
                dve.wait_ge(S["qb_done"], b + 1)
                kb = kv[b % 2]
                for j in range(2):
                    last = tt(kb[:, :, j * CW:(j + 1) * CW], kb[:, :, j * CW:(j + 1) * CW],
                              bc(bank[6 + j][:, 0:CW], 1, 2, [P, 2, CW]), ALU.mult)
                last.then_inc(S["qb_used"], 1)
                dve.wait_ge(S["qb_used"], b + 1)
                for i in range(2):
                    last = dve.tensor_reduce(sc[:, i, b * H:(b + 1) * H], kb[:, i, :].rearrange("p (h d) -> p h d", h=H),
                                             AX.X, ALU.add)
                last.then_inc(S["scores_s"], 1)

            k = 0
            scores_at = {(3, 0): 0, (3, 2): 1, (3, 3): 2, (4, 0): 3}
            for c in range(QK_CHUNKS + 1):
                for t in range(NT):
                    if c < QK_CHUNKS:
                        n = unit(c, t)
                        dve.wait_ge(S["z_done"], n + 1)
                        if n >= 2:
                            dve.wait_ge(S["rot_turned"], n - 1)
                            if n - 2 >= 2 * NT:
                                dve.wait_ge(rot_out[n % 2], 16 * ((n - 2 - 2 * NT) // 2 + 1))
                        norm_rope(bank[n % 3][:, 0:CW], P, c, t, k, rot[n % 2], S["rot_done"])
                        k += 1
                    if t == 1 and c >= 1:
                        cc = c - 1
                        dve.wait_ge(S["comb_done"], cc + 1)
                        norm_rope(bank[4][0:DEC, 0:CW], DEC, cc, NT, k, (qs if cc < 2 else ks)[0:DEC, (cc % 2) * CW:(cc % 2 + 1) * CW],
                                  S["rope_ready"])
                        k += 1
                    if (c, t) in scores_at:
                        sample_scores(scores_at[c, t])
            for b in range(4, DEC):
                sample_scores(b)
            dve.wait_ge(S["rope_ready"], 1 + QK_CHUNKS)
            chain.step(tt(qs[0:DEC, :], qs[0:DEC, :], ks[0:DEC, :], ALU.mult))
            dve.tensor_reduce(sself[0:DEC, :], qs[0:DEC, :].rearrange("p (h d) -> p h d", h=H), AX.X, ALU.add)\
                .then_inc(S["scores_s"], 1)
            chain.step(dve.memset(nm_s, 0.0))
            dve.wait_ge(S["turned_s"], 1)
            dve.wait_ge(S["self_spread"], 1)
            tt(smask[0:96, :], bank[7][0:96, 0:H], sm("head")[0:96, :], ALU.mult)
            chain.step(dve.tensor_copy(raw_s[0:96, 0:256], bank[6][0:96, 0:256]))
            chain.step(dve.tensor_reduce(raw_s[0:96, 256:257], smask[0:96, :], AX.X, ALU.add))
            dve.wait_ge(S["logc_in"], 32)
            dve.wait_ge(S["state_turned"], 1)
            dve.tensor_tensor_reduce(neg_s[0:96, :], raw_s[0:96, :], slogc[0:96, :], -1.0, 3.0e38, ALU.add, ALU.min,
                                     nm_s[0:96, :]).then_inc(S["soft_in"], 1)
            dve.wait_ge(S["soft_done"], 1)
            dve.reciprocal(rden_s[0:96, :], den_s[0:96, :])
            dve.tensor_scalar(self8[0:96, :], sm("sample")[0:96, :], prob_s[0:96, 256:257], None, ALU.mult)\
                .then_inc(S["soft_done"], 1)
            dve.wait_ge(S["probs_turned"], 1)
            dve.wait_ge(S["zero_rows"], 1)
            turned = bank[5][:, 0:192].rearrange("p (i q) -> p i q", i=2)
            for b in range(DEC):
                dve.tensor_copy(probs_s[:, :, b, b * H:(b + 1) * H], turned[:, :, b * H:(b + 1) * H])
            dve.tensor_copy(selfT, bank[5][0:DEC, 192:192 + DEC * H]).then_inc(S["probs_placed"], 1)

            def masked_scores(p):
                n = (pair_units[p][0] + 1) * P
                for h in range(2):
                    u = 2 * p + h
                    dve.wait_ge(S["s_done"], u + 1)
                    if p >= 2:
                        dve.wait_ge(S["p_turned"], u - 3)
                    dve.tensor_tensor_reduce(scores_sb[p % 2][h][:, 0:n], score_bank[p % 2][h][:, 0:n],
                                             logc[:, SEQ - n:SEQ], -1.0, 3.0e38, ALU.add, ALU.min,
                                             nmax[:, u % 4:u % 4 + 1]).then_inc(S["masked"], 1)

            chain.step(dve.memset(cuT[:, :, 0:2], 0.0))
            for h in range(2):
                i = 2 * h + 1
                dve.wait_ge(S["blk_done"], i + 1)
                dve.wait_ge(S["blk_evac_a"], h + 1)
                tt(cuT[:, h, 2:2 + SEQ], cuT[:, h, 2:2 + SEQ], bank[i % 3][:, :], ALU.mult)
                tt(cu_s[:, h, 2, :], cu_s[:, h, 2, :], bank[5][:, 0:DEC], ALU.mult).then_inc(S["blk_evac_v"], 1)
                dve.wait_ge(S["blk_evac_v"], h + 1)
                dve.wait_ge(S["cu_ready"], 2)
                for j in range(3):
                    tap = gains[:, 24 + 2 * j + h:25 + 2 * j + h]
                    for dst, src in ((yT[:, h, 0:SEQ], cuT[:, h, j:j + SEQ]), (yT[:, h, SEQ:TOK], cu_s[:, h, j, :])):
                        if j == 0:
                            last = dve.tensor_scalar(dst, src, tap, None, ALU.mult)
                        else:
                            last = dve.scalar_tensor_tensor(dst, src, tap, dst, ALU.mult, ALU.add)
                    chain.step(last)
            for h in range(2):
                i = 4 + h
                dve.wait_ge(S["blk_done"], i + 1)
                tt(yT[:, h, 0:SEQ], yT[:, h, 0:SEQ], bank[i % 3][:, :], ALU.mult)
                tt(yT[:, h, SEQ:TOK], yT[:, h, SEQ:TOK], bank[3 + 2 * (i % 2)][:, 0:DEC], ALU.mult).then_inc(S["blk_evac_v"], 1)
                if h == 0:
                    masked_scores(0)
                    dve.wait_ge(S["pv_s"], 1)
                    for i in range(2):
                        dve.wait_ge(rot_out[i], 16 * NT)
                    for j in range(2):
                        dve.scalar_tensor_tensor(head_out[0:96, j * CW:(j + 1) * CW].rearrange("p (a b) -> p a b", a=6),
                                                 bank[6 + j][0:96, 0:CW].rearrange("p (a b) -> p a b", a=6), rden_s[0:96, :],
                                                 bc(sm("head")[0:96, 6 * j:6 * j + 6], 2, DH, [96, 6, DH]), ALU.mult, ALU.mult)\
                            .then_inc(S["head_done"], 1)
            dve.wait_ge(S["blk_evac_v"], 4)
            dve.engine_nop().then_inc(S["conv_done"], 1)

            for p in range(NU + 3):
                if 1 <= p < NU:
                    masked_scores(p)
                if p == 0:
                    dve.wait_ge(S["gathered_s"], 1)
                    dve.tensor_copy(attn_s[0:DEC, 0:CW], bank[6][0:DEC, 0:CW])
                    dve.tensor_copy(attn_s[0:DEC, CW:DA], bank[7][0:DEC, 0:CW]).then_inc(S["attn_s_done"], 1)
                if p == 3:
                    dve.wait_ge(S["y_squared"], 1)
                    tt(yT, yT, bc(gains[:, 22:24], 2, TOK, [P, 2, TOK]), ALU.mult).then_inc(S["y_gained"], 1)
                    dve.wait_ge(S["y_gained"], 1)
                    dve.tensor_copy(mixsT[:, NP:KD, 0:DEC], yT[:, :, SEQ:TOK])
                if 1 <= p <= NU:
                    u = p - 1
                    n = (pair_units[u][0] + 1) * P
                    dve.wait_ge(S["p_turned"], 2 * u + 2)
                    if u >= 2:
                        dve.wait_ge(S["o_done"], u - 1)
                    dve.tensor_copy(probs_t[u % 2][1][:, 0:n], turn_bank[1][:, 0:n]).then_inc(S["p_evac_v"], 1)
                if p >= 3:
                    u = p - 3
                    qt, hp = pair_units[u]
                    dve.wait_ge(S["o_done"], u + 1)
                    chain.step(dve.reciprocal(rden[u % 2], den[:, (2 * u) % 24:(2 * u) % 24 + 2]))
                    tt(attn[:, qt, 2 * hp * DH:2 * (hp + 1) * DH].rearrange("p (a b) -> p a b", a=2),
                       bank[6 + u % 2][:, 0:P].rearrange("p (a b) -> p a b", a=2),
                       bc(rden[u % 2], 2, DH, [P, 2, DH]), ALU.mult).then_inc(S["o_evac"], 1)
            dve.wait_ge(S["ssc_std"], 1)
            dve.reciprocal(rc[:, 0:NT], ssc[:, 0:NT])
            dve.reciprocal(rc[0:DEC, NT:NT + 1], ssc[0:DEC, NT:NT + 1]).then_inc(S["conv_std"], 1)

            for g in range(2 * NT + 1):
                t = g // 2
                dve.wait_ge(S["a_turned"], g + 1)
                if t < NT:
                    k = 3 * (g % 2)
                    tt(attnT[:, k:k + 3, t * P:(t + 1) * P], bank[g % 2][:, 0:CW].rearrange("p (a b) -> p a b", a=3),
                       bc(gains[:, 16 + k:19 + k], 2, P, [P, 3, P]), ALU.mult).then_inc(S["a_evac"], 1)
                else:
                    tt(mixsT[:, 0:NP, 0:DEC], bank[g % 2][:, 0:NP * DEC].rearrange("p (a b) -> p a b", a=NP),
                       bc(gains[:, 16:16 + NP], 2, DEC, [P, NP, DEC]), ALU.mult).then_inc(S["a_evac"], 1)
            dve.wait_ge(S["a_std"], 1)
            dve.reciprocal(ra[:, 0:NT], stda[:, 0:NT])
            chain.step(dve.reciprocal(ra[0:DEC, NT:NT + 1], stda[0:DEC, NT:NT + 1]))
            dve.wait_ge(S["conv_std"], 1)

            def h_copy(m):
                n = TILES[ORDER[m]]
                for g in range(2):
                    dve.wait_ge(S["h_turned"], 2 * m + g + 1)
                    if m >= 2:
                        dve.wait_ge(S["r_done"], m - 1)
                    tt(hnT[m % 2][:, 4 * g:4 * g + 4, 0:n], bank[4 + g][:, :].rearrange("p (a b) -> p a b", a=4)[:, :, 0:n],
                       bc(gains[:, 8 + 4 * g:12 + 4 * g], 2, n, [P, 4, n]), ALU.mult).then_inc(S["h_evac"], 1)

            iota = sm("iota")
            step = chain.step
            stt = dve.scalar_tensor_tensor

            def first_max(vals, m, c_, out, n):
                w = vals.shape[1]
                step(dve.tensor_reduce(m, vals, AX.X, ALU.max))
                step(tt(c_, vals, bc(m, 2, n, [P, w, n]), ALU.is_equal))
                step(tt(c_, c_, bc(iota[:, 0:n], 1, w, [P, w, n]), ALU.mult))
                step(dve.tensor_reduce(mn[:, 0:w], c_, AX.X, ALU.min))
                step(tt(out, c_, bc(mn[:, 0:w], 2, n, [P, w, n]), ALU.is_equal))

            def r_copy(m):
                n = TILES[ORDER[m]]
                dve.wait_ge(S["r_done"], m + 1)
                dve.tensor_copy(logits[0:n, m, :], bank[6][0:n, 0:G + E]).then_inc(S["r_evac"], 1)

            def choose(b):
                m0, m1 = GROUPS[b]
                w = m1 - m0
                here = slice(m0, m1)
                dve.wait_ge(S["r_evac"], m1)
                o = ohg[:, here, :]
                first_max(logits[:, here, 0:G], gm[:, here], cg[:, here, :], o, G)
                if b == 0:
                    step(tt(o, o, bc(sm("valid"), 2, G, [P, 2, G]), ALU.mult))
                t4 = tmp[:, 0, here, :].rearrange("p t (g e) -> p t g e", g=G)
                step(tt(t4, logits[:, here, G:G + E].rearrange("p t (g e) -> p t g e", g=G), bc(o, 3, EG, [P, w, G, EG]), ALU.mult))
                step(dve.tensor_reduce(leg[:, here, :], t4.rearrange("p t g e -> p t e g"), AX.X, ALU.add))
                first_max(leg[:, here, :], m1_[:, here], cand[:, here, :], oh1[:, here, :], EG)
                step(stt(cand2[:, here, :], oh1[:, here, :], NEG, leg[:, here, :], ALU.mult, ALU.add))
                first_max(cand2[:, here, :], m2_[:, here], cand[:, here, :], oh2[:, here, :], EG)
                for i, oh in enumerate((oh1, oh2)):
                    step(tt(e12[:, i, here, :].rearrange("p t (g e) -> p t g e", g=G), bc(o, 3, EG, [P, w, G, EG]),
                            bc(oh[:, here, :], 2, G, [P, w, G, EG]), ALU.mult))
                tt(assigned[:, m0 * E:m1 * E].rearrange("p (t e) -> p t e", t=w), e12[:, 0, here, :], e12[:, 1, here, :], ALU.add)\
                    .then_inc(S["assign"], 1)
                for dst, by in ((mr, sm("mainrow")), (ov, sm("ovrow"))):
                    for i in range(2):
                        last = tt(tmp[:, i, here, :], e12[:, i, here, :], bc(by, 1, w, [P, w, E]), ALU.mult)
                    step(last)
                    step(dve.tensor_reduce(dst[:, :, here], tmp[:, :, here, :], AX.X, ALU.add))

            def place(b):
                m0, m1 = GROUPS[b]
                here = slice(m0, m1)
                dve.wait_ge(S["count_done"], b + 1)
                for m in range(m0, m1):
                    o = (m - m0) * 2 * E
                    step(tt(posn[:, m, :], total, bank[7][:, o:o + E], ALU.add))
                    step(tt(total, total, bank[7][:, o + E:o + 2 * E], ALU.add))
                dve.engine_nop().then_inc(S["count_read"], 1)
                for i in range(2):
                    last = tt(tmp[:, i, here, :], e12[:, i, here, :], posn[:, here, :], ALU.mult)
                step(last)
                p_, m_, o_ = (a[:, :, here] for a in (pk, mr, ov))
                step(dve.tensor_reduce(p_, tmp[:, :, here, :], AX.X, ALU.add))
                step(stt(m_, p_, float(PAIRS), m_, ALU.mult, ALU.add))
                step(stt(o_, p_, 1.0 - PAIRS, o_, ALU.mult, ALU.add))
                step(stt(o_, p_, float(SL), o_, ALU.is_ge, ALU.mult))
                step(tt(m_, m_, o_, ALU.add))
                dve.tensor_copy(addr[:, :, here], m_).then_inc(S["addr_done"], 1)

            step(dve.memset(total, 0.0))

            def add_group(m, g):
                t, u = ORDER[m], 4 * m + g
                n = TILES[t]
                dve.wait_ge(S["op_done"], u + 1)
                cols = slice((g % 2) * 512, (g % 2 + 1) * 512)
                r_ = (ra if g < 2 else rc)[0:n, t:t + 1]
                if g >= 2:
                    dve.wait_ge(S["op_evac"], u - 1)
                stt(x[0:n, t, cols], bank[g][0:n, :], r_, x[0:n, t, cols], ALU.mult, ALU.add).then_inc(S["op_evac"], 1)

            def h_scale(m):
                t = ORDER[m]
                n = TILES[t]
                dve.wait_ge(S["op_evac"], 4 * m + 4)
                dve.engine_nop().then_inc(S["h_done"], 1)
                dve.wait_ge(S["h_std"], m + 1)
                step(dve.reciprocal(rf[0:n, t:t + 1], stdf[0:n, t:t + 1]))
                if m >= 2:
                    dve.wait_ge(hn_sem[m % 2], 16 * (m // 2))
                dve.tensor_scalar(hn[m % 2][0:n, :], x[0:n, t, :], rf[0:n, t:t + 1], None, ALU.mult).then_inc(S["h_scaled"], 1)

            for m in (0, 1):
                for g in range(4):
                    add_group(m, g)
                h_scale(m)
            h_copy(0)
            add_group(2, 0)
            h_copy(1)
            add_group(2, 1)
            r_copy(0)
            add_group(2, 2)
            r_copy(1)
            add_group(2, 3)
            h_scale(2)
            choose(0)
            add_group(3, 0)
            h_copy(2)
            add_group(3, 1)
            r_copy(2)
            add_group(3, 2)
            place(0)
            add_group(3, 3)
            h_scale(3)
            choose(1)
            add_group(4, 0)
            h_copy(3)
            add_group(4, 1)
            r_copy(3)
            add_group(4, 2)
            add_group(4, 3)
            h_scale(4)
            place(1)
            h_copy(4)
            r_copy(4)
            choose(2)
            place(2)
            step(dve.tensor_reduce(gm_max, total, AX.X, ALU.max))
            dve.tensor_scalar(flag[:, :], gm_max, float(SL), None, ALU.is_gt).then_inc(S["flag_ready"], 1)
            lg = logits[:, :, 0:G]
            step(tt(eg, lg, bc(gm, 2, G, [P, T5, G]), ALU.subtract))
            dve.engine_nop().then_inc(S["r_sub"], 1)
            step(tt(dd, m2_, m1_, ALU.subtract))
            dve.engine_nop().then_inc(S["r_sub2"], 1)
            dve.wait_ge(S["r_exp1"], 1)
            step(dve.tensor_reduce(gsum, eg, AX.X, ALU.add))
            step(dve.reciprocal(pg, gsum))
            dve.wait_ge(S["r_exp2"], 1)
            step(dve.tensor_scalar(dd, e2, 1.0, None, ALU.add))
            step(dve.reciprocal(dd, dd))
            step(tt(w12[:, 0, :], dd, pg, ALU.mult))
            step(tt(w12[:, 1, :], w12[:, 0, :], e2, ALU.mult))

            def tokens(i, s):
                dve.wait_ge(S["xg_turned"], i + 1)
                if not isinstance(i, int) or i > 0:
                    dve.wait_ge(S["gu_done"], i)
                for g in range(2):
                    last = tt(xgT[:, 4 * g:4 * g + 4, :], bank[g][:, :].rearrange("p (a b) -> p a b", a=4),
                              bc(gains[:, 8 + 4 * g:12 + 4 * g], 2, P, [P, 4, P]), ALU.mult)
                last.then_inc(S["xg_evac"], 1)

            def hidden(i, first):
                dve.wait_ge(S["silu_done"], i + 1)
                if not first:
                    dve.wait_ge(S["ht_done"], i)
                tt(hgu, hs, bank[2][:, F:2 * F], ALU.mult).then_inc(S["act_done"], 1)

            def result(i, s, turn):
                if turn is not None:
                    dve.wait_ge(res_sem[s], turn)
                dve.wait_ge(S["dn_done"], i + 1)
                dve.tensor_copy(yo[s][:, 512:D], bank[5][:, :]).then_inc(S["dn_evac_v"], 1)

            tokens(0, 0)
            for i in range(4):
                hidden(i, i == 0)
                tokens(i + 1, 0)
                result(i, i % 3, 16 * (i // 3) if i >= 3 else None)
            with dve.Fori(0, 3) as j:
                for n, s in enumerate((1, 2, 0)):
                    i = 3 * j + 4 + n
                    hidden(i, False)
                    tokens(i + 1, 0)
                    result(i, s, 16 * (j + 1) + (16 if s == 0 else 0))
            for i in range(13, 16):
                hidden(i, False)
                if i < 15:
                    tokens(i + 1, 0)
                result(i, i % 3, 16 * (i // 3))
            more = dve.value_load(flag[0:1, 0:1], min_val=0, max_val=1)
            with dve.If(more > 0):
                link = S["rope_ready"]
                at = [1 + QK_CHUNKS]

                def lstep(ins):
                    at[0] += 1
                    ins.then_inc(link, 1)
                    dve.wait_ge(link, at[0])

                big = cut(rt, 0, E, 8)
                lstep(tt(big[0:1], bc(total[0:1, :], 2, 8, [1, E, 8]), bc(sm("limits")[0:1, :], 1, E, [1, E, 8]), ALU.is_gt))
                lstep(dve.tensor_reduce(nb[0:1, :], big[0:1], AX.X, ALU.add))
                lstep(dve.tensor_copy(cum_a[0:1, :], nb[0:1, :]))
                a, b = cum_a, cum_b
                for sh in (1, 2, 4, 8, 16):
                    lstep(dve.tensor_copy(b[0:1, 0:sh], a[0:1, 0:sh]))
                    lstep(tt(b[0:1, sh:E], a[0:1, sh:E], a[0:1, 0:E - sh], ALU.add))
                    a, b = b, a
                for n in range(2 * OV_PAIRS):
                    lstep(dve.tensor_scalar(b[0:1, :], a[0:1, :], float(n), None, ALU.is_le))
                    lstep(dve.tensor_reduce(lst[0:1, n:n + 1], b[0:1, :], AX.X, ALU.add))
                    lstep(tt(b[0:1, :], b[0:1, :], nb[0:1, :], ALU.mult))
                    lstep(dve.tensor_reduce(lst2[0:1, n:n + 1], b[0:1, :], AX.X, ALU.add))
                    lstep(dve.tensor_scalar(lst2[0:1, n:n + 1], lst2[0:1, n:n + 1], -float(SL), OV_BASE + float(n * SL),
                                            ALU.mult, ALU.add))
                lstep(dve.scalar_tensor_tensor(lst2[0:1, :], lst[0:1, :], float(OV_ROWS), lst2[0:1, :], ALU.mult, ALU.add))
                lstep(dve.tensor_scalar(lst[0:1, :], lst[0:1, :], float(E - 1), None, ALU.min))
                lstep(dve.tensor_copy(ov_list[0:1, 0, :], lst[0:1, :]))
                dve.tensor_copy(ov_list[0:1, 1, :], lst2[0:1, :]).then_inc(S["list_done"], 1)
                with dve.Fori(0, OV_PAIRS // 3) as j:
                    for n, s in enumerate((1, 2, 0)):
                        i = 3 * j + 16 + n
                        tokens(i, 0)
                        hidden(i, False)
                        result(i, s, 16 * (j + 5) + (16 if s == 0 else 0))
                dve.nop()
            for t in range(NT + 1):
                n = TILES[t]
                dve.wait_ge(back_in[t], 16)
                for i in range(2):
                    if i == 1:
                        dve.wait_ge(S["x_scaled"], NT + 1 + t + 1)
                    dve.scalar_tensor_tensor(x[0:n, t, :], back[t][0:n, i, :], w12[0:n, i, ORDER.index(t):ORDER.index(t) + 1], x[0:n, t, :],
                                             ALU.mult, ALU.add).then_inc(S["x_scaled" if i == 0 else "h_done"], 1)

        @block.gpsimd
        def _(pool):
            k = 0
            half = DH // 2
            for c in range(QK_CHUNKS + 1):
                todo = []
                for t in range(NT):
                    if c < QK_CHUNKS:
                        todo.append((c, t, P))
                    if t == 1 and c >= 1:
                        todo.append((c - 1, NT, DEC))
                for cc, t, w in todo:
                    pool.wait_ge(S["z_cos"], k + 1)
                    pool.wait_ge(S["rope_ready"], 1)
                    if w == P and unit(cc, t) >= 1 or w == DEC:
                        n_done = unit(cc, t) if w == P else 0
                        if w == P:
                            pool.wait_ge(S["rot_done"], n_done)
                        else:
                            pool.wait_ge(S["rot_done"], min(unit(cc + 1, 1) + 1, QK_CHUNKS * NT))
                    if w == P and t == 2 and cc >= 1:
                        pool.wait_ge(S["rope_ready"], 1 + cc)
                    zv = zn[0:w, :].rearrange("p (a b) -> p a b", a=6)
                    sv = zsin[0:w, :].rearrange("p (a b) -> p a b", a=6)
                    for a in range(2):
                        b = 1 - a
                        last = pool.tensor_tensor(sv[:, :, a * half:(a + 1) * half], zv[:, :, b * half:(b + 1) * half],
                                                  bc(rope_g[2 * (cc // 2) + 1][0:w, t, a * half:(a + 1) * half], 1, 6,
                                                     [w, 6, half]), ALU.mult)
                    last.then_inc(S["z_sin"], 1)
                    k += 1
                    if w == P and cc >= 2:
                        n = unit(cc, t)
                        pool.wait_ge(S["rot_done"], n + 1)
                        pool.dma_start(k_out[t][:, (cc - 2) * CW:(cc - 1) * CW], rot[n % 2]).then_inc(rot_out[n % 2], 16)
            pool.wait_ge(S["rope_ready"], 1 + QK_CHUNKS)
            pool.memset(probs_s, 0.0).then_inc(S["zero_rows"], 1)

            def dispatch(b):
                pool.wait_ge(S["addr_done"], b + 1)
                if b == 0:
                    pool.wait_ge(S["table_in"], 16)
                    pool.wait_ge(S["wr_in"], 80)
                for m in range(*GROUPS[b]):
                    t = ORDER[m]
                    n = TILES[t]
                    for i in range(2):
                        pool.indirect_dma_start(table, bass.IndirectOffsetOnAxis(addr[0:n, i, m:m + 1], 0),
                                                pay_sb[0:n, t, i, :], None, bounds_check=TABLE - 1, oob_is_err=False)\
                            .then_inc(S["scattered"], 16)

            for m, t in enumerate(ORDER):
                pool.wait_ge(S["h_scaled"], m + 1)
                pool.dma_start(hn_rows[t * P:t * P + TILES[t], :], hn[m % 2][0:TILES[t], :]).then_inc(hn_sem[m % 2], 16)
                for b in ((), (), (0,), (), (1,))[m]:
                    dispatch(b)
            pool.wait_ge(hn_sem[1], 32)
            pool.wait_ge(S["h_evac"], 2 * NT + 2)
            pool.wait_ge(S["r_done"], NT + 1)
            pool.memset(xg[1], 0.0).then_inc(S["pool_link"], 1)
            pool.memset(xg[2], 0.0).then_inc(S["pool_link"], 1)
            dispatch(2)
            pool.wait_ge(hn_sem[0], 48)
            pool.memset(xg[0], 0.0).then_inc(S["pool_link"], 1)
            pool.wait_ge(S["pool_link"], WSLOTS)
            pool.wait_ge(S["scattered"], 160)
            pool.dma_start(tbl[:, :, :], table[0:E * SL].rearrange("(p i) w -> p i w", i=PAIRS)).then_inc(S["tbl_in"], 16)
            pool.wait_ge(S["tbl_in"], 16)

            def gather(s, tokens):
                pool.sem_inc(S["gather_go"], 1)
                pool.indirect_dma_start(xg[s], None, hn_rows, bass.IndirectOffsetOnAxis(tokens, 0),
                                        bounds_check=TOK - 1, oob_is_err=False).then_inc(xg_sem[s], 16)

            def next_tokens(i, s):
                pool.tensor_copy(idx_g[:, s:s + 1], tbl[:, ds(i, 1), 0:1].rearrange("p i w -> p (i w)"))\
                    .then_inc(S["idx_g_ready"], 1)
                pool.wait_ge(S["idx_g_ready"], i + 1)
                gather(s, idx_g[:, s:s + 1])

            def scatter(i, s, of_table=True):
                pool.wait_ge(S["dn_evac_a"], i + 1)
                if of_table:
                    pool.tensor_copy(idx[:, s, :], tbl[:, ds(i, 1), :].rearrange("p i w -> p (i w)")).then_inc(S["idx_ready"], 1)
                    pool.wait_ge(S["idx_ready"], i + 1)
                    pool.sem_inc(S["scatter_go"], 1)
                pool.wait_ge(S["dn_evac_v"], i + 1)
                pool.sem_inc(S["scatter_go"], 1)
                pool.indirect_dma_start(results, bass.IndirectOffsetOnAxis(idx[:, s, 1:2], 0), yo[s], None,
                                        bounds_check=CHOICES - 1, oob_is_err=False).then_inc(res_sem[s], 16)

            for i in range(WSLOTS):
                next_tokens(i, i)
            pool.wait_ge(S["xg_turned"], 1)
            next_tokens(WSLOTS, 0)
            with pool.Fori(0, (PAIRS - 4) // 3) as j:
                for n in range(3):
                    i = 3 * j + n
                    pool.wait_ge(S["xg_turned"], i + 2)
                    next_tokens(i + 4, (n + 1) % 3)
                    scatter(i, n)
            for i in range(PAIRS - 4, PAIRS):
                scatter(i, i % 3)
            pool.wait_ge(res_sem[0], 96)
            pool.wait_ge(res_sem[1], 80)
            pool.wait_ge(res_sem[2], 80)
            pool.wait_ge(S["flag_ready"], 1)
            more = pool.value_load(flag[0:1, 0:1], min_val=0, max_val=1)
            with pool.If(more > 0):
                pool.wait_ge(S["list_done"], 1)
                with pool.Fori(0, OV_PAIRS // 3) as j:
                    for n, s in enumerate((1, 2, 0)):
                        i = 3 * j + 16 + n
                        k2 = 2 * (3 * j + n)
                        for h in range(2):
                            row = pool.value_load(ov_list[0:1, 1, ds(k2 + h, 1)], min_val=0, max_val=TABLE - SL)
                            pool.dma_start(idx[h * SL:(h + 1) * SL, s, :], table[ds(row, SL), :]).then_inc(S["ov_in"], 16)
                        pool.wait_ge(S["ov_in"], 32 * (3 * j + n + 1))
                        gather(s, idx[:, s, 0:1])
                        scatter(i, s, False)
                        pool.wait_ge(res_sem[s], 16 * (j + 6) + (16 if s == 0 else 0))
                        pool.sem_inc(S["ov_done"], 1)
                pool.nop()
            pool.engine_nop().then_inc(S["y_ready"], 1)


_INS = ["x_prompt", "x_sample", "cache_k", "cache_v", "state_conv", "g_norm_mix", "w_in", "g_q", "g_k", "w_conv",
        "g_attn_out", "g_conv_out", "w_out", "g_norm_ffn", "w_router_group", "w_router_expert", "w_gate", "w_up", "w_down"]
_OUTS = [(1, SEQ, D), (DEC, 1, D), (1, 1, SEQ, H, DH), (1, 1, SEQ, H, DH), (1, 1, 2, DC), (1, DEC, 1, H, DH),
         (1, DEC, 1, H, DH), (1, DEC, 2, DC)]


def kernel(**inputs):
    import concourse.bacc as _bacc
    from concourse.bass_utils import run_bass_kernel_spmd as _run

    nc = _bacc.Bacc("TRN2", target_bir_lowering=False, num_devices=1)
    arrays, args = {}, []
    given = [(n, inputs[n]) for n in _INS] + [("const", constants()[0]), ("pay", payload()), ("empty", empty_table())]
    for name, a in given:
        a = np.ascontiguousarray(a)
        arrays[f"in_{name}_dram"] = a
        args.append(nc.dram_tensor(f"in_{name}_dram", a.shape, mybir.dt.from_np(a.dtype), kind="ExternalInput").ap())
    for i, shape in enumerate(_OUTS):
        args.append(nc.dram_tensor(f"out_{i}_dram", shape, F32, kind="ExternalOutput").ap())
    build(nc, *args)
    r = _run(nc, [arrays], core_ids=[0])
    return tuple(r.results[0][f"out_{i}_dram"] for i in range(len(_OUTS)))
```
